# Optimizing a Trainium2 kernel written in Bass

```python
import jax, jax.numpy as jnp
from jax import lax
import numpy as np

D_MODEL = 2048
BATCH = 1
SEQ = 256
DEPTH = 1

HEAD_DIM = 128
N_HEADS_DSA = 8
N_HEADS_MOBA = 8
KV_LATENT = 256
IDX_HEADS = 16
IDX_DIM = 64
DSA_TOPK_MAX = 256
MOBA_BLOCK = 256
MOBA_TOPK_MAX = 3
N_MEM = 256
N_HEADS_MEM = 4
D_FF = -(-8 * D_MODEL // (3 * 256)) * 256
ATTN_Q_BLOCK = 128
MOBA_Q_BLOCK = 64
DSA_WIDTH = N_HEADS_DSA * HEAD_DIM
MOBA_WIDTH = N_HEADS_MOBA * HEAD_DIM
MEM_WIDTH = N_HEADS_MEM * HEAD_DIM
SPLIT_SIZES = (DSA_WIDTH, KV_LATENT, IDX_HEADS * IDX_DIM, IDX_DIM, IDX_HEADS,
               MOBA_WIDTH, MOBA_WIDTH, MOBA_WIDTH, D_MODEL, D_MODEL)
IN_WIDTH = sum(SPLIT_SIZES)
ALPHA = (2.0 * DEPTH) ** 0.25
BETA = (8.0 * DEPTH) ** -0.25
LN_EPS = 1e-5


def layer_norm(x, g, b):
    xf = x.astype(jnp.float32)
    mu = xf.mean(-1, keepdims=True)
    var = jnp.square(xf - mu).mean(-1, keepdims=True)
    return ((xf - mu) * lax.rsqrt(var + LN_EPS) * g.astype(jnp.float32) + b.astype(jnp.float32)).astype(x.dtype)

def rms_norm(x, g):
    xf = x.astype(jnp.float32)
    return (xf * lax.rsqrt(jnp.mean(xf * xf, -1, keepdims=True) + LN_EPS) * g.astype(jnp.float32)).astype(x.dtype)

def alibi_slopes(n):
    return jnp.asarray([2.0 ** (-8.0 * (i + 1) / n) for i in range(n)], dtype=jnp.float32)

def dsa_attention(q, c_kv, q_idx, k_idx, w_idx, w_uk, w_uv):
    S = q.shape[0]
    topk = min(DSA_TOPK_MAX, S // 4)
    slopes = alibi_slopes(N_HEADS_DSA)
    q_lat = jnp.einsum('shd,hdc->shc', q, w_uk)
    key_pos = jnp.arange(S)
    idx_scale = IDX_DIM ** -0.5
    w_scale = IDX_HEADS ** -0.5

    def block(i):
        t0 = i * ATTN_Q_BLOCK
        qi = lax.dynamic_slice_in_dim(q_idx, t0, ATTN_Q_BLOCK, 0)
        wi = lax.dynamic_slice_in_dim(w_idx, t0, ATTN_Q_BLOCK, 0)
        ql = lax.dynamic_slice_in_dim(q_lat, t0, ATTN_Q_BLOCK, 0)
        qpos = t0 + jnp.arange(ATTN_Q_BLOCK)
        logits = jnp.einsum('thd,sd->ths', qi, k_idx, preferred_element_type=jnp.float32) * idx_scale
        score = jnp.einsum('th,ths->ts', wi.astype(jnp.float32) * w_scale, jax.nn.relu(logits))
        score = jnp.where(key_pos[None, :] <= qpos[:, None], score, -jnp.inf)
        _, sel = lax.top_k(score, topk)
        valid = sel <= qpos[:, None]
        c_sel = c_kv[sel]
        s = jnp.einsum('thc,tkc->thk', ql, c_sel, preferred_element_type=jnp.float32) * (HEAD_DIM ** -0.5)
        dist = (qpos[:, None] - sel).astype(jnp.float32)
        s = s - slopes[None, :, None] * dist[:, None, :]
        s = jnp.where(valid[:, None, :], s, -jnp.inf)
        p = jax.nn.softmax(s, axis=-1).astype(c_kv.dtype)
        return jnp.einsum('thk,tkc->thc', p, c_sel)

    o_lat = lax.map(block, jnp.arange(S // ATTN_Q_BLOCK)).reshape(S, N_HEADS_DSA, KV_LATENT)
    o = jnp.einsum('shc,hcd->shd', o_lat, w_uv)
    return o.reshape(S, DSA_WIDTH)

def moba_attention(q, k, v):
    S, H, Dh = q.shape
    n_blk = -(-S // MOBA_BLOCK)
    pad = n_blk * MOBA_BLOCK - S
    kb = jnp.pad(k, ((0, pad), (0, 0), (0, 0))).reshape(n_blk, MOBA_BLOCK, H, Dh).transpose(2, 0, 1, 3)
    vb = jnp.pad(v, ((0, pad), (0, 0), (0, 0))).reshape(n_blk, MOBA_BLOCK, H, Dh).transpose(2, 0, 1, 3)
    k_mean = kb.astype(jnp.float32).mean(axis=2)
    n_sel = min(MOBA_TOPK_MAX, n_blk - 1)
    n_past = n_sel * MOBA_BLOCK
    slopes = alibi_slopes(H)
    scale = Dh ** -0.5
    offs = jnp.arange(MOBA_BLOCK)
    blk_ids = jnp.arange(n_blk)
    head_ix = jnp.arange(H)[None, :, None]

    def block(i):
        t0 = i * MOBA_Q_BLOCK
        qi = lax.dynamic_slice_in_dim(q, t0, MOBA_Q_BLOCK, 0)
        qpos = t0 + jnp.arange(MOBA_Q_BLOCK)
        own = t0 // MOBA_BLOCK
        k_own = lax.dynamic_index_in_dim(kb, own, axis=1, keepdims=False)
        v_own = lax.dynamic_index_in_dim(vb, own, axis=1, keepdims=False)
        own_pos = own * MOBA_BLOCK + offs
        s_own = jnp.einsum('thd,hkd->thk', qi, k_own, preferred_element_type=jnp.float32) * scale
        s_own = s_own - slopes[None, :, None] * (qpos[:, None] - own_pos[None, :]).astype(jnp.float32)[:, None, :]
        s_own = jnp.where((own_pos[None, :] <= qpos[:, None])[:, None, :], s_own, -jnp.inf)
        if n_sel == 0:
            p = jax.nn.softmax(s_own, axis=-1).astype(v.dtype)
            return jnp.einsum('thk,hkd->thd', p, v_own)
        gate = jnp.einsum('thd,hnd->thn', qi.astype(jnp.float32), k_mean)
        gate = jnp.where(blk_ids[None, None, :] < own, gate, -jnp.inf)
        _, sel = lax.top_k(gate, n_sel)
        k_sel = kb[head_ix, sel]
        v_sel = vb[head_ix, sel].reshape(MOBA_Q_BLOCK, H, n_past, Dh)
        pos_sel = sel[..., None] * MOBA_BLOCK + offs
        s_sel = jnp.einsum('thd,thnkd->thnk', qi, k_sel, preferred_element_type=jnp.float32) * scale
        s_sel = s_sel - slopes[None, :, None, None] * (qpos[:, None, None, None] - pos_sel).astype(jnp.float32)
        s_sel = jnp.where((sel < own)[..., None], s_sel, -jnp.inf).reshape(MOBA_Q_BLOCK, H, n_past)
        s = jnp.concatenate([s_sel, s_own], axis=-1)
        p = jax.nn.softmax(s, axis=-1).astype(v.dtype)
        return (jnp.einsum('thk,thkd->thd', p[..., :n_past], v_sel)
                + jnp.einsum('thk,hkd->thd', p[..., n_past:], v_own))

    o = lax.map(block, jnp.arange(S // MOBA_Q_BLOCK))
    return o.reshape(S, H * Dh)

def hybrid_mixer(x, w_in, b_gate, kv_norm_g, idx_k_norm_g, idx_k_norm_b, w_uk, w_uv, w_o_dsa, w_o_moba, w_out):
    B, S, _ = x.shape
    points = np.cumsum(SPLIT_SIZES)[:-1].tolist()
    proj = x @ w_in
    q_dsa, c_kv, q_idx, k_idx, w_idx, q_m, k_m, v_m, ga, gb = jnp.split(proj, points, axis=-1)
    c_kv = rms_norm(c_kv, kv_norm_g)
    k_idx = layer_norm(k_idx, idx_k_norm_g, idx_k_norm_b)
    q_dsa = q_dsa.reshape(B, S, N_HEADS_DSA, HEAD_DIM)
    q_idx = q_idx.reshape(B, S, IDX_HEADS, IDX_DIM)
    o_a = jax.vmap(dsa_attention, in_axes=(0, 0, 0, 0, 0, None, None))(q_dsa, c_kv, q_idx, k_idx, w_idx, w_uk, w_uv)
    hm = (B, S, N_HEADS_MOBA, HEAD_DIM)
    o_b = jax.vmap(moba_attention)(q_m.reshape(hm), k_m.reshape(hm), v_m.reshape(hm))
    g_a = jax.nn.sigmoid(ga + b_gate[0])
    g_b = jax.nn.sigmoid(gb + b_gate[1])
    merged = g_a * (o_a @ w_o_dsa) + g_b * (o_b @ w_o_moba)
    return merged @ w_out

def mem_cross_attention(x, mem, w_q, w_kv, w_o):
    B, S, _ = x.shape
    q = (x @ w_q).reshape(B, S, N_HEADS_MEM, HEAD_DIM)
    k, v = jnp.split(mem @ w_kv, 2, axis=-1)
    k = k.reshape(B, N_MEM, N_HEADS_MEM, HEAD_DIM)
    v = v.reshape(B, N_MEM, N_HEADS_MEM, HEAD_DIM)
    s = jnp.einsum('bshd,bmhd->bhsm', q, k, preferred_element_type=jnp.float32) * (HEAD_DIM ** -0.5)
    p = jax.nn.softmax(s, axis=-1).astype(x.dtype)
    o = jnp.einsum('bhsm,bmhd->bshd', p, v).reshape(B, S, MEM_WIDTH)
    return o @ w_o

def swiglu(x, w_in, w_out):
    g, u = jnp.split(x @ w_in, 2, axis=-1)
    return (jax.nn.silu(g) * u) @ w_out

def first_inputs(seed: int = 0) -> dict:
    key = jax.random.key(seed)
    ks = jax.random.split(key, 20)
    f32 = jnp.float32

    def nrm(k, shape, scale):
        return jax.random.normal(k, shape, f32) * scale

    v_off = sum(SPLIT_SIZES[:7])
    col_scale = jnp.ones((IN_WIDTH,), f32).at[v_off:v_off + MOBA_WIDTH].set(BETA)
    kv_scale = jnp.ones((2 * MEM_WIDTH,), f32).at[MEM_WIDTH:].set(BETA)
    return {
        'x': nrm(ks[0], (BATCH, SEQ, D_MODEL), 1.0),
        'mem': nrm(ks[1], (BATCH, N_MEM, D_MODEL), 1.0),
        'w_in': nrm(ks[2], (DEPTH, D_MODEL, IN_WIDTH), D_MODEL ** -0.5) * col_scale,
        'b_gate': nrm(ks[3], (DEPTH, 2, D_MODEL), 0.02),
        'kv_norm_g': 1.0 + nrm(ks[4], (DEPTH, KV_LATENT), 0.02),
        'idx_k_norm_g': 1.0 + nrm(ks[5], (DEPTH, IDX_DIM), 0.02),
        'idx_k_norm_b': nrm(ks[6], (DEPTH, IDX_DIM), 0.02),
        'w_uk': nrm(ks[7], (DEPTH, N_HEADS_DSA, HEAD_DIM, KV_LATENT), HEAD_DIM ** -0.5),
        'w_uv': nrm(ks[8], (DEPTH, N_HEADS_DSA, KV_LATENT, HEAD_DIM), BETA * KV_LATENT ** -0.5),
        'w_o_dsa': nrm(ks[9], (DEPTH, DSA_WIDTH, D_MODEL), BETA * DSA_WIDTH ** -0.5),
        'w_o_moba': nrm(ks[10], (DEPTH, MOBA_WIDTH, D_MODEL), BETA * MOBA_WIDTH ** -0.5),
        'w_out': nrm(ks[11], (DEPTH, D_MODEL, D_MODEL), BETA * D_MODEL ** -0.5),
        'w_q_mem': nrm(ks[12], (DEPTH, D_MODEL, MEM_WIDTH), D_MODEL ** -0.5),
        'w_kv_mem': nrm(ks[13], (DEPTH, D_MODEL, 2 * MEM_WIDTH), D_MODEL ** -0.5) * kv_scale,
        'w_o_mem': nrm(ks[14], (DEPTH, MEM_WIDTH, D_MODEL), BETA * MEM_WIDTH ** -0.5),
        'w_ffn_in': nrm(ks[15], (DEPTH, D_MODEL, 2 * D_FF), BETA * D_MODEL ** -0.5),
        'w_ffn_out': nrm(ks[16], (DEPTH, D_FF, D_MODEL), BETA * D_FF ** -0.5),
        'ln_g': 1.0 + nrm(ks[17], (DEPTH, 3, D_MODEL), 0.02),
        'ln_b': nrm(ks[18], (DEPTH, 3, D_MODEL), 0.02),
    }

def first_block(x, mem, w_in, b_gate, kv_norm_g, idx_k_norm_g, idx_k_norm_b, w_uk, w_uv, w_o_dsa, w_o_moba,
              w_out, w_q_mem, w_kv_mem, w_o_mem, w_ffn_in, w_ffn_out, ln_g, ln_b):
    for l in range(DEPTH):
        y = hybrid_mixer(x, w_in[l], b_gate[l], kv_norm_g[l], idx_k_norm_g[l], idx_k_norm_b[l], w_uk[l], w_uv[l],
                         w_o_dsa[l], w_o_moba[l], w_out[l])
        x = layer_norm(ALPHA * x + y, ln_g[l, 0], ln_b[l, 0])
        y = mem_cross_attention(x, mem, w_q_mem[l], w_kv_mem[l], w_o_mem[l])
        x = layer_norm(ALPHA * x + y, ln_g[l, 1], ln_b[l, 1])
        y = swiglu(x, w_ffn_in[l], w_ffn_out[l])
        x = layer_norm(ALPHA * x + y, ln_g[l, 2], ln_b[l, 2])
    return x


D_MIX = D_MODEL
D_FOURIER = D_MIX // 2
N_FOURIER_GROUPS = 4
FOURIER_GROUP = D_FOURIER // N_FOURIER_GROUPS
D_MLSTM = D_MIX - D_FOURIER
N_MLSTM_HEADS = 4
HEAD_V = D_MLSTM // N_MLSTM_HEADS
HEAD_QK = HEAD_V // 2
D_QK = N_MLSTM_HEADS * HEAD_QK
N_GATES = 4 * N_MLSTM_HEADS
D_IN = D_FOURIER + 2 * D_QK + 2 * D_MLSTM + N_GATES
CHUNK = 64
D_FF_2 = 5632
CONV_W = 3
N_MOD = 6
EPS = 1e-6
M_INIT = -1e30


def rms_norm_2(x, w):
    xf = x.astype(jnp.float32)
    y = xf * lax.rsqrt(jnp.mean(xf * xf, axis=-1, keepdims=True) + EPS)
    return (y * w.astype(jnp.float32)).astype(x.dtype)

def modulate(h, shift, scale):
    return h * (1 + scale[:, None, :]) + shift[:, None, :]

def fourier_mix(u):
    B, S, _ = u.shape
    ug = u.astype(jnp.float32).reshape(B, S, N_FOURIER_GROUPS, FOURIER_GROUP)
    y = jnp.fft.fft2(ug, axes=(1, 3), norm="ortho").real
    return y.reshape(B, S, D_FOURIER).astype(u.dtype)

def mlstm_chunkwise(q, k, v, ig, fg):
    B, H, S, Dk = q.shape
    Dv = v.shape[-1]
    NC = S // CHUNK
    lf = jax.nn.log_sigmoid(fg)
    q = q.reshape(B, H, NC, CHUNK, Dk) * (Dk ** -0.5)
    k = k.reshape(B, H, NC, CHUNK, Dk)
    v = v.reshape(B, H, NC, CHUNK, Dv)
    ig = ig.reshape(B, H, NC, CHUNK)
    lf = lf.reshape(B, H, NC, CHUNK)
    b = jnp.cumsum(lf, axis=-1)
    g = b[..., -1]

    a = g[..., None] - b + ig
    m_loc = jnp.max(a, axis=-1)
    w_loc = jnp.exp(a - m_loc[..., None])
    C_loc = jnp.einsum('bhclv,bhclk->bhcvk', v * w_loc[..., None], k)
    n_loc = jnp.einsum('bhcl,bhclk->bhck', w_loc, k)

    def step(carry, inp):
        C, n, m = carry
        g_c, m_c, C_c, n_c = inp
        m_new = jnp.maximum(g_c + m, m_c)
        s_old = jnp.exp(g_c + m - m_new)
        s_loc = jnp.exp(m_c - m_new)
        C_new = s_old[..., None, None] * C + s_loc[..., None, None] * C_c
        n_new = s_old[..., None] * n + s_loc[..., None] * n_c
        return (C_new, n_new, m_new), (C, n, m)

    init = (jnp.zeros((B, H, Dv, Dk), jnp.float32),
            jnp.zeros((B, H, Dk), jnp.float32),
            jnp.full((B, H), M_INIT, jnp.float32))
    xs = (jnp.moveaxis(g, 2, 0), jnp.moveaxis(m_loc, 2, 0),
          jnp.moveaxis(C_loc, 2, 0), jnp.moveaxis(n_loc, 2, 0))
    _, (C_st, n_st, m_st) = lax.scan(step, init, xs)
    C_st = jnp.moveaxis(C_st, 0, 2)
    n_st = jnp.moveaxis(n_st, 0, 2)
    m_st = jnp.moveaxis(m_st, 0, 2)

    tri = jnp.tril(jnp.ones((CHUNK, CHUNK), dtype=bool))
    Dlog = jnp.where(tri, b[..., :, None] - b[..., None, :] + ig[..., None, :], -jnp.inf)
    inter = b + m_st[..., None]
    m_row = jnp.maximum(jnp.max(Dlog, axis=-1), inter)
    P = jnp.exp(Dlog - m_row[..., None]) * jnp.einsum('bhcjd,bhctd->bhcjt', q, k)
    s_inter = jnp.exp(inter - m_row)
    num = (jnp.einsum('bhcjt,bhctv->bhcjv', P, v)
           + s_inter[..., None] * jnp.einsum('bhcjk,bhcvk->bhcjv', q, C_st))
    den = jnp.sum(P, axis=-1) + s_inter * jnp.einsum('bhcjk,bhck->bhcj', q, n_st)
    h = num / jnp.maximum(jnp.abs(den), jnp.exp(-m_row))[..., None]
    return h.reshape(B, H, S, Dv)

def mlstm_bidirectional(q_in, k_in, v_in, gates, mlstm_norm_w):
    B, S, _ = q_in.shape
    H = N_MLSTM_HEADS
    q = q_in.astype(jnp.float32).reshape(B, S, H, HEAD_QK).transpose(0, 2, 1, 3)
    k = k_in.astype(jnp.float32).reshape(B, S, H, HEAD_QK).transpose(0, 2, 1, 3)
    v = v_in.astype(jnp.float32).reshape(B, S, H, HEAD_V).transpose(0, 2, 1, 3)
    gt = gates.astype(jnp.float32).reshape(B, S, 4, H).transpose(2, 0, 3, 1)
    i_f, f_f, i_b, f_b = gt[0], gt[1], gt[2], gt[3]
    h_fwd = mlstm_chunkwise(q, k, v, i_f, f_f)
    h_bwd = jnp.flip(mlstm_chunkwise(jnp.flip(q, 2), jnp.flip(k, 2), jnp.flip(v, 2),
                                     jnp.flip(i_b, 2), jnp.flip(f_b, 2)), 2)
    h = (h_fwd + h_bwd).transpose(0, 2, 1, 3)
    h = h * lax.rsqrt(jnp.mean(h * h, axis=-1, keepdims=True) + EPS)
    h = h.reshape(B, S, D_MLSTM) * mlstm_norm_w.astype(jnp.float32)
    return h.astype(q_in.dtype)

def depthwise_conv_centred(u, w_conv, b_conv):
    C = u.shape[-1]
    y = lax.conv_general_dilated(u, w_conv[:, None, :].astype(u.dtype), window_strides=(1,),
                                 padding='SAME', dimension_numbers=('NWC', 'WIO', 'NWC'),
                                 feature_group_count=C)
    return y + b_conv

def second_inputs(seed: int = 0) -> dict:
    key = jax.random.key(seed)
    ks = jax.random.split(key, 20)
    f32 = jnp.float32
    H = N_MLSTM_HEADS
    x = jax.random.normal(ks[0], (BATCH, SEQ, D_MODEL), f32)
    c = jax.random.normal(ks[1], (BATCH, D_MODEL), f32)
    w_ada = jax.random.normal(ks[2], (D_MODEL, N_MOD * D_MODEL), f32) * (0.5 * D_MODEL ** -0.5)
    b_ada = 0.02 * jax.random.normal(ks[3], (N_MOD * D_MODEL,), f32)
    norm1_w = 1.0 + 0.02 * jax.random.normal(ks[4], (D_MODEL,), f32)
    w_in = jax.random.normal(ks[5], (D_MODEL, D_IN), f32) * (D_MODEL ** -0.5)
    bi_f = -1.0 + 0.1 * jax.random.normal(ks[6], (H,), f32)
    bf_f = jnp.linspace(3.0, 6.0, H, dtype=f32) + 0.1 * jax.random.normal(ks[7], (H,), f32)
    bi_b = -1.0 + 0.1 * jax.random.normal(ks[8], (H,), f32)
    bf_b = jnp.linspace(3.0, 6.0, H, dtype=f32) + 0.1 * jax.random.normal(ks[9], (H,), f32)
    b_gates = jnp.concatenate([bi_f, bf_f, bi_b, bf_b])
    mlstm_norm_w = 1.0 + 0.02 * jax.random.normal(ks[10], (D_MLSTM,), f32)
    w_out = jax.random.normal(ks[11], (D_MIX, D_MODEL), f32) * (D_MIX ** -0.5)
    norm2_w = 1.0 + 0.02 * jax.random.normal(ks[12], (D_MODEL,), f32)
    w_up = jax.random.normal(ks[13], (D_MODEL, 2 * D_FF_2), f32) * (D_MODEL ** -0.5)
    w_conv = jax.random.normal(ks[14], (CONV_W, 2 * D_FF_2), f32) * (CONV_W ** -0.5)
    b_conv = 0.02 * jax.random.normal(ks[15], (2 * D_FF_2,), f32)
    w_down = jax.random.normal(ks[16], (D_FF_2, D_MODEL), f32) * (D_FF_2 ** -0.5)
    norm_f_w = 1.0 + 0.02 * jax.random.normal(ks[17], (D_MODEL,), f32)
    return {"x": x, "c": c, "w_ada": w_ada, "b_ada": b_ada, "norm1_w": norm1_w,
            "w_in": w_in, "b_gates": b_gates, "mlstm_norm_w": mlstm_norm_w, "w_out": w_out,
            "norm2_w": norm2_w, "w_up": w_up, "w_conv": w_conv, "b_conv": b_conv,
            "w_down": w_down, "norm_f_w": norm_f_w}

def second_block(x, c, w_ada, b_ada, norm1_w, w_in, b_gates, mlstm_norm_w, w_out,
              norm2_w, w_up, w_conv, b_conv, w_down, norm_f_w):
    mod = jax.nn.silu(c) @ w_ada + b_ada
    shift1, scale1, gate1, shift2, scale2, gate2 = jnp.split(mod, N_MOD, axis=-1)
    o1 = D_FOURIER
    o2 = o1 + D_QK
    o3 = o2 + D_QK
    o4 = o3 + D_MLSTM
    o5 = o4 + D_MLSTM
    for _ in range(DEPTH):
        h = modulate(rms_norm_2(x, norm1_w), shift1, scale1)
        p = h @ w_in
        u_f = p[..., :o1]
        q_in, k_in, v_in = p[..., o1:o2], p[..., o2:o3], p[..., o3:o4]
        o_gate = jax.nn.sigmoid(p[..., o4:o5])
        gates = p[..., o5:] + b_gates
        y_f = fourier_mix(u_f)
        y_m = mlstm_bidirectional(q_in, k_in, v_in, gates, mlstm_norm_w) * o_gate
        mix = jnp.concatenate([y_f, y_m], axis=-1)
        x = x + gate1[:, None, :] * (mix @ w_out)
        h2 = modulate(rms_norm_2(x, norm2_w), shift2, scale2)
        u = depthwise_conv_centred(h2 @ w_up, w_conv, b_conv)
        a, v = jnp.split(u, 2, axis=-1)
        x = x + gate2[:, None, :] * ((jax.nn.silu(a) * v) @ w_down)
    return rms_norm_2(x, norm_f_w)


def setup_inputs(seed=0):
    out = dict(first_inputs(seed))
    for name, value in second_inputs(seed + 1).items():
        if name != "x":
            out[name + "_2"] = value
    return out


def reference(
    x, mem, w_in, b_gate, kv_norm_g, idx_k_norm_g, idx_k_norm_b, w_uk, w_uv, w_o_dsa, w_o_moba,
    w_out, w_q_mem, w_kv_mem, w_o_mem, w_ffn_in, w_ffn_out, ln_g, ln_b, c_2, w_ada_2, b_ada_2,
    norm1_w_2, w_in_2, b_gates_2, mlstm_norm_w_2, w_out_2, norm2_w_2, w_up_2, w_conv_2,
    b_conv_2, w_down_2, norm_f_w_2,
):
    x = first_block(
        x, mem, w_in, b_gate, kv_norm_g, idx_k_norm_g, idx_k_norm_b, w_uk, w_uv, w_o_dsa,
        w_o_moba, w_out, w_q_mem, w_kv_mem, w_o_mem, w_ffn_in, w_ffn_out, ln_g, ln_b,
    )
    return second_block(
        x, c_2, w_ada_2, b_ada_2, norm1_w_2, w_in_2, b_gates_2, mlstm_norm_w_2, w_out_2,
        norm2_w_2, w_up_2, w_conv_2, b_conv_2, w_down_2, norm_f_w_2,
    )


_drawn_inputs = setup_inputs


def setup_inputs(seed=0):
    import zlib

    import numpy as np

    out = dict(_drawn_inputs(seed))
    spreads = {}
    factors = {'b_gate': 8.0,
     'kv_norm_g': 8.0,
     'idx_k_norm_g': 8.0,
     'idx_k_norm_b': 8.0,
     'norm1_w_2': 8.0,
     'mlstm_norm_w_2': 28.144,
     'norm2_w_2': 8.0,
     'b_conv_2': 8.0,
     'norm_f_w_2': 7.681}
    for name, (base, spread) in spreads.items():
        noise = np.random.default_rng([zlib.crc32(name.encode()), seed]).standard_normal(out[name].shape)
        drawn = base * np.exp(spread * noise) if base else spread * noise
        out[name] = __import__('jax').numpy.asarray(drawn.astype(out[name].dtype))
    for name, factor in factors.items():
        out[name] = (out[name] * factor).astype(out[name].dtype)
    return out
```

```python
from contextlib import ExitStack

import numpy as np
import concourse.bass as bass
from concourse import mybir

F32 = mybir.dt.float32
F32R = mybir.dt.float32r
BF16 = mybir.dt.bfloat16
I32 = mybir.dt.int32
ALU = mybir.AluOpType
ACT = mybir.ActivationFunctionType
AX_X = mybir.AxisListType.X

P = 128
S = 256
T = S // P
D = 2048
KT = D // P
HD = 128
HEADS = 8
HEADS_MEM = 4
LATENT = 256
IDX_HEADS = 16
IDX_DIM = 64
TOPK = min(256, S // 4)
FF = 5632
FT = FF // P
FC = FF // 512
LH = 4
DV = 256
ADA = 6 * D // P
ALPHA = 2.0 ** 0.25
LN_EPS = 1e-5
RMS_EPS = 1e-6
OUT_OF_SIGHT = -1e30
TAKEN = -3e38

TILES = [("k_mem", 4), ("v_mem", 4), ("c_kv", 2), ("k_idx", 1), ("q_idx", 8), ("v_moba", 8), ("w_uk", 1), ("w_uv", 1),
         ("qk", 24), ("gates", 48), ("out1", 16), ("q_mem", 4), ("o_mem", 4), ("up1", 8 * FC), ("down1", FT),
         ("lstm_gates", 1), ("lstm_q", 4), ("lstm_k", 4), ("lstm_v", 8), ("lstm_o", 8), ("fourier", 8), ("out2", 16),
         ("up2", 8 * FC), ("down2", FT)]
CHUNKS = [("k_mem", 1), ("v_mem", 1), ("c_kv", 1), ("k_idx", 1), ("q_idx", 2), ("v_moba", 2), ("w_uk", 2), ("w_uv", 2),
          ("qk", 6), ("gates", 16), ("q_mem", 1), ("up1", 2 * FC), ("lstm_gates", 1), ("lstm_q", 1), ("lstm_k", 1),
          ("lstm_v", 2), ("lstm_o", 2), ("fourier", 2), ("up2", 2 * FC)]
WIDE = [("out1", 16), ("o_mem", 4), ("down1", FT), ("out2", 16), ("down2", FT)]
COLS = [("b_gate", 2 * KT), ("b_ada", ADA), ("norm1", KT), ("norm2", KT), ("norm_m", 8), ("w_conv", 3 * 2 * FT),
        ("b_conv", 2 * FT), ("slope", HEADS)]


def starts(parts):
    found, n = {}, 0
    for name, size in parts:
        found[name] = n
        n += size
    return found, n


AT, G = starts(TILES)
CH, _ = starts(CHUNKS)
SRC, _ = starts(WIDE)
COL, NCOL = starts(COLS)
ADA_QK, ADA_GATES, ADA_UP, ADA_DOWN = 2, 6, 4, 2
assert 3 * ADA_QK + 4 * ADA_GATES + FC * ADA_UP + (FT // 4) * ADA_DOWN == ADA
BLOCKS = [(0, 0, 0, 256, 0), (0, 1, 128, 256, 256), (1, 0, 0, 128, 384), (1, 1, 0, 256, 512)]


class Order:

    def __init__(self, eng, sem):
        self.eng, self.sem, self.n, self.i, self.per = eng, sem, 0, None, 0

    def mark(self, ins):
        ins.then_inc(self.sem, 1)
        self.n += 1

    def wait(self):
        self.eng.wait_ge(self.sem, at(self.n, self.i, self.per))

    def enter(self, i, per):
        self.i, self.per, self.n0 = i, per, self.n

    def leave(self, turns):
        assert self.n - self.n0 == self.per, (self.n - self.n0, self.per)
        self.i, self.n = None, self.n0 + turns * self.per


def at(first, i=None, per=0):
    return first if i is None else i * per + first


def two_blocks(nc, x, mem, stream, w_ada, cols, rows, ln_g, ln_b, norm_f, c_row, gate_bias, dft, out):
    with ExitStack() as ctx:
        def sem(name):
            return ctx.enter_context(nc.semaphore(name))

        place = [16512]

        def sb(name, shape, dt=F32, offset=None):
            here = place[0] if offset is None else offset
            if offset is None:
                size = int(np.prod(shape[1:])) * (2 if dt == BF16 else 4)
                place[0] += -(-size // 32) * 32
            return nc.alloc_sbuf_tensor_at(name, shape, dt, offset=here)

        raw = [sb(f"raw{s}", [P, D]) for s in range(4)]
        whi = sb("whi", [P, 4, 1024], F32R)
        wlo = sb("wlo", [P, 4, 1024], F32R)
        at_xhi = place[0]
        xhi = sb("xhi", [P, KT, S], F32R)
        at_xlo = place[0]
        xlo = sb("xlo", [P, KT, S], F32R)
        at_res = place[0]
        res = sb("res", [P, T, D])
        ident = sb("ident", [P, P])
        ones = sb("ones", [P, P])
        zeros = sb("zeros", [P, 512], BF16)
        dist = sb("dist", [P, 384])
        causal = sb("causal", [P, 384])
        chosen = sb("chosen", [P, 384])
        col = sb("col", [P, NCOL])
        row = sb("row", [P, LATENT + 2 * IDX_DIM])
        mod = sb("mod", [P, ADA])
        scale_col = sb("scale_col", [P, KT])
        expo = sb("expo", [P, 4])
        small = sb("small", [P, 128])
        at_pool = place[0]
        at_pool2 = at_pool + 49152
        shi = sb("shi", [P, 4, S], F32R, at_xhi)
        slo = sb("slo", [P, 4, S], F32R, at_xhi + 4096)
        gate_row = sb("gate_row", [P, D], F32, at_xhi + 8192)
        gamma = sb("gamma", [P, D], F32, at_xlo)
        beta = sb("beta", [P, D], F32, at_xlo + 8192)
        qk = sb("qk", [P, 32, S], F32, at_pool)
        ohi = sb("ohi", [P, 16, S], F32R, at_pool)
        olo = sb("olo", [P, 16, S], F32R, at_pool + 16384)
        vall = sb("vall", [P, T, D], F32, at_pool + 32768)
        mem_nat = sb("mem_nat", [P, T, D], F32, at_pool + 32768)
        merged = sb("merged", [P, KT, S], F32, at_pool + 32768)
        ckv = sb("ckv", [P, T, LATENT], F32, at_pool)
        kw = sb("kw", [P, T, IDX_DIM + IDX_HEADS], F32, at_pool + 2048)
        kn = sb("kn", [P, T, 2 * IDX_DIM], F32, at_pool + 3072)
        kc = sb("kc", [P, T, IDX_DIM], F32, at_pool + 4096)
        ksq = sb("ksq", [P, T, IDX_DIM], F32, at_pool + 4608)
        qi = sb("qi", [P, 8, S], F32, at_res)
        idx_r = sb("idx_r", [P, 2, 512], F32, at_res + 8192)
        score = sb("score", [P, T, S], F32, at_res + 12288)
        best8 = sb("best8", [P, T, 8], F32, at_res + 14336)
        wi = sb("wi", [P, T, IDX_HEADS], F32, at_res + 14400)
        kiT = sb("kiT", [P, S], F32, at_res + 14592)
        qs = sb("qs", [P, 2, S], F32, at_res)
        vs = sb("vs", [P, 2, T, HD], F32, at_res + 2048)
        att_ab = sb("att_ab", [P, 2, 384], F32, at_res + 4096)
        att_s = sb("att_s", [P, 2, 384], F32, at_res + 7168)
        att_e = sb("att_e", [P, 2, 384], F32, at_res + 10240)
        att_pT = sb("att_pT", [P, 2, 384], F32, at_res + 13312)
        sig = sb("sig", [P, 1024], F32, at_res)
        gated_a = sb("gated_a", [P, 1024], F32, at_res + 4096)
        gated_b = sb("gated_b", [P, 1024], F32, at_res + 8192)
        place[0] = at_pool2
        kmT = sb("kmT", [P, HEADS_MEM, S])
        vm = sb("vm", [P, T, HEADS_MEM * HD])
        cb = sb("cb", [P, D])
        ada = [sb(f"ada{s}", [P, D]) for s in range(2)]
        at_end = place[0]
        assert at_end <= 229344, at_end
        ckhi = sb("ckhi", [P, 2, S], F32R, at_pool + 8192)
        cklo = sb("cklo", [P, 2, S], F32R, at_pool + 10240)
        qmT = sb("qmT", [P, HEADS_MEM, S], F32, at_pool)
        omT = sb("omT", [P, HEADS_MEM, S], F32, at_pool + 4096)
        mem_p = sb("mem_p", [P, 2, T * S], F32, at_pool + 8192)
        mem_pT = sb("mem_pT", [P, 2, T * S], F32, at_pool + 12288)
        hid = sb("hid", [P, FT, S], F32, at_pool)
        silu = sb("silu", [P, 1024], F32, at_pool2)
        conv = sb("conv", [P, 2, 1024], F32, at_pool2 + 4096)
        diag = sb("diag", [P, KT, P], F32, at_pool2 + 12288)
        xn = sb("xn", [P, T, D], F32, at_pool)
        modulated = sb("modulated", [P, 2, 512], F32, at_pool + 16384)
        so = sb("so", [P, 8, S], F32, at_pool + 16384)
        lq = sb("lq", [P, LH, S], F32, at_pool + 24576)
        lk = sb("lk", [P, LH, S], F32, at_pool + 28672)
        mixT = sb("mixT", [P, KT, S], F32, at_pool + 32768)
        uf = sb("uf", [P, T, 1024], F32, at_pool2)
        lv = sb("lv", [P, T, LH, DV + 2], F32, at_pool2 + 8192)
        dftc = sb("dftc", [P, T, 768], F32, at_pool2 + 16448)
        fa = sb("fa", [P, 2, 512], F32, at_pool2 + 22592)
        tri = sb("tri", [P, 768], F32, at_pool2 + 26688)
        sel = sb("sel", [LH, LH, P], F32, at_pool2 + 29760)
        lcols = sb("lcols", [P, 2, 16], F32, at_pool2 + 31808)
        gbias = sb("gbias", [LH, 4], F32, at_pool2 + 31936)
        gn = sb("gn", [P, T, 16], F32, at_pool2 + 31968)
        lx = sb("lx", [P, 768], F32, at_pool)
        le = sb("le", [P, 768], F32, at_pool + 3072)
        lp = sb("lp", [P, 768], F32, at_pool + 6144)
        lh = sb("lh", [P, T, DV], F32, at_pool + 9216)
        g_in = sb("g_in", [LH, 2, S], F32, at_pool)
        g_fo = sb("g_fo", [LH, 2, S], F32, at_pool + 2048)
        g_e = sb("g_e", [LH, 2, S], F32, at_pool + 4096)
        g_sum = sb("g_sum", [LH, 2, S], F32, at_pool + 6144)
        g_a = sb("g_a", [LH, 2, S], F32, at_pool + 8192)
        g_max = sb("g_max", [LH, 2, S], F32, at_pool + 11264)
        g_m = sb("g_m", [LH, 2, S], F32, at_pool + 13312)
        iota_i = sb("iota_i", [P, 384], I32, at_pool)

        ps = ctx.enter_context(nc.psum_tensor("ps", [P, 8, 512], F32))

        def var(n, t=0, w=1):
            return small[:, 2 * n + t:2 * n + t + w]

        def rstd(n, t=0, w=1):
            return small[:, 40 + 2 * n + t:40 + 2 * n + t + w]

        def misc(n, w=1):
            return small[:, 80 + n:80 + n + w]

        raw_landed = [sem(f"raw_landed{s}") for s in range(4)]
        hi_ready = sem("hi_ready")
        lo_ready = sem("lo_ready")
        weights_used = sem("weights_used")
        pair_read = [sem(f"pair_read{p}") for p in range(2)]
        x_landed = sem("x_landed")
        mem_landed = sem("mem_landed")
        consts_landed = sem("consts_landed")
        late_landed = sem("late_landed")
        cb_landed = sem("cb_landed")
        cb_ready = sem("cb_ready")
        ln_landed = sem("ln_landed")
        ada_landed = [sem(f"ada_landed{s}") for s in range(2)]
        ada_used = sem("ada_used")
        built = sem("built")
        xT_done = sem("xT_done")
        xhi_ready = sem("xhi_ready")
        xlo_ready = sem("xlo_ready")
        shi_ready = sem("shi_ready")
        slo_ready = sem("slo_ready")
        var_ready = sem("var_ready")
        rstd_ready = sem("rstd_ready")
        mean_ready = sem("mean_ready")
        sq_ready = sem("sq_ready")
        res_ready = sem("res_ready")
        xn_ready = sem("xn_ready")
        mod_ready = sem("mod_ready")
        ck_squared = sem("ck_squared")
        ck_ready = sem("ck_ready")
        kn_ready = sem("kn_ready")
        small_T = sem("small_T")
        ckhi_ready = sem("ckhi_ready")
        cklo_ready = sem("cklo_ready")
        ki_ready = sem("ki_ready")
        idx_done = sem("idx_done")
        idx_relu = sem("idx_relu")
        idx_added = sem("idx_added")
        qv_ready = sem("qv_ready")
        att_free = sem("att_free")
        att_scores = sem("att_scores")
        att_max = sem("att_max")
        att_exp = sem("att_exp")
        att_p = sem("att_p")
        att_T = sem("att_T")
        att_pT_ready = sem("att_pT_ready")
        att_o = sem("att_o")
        att_ohi = sem("att_ohi")
        merged_ready = sem("merged_ready")
        m_scores = sem("m_scores")
        m_max = sem("m_max")
        m_exp = sem("m_exp")
        m_p = sem("m_p")
        m_T = sem("m_T")
        m_pT = sem("m_pT")
        m_o = sem("m_o")
        m_out = sem("m_out")
        conv_mid = sem("conv_mid")
        conv_done = sem("conv_done")
        silu_ready = sem("silu_ready")
        g_copied = sem("g_copied")
        g_rows_T = sem("g_rows_T")
        g_abs = sem("g_abs")
        g_exp = sem("g_exp")
        g_one = sem("g_one")
        g_ln = sem("g_ln")
        g_stab = sem("g_stab")
        g_floor = sem("g_floor")
        g_cols_T = sem("g_cols_T")
        g_cols = sem("g_cols")
        l_bc = sem("l_bc")
        l_x = sem("l_x")
        l_e = sem("l_e")
        l_st = sem("l_st")
        l_p = sem("l_p")
        l_num = sem("l_num")
        l_h = sem("l_h")
        l_sq = sem("l_sq")
        l_hn = sem("l_hn")
        l_hT = sem("l_hT")
        mix_m = sem("mix_m")
        f_first = sem("f_first")
        f_copied = sem("f_copied")
        f_second = sem("f_second")
        mix_f = sem("mix_f")
        diag_ready = sem("diag_ready")
        gate_T = sem("gate_T")
        gate_ready = sem("gate_ready")
        out_ready = sem("out_ready")
        out_landed = sem("out_landed")
        act_order = sem("act_order")
        dve_order = sem("dve_order")

        def through(g, half=2):
            return 2 * g + half

        def pair(c):
            return ps[:, 2 * (c % 2):2 * (c % 2) + 2, :].rearrange("p b n -> p (b n)")

        def reads(c):
            return c // 2 + 1

        block = ctx.enter_context(nc.Block())

        @block.sync
        def _(sp):
            sp.dma_start(mem_nat[:], mem.rearrange("(t p) d -> p t d", p=P)).then_inc(mem_landed, 16)
            for s in range(4):
                sp.dma_start(raw[s][:], stream[s]).then_inc(raw_landed[s], 16)
            sp.dma_start(res[:], x.rearrange("(t p) d -> p t d", p=P)).then_inc(x_landed, 16)
            with sp.Fori(1, G // 4) as i:
                for s in range(4):
                    sp.wait_ge(lo_ready, at(2 * s - 6, i, 8))
                    sp.dma_start(raw[s][:], stream[at(s, i, 4)]).then_inc(raw_landed[s], 16)
            for g in range(G // 4 * 4, G):
                sp.wait_ge(lo_ready, 2 * (g - 4) + 2)
                sp.dma_start(raw[g % 4][:], stream[g]).then_inc(raw_landed[g % 4], 16)
            for t in range(T):
                sp.wait_ge(out_ready, t + 1)
                sp.dma_start(out[t * P:(t + 1) * P, :], xn[:, t]).then_inc(out_landed, 16)
            sp.wait_ge(out_landed, 16 * T)

        @block.gpsimd
        def _(pool):
            pool.memset(ident[:], 0.0).then_inc(built, 1)
            pool.memset(ones[:], 1.0).then_inc(built, 1)
            pool.memset(zeros[:], 0.0).then_inc(built, 1)
            pool.memset(expo[:], -0.5).then_inc(built, 1)
            pool.memset(causal[:], 0.0).then_inc(built, 1)
            pool.wait_ge(built, 5)
            pool.affine_select(out=ident[:], in_=ident[:], compare_op=ALU.not_equal, fill=1.0, base=0,
                               pattern=[[-1, P]], channel_multiplier=1).then_inc(built, 1)
            for q0, c0, c1 in ((0, 0, 128), (128, 128, 384)):
                pool.affine_select(out=causal[:, c0:c1], in_=causal[:, c0:c1], compare_op=ALU.is_ge, fill=OUT_OF_SIGHT,
                                   base=q0, pattern=[[-1, c1 - c0]], channel_multiplier=1).then_inc(built, 1)
                pool.iota(iota_i[:, c0:c1], pattern=[[1, c1 - c0]], base=-q0, channel_multiplier=-1).then_inc(built, 1)
            pool.wait_ge(built, 10)
            pool.tensor_copy(dist[:], iota_i[:]).then_inc(built, 1)

            def power(n, w):
                pool.wait_ge(var_ready, n + 1)
                pool.tensor_tensor(rstd(n, 0, w), var(n, 0, w), expo[:, 0:w], ALU.pow).then_inc(rstd_ready, 1)

            for n in range(2):
                pool.dma_start(ada[n][:], w_ada[n]).then_inc(ada_landed[n], 16)
            power(0, 2)
            power(1, 2)

            def ada_turns(n0, turns, per):
                with pool.Fori(0, turns) as i:
                    for s in range(per):
                        pool.wait_ge(ada_used, at(n0 + s - 1, i, per))
                        pool.wait_ge(built, 11)
                        pool.dma_start(ada[s % 2][:], w_ada[at(n0 + s, i, per)]).then_inc(ada_landed[s % 2], 16)

            first = 3 * ADA_QK + 4 * ADA_GATES
            ada_turns(2, first // 2, 2)
            power(2, 1)
            power(3, 1)
            power(4, 1)
            power(5, 1)
            ada_turns(first + 2, (ADA - first - 2) // 2, 2)
            pool.wait_ge(ada_used, ADA)
            pool.dma_start(dftc[:], dft.rearrange("(t p) n -> p t n", p=P)).then_inc(late_landed, 16)
            pool.dma_start(gbias[:], gate_bias).then_inc(late_landed, 16)
            pool.memset(tri[:], 1.0).then_inc(built, 1)
            pool.memset(sel[:], 0.0).then_inc(built, 1)
            pool.memset(lv[:, :, :, DV:DV + 2], 1.0).then_inc(built, 1)
            pool.wait_ge(built, 14)
            for d, st, t0, t1, c0 in BLOCKS:
                sign = 1 if d == 0 else -1
                pool.affine_select(out=tri[:, c0:c0 + t1 - t0], in_=tri[:, c0:c0 + t1 - t0], compare_op=ALU.is_ge,
                                   fill=0.0, base=sign * (t0 - P * st), pattern=[[sign, t1 - t0]],
                                   channel_multiplier=-sign).then_inc(built, 1)
            pool.affine_select(out=sel[:], in_=sel[:], compare_op=ALU.not_equal, fill=1.0, base=0,
                               pattern=[[-1, LH], [0, P]], channel_multiplier=1).then_inc(built, 1)
            for n, w in [(6, 1), (7, 1), (8, 1), (9, 1), (10, 2), (11, 2), (12, 2), (13, 2), (14, 1), (15, 1), (16, 1), (17, 1)]:
                power(n, w)

        @block.scalar
        def _(act):
            order = Order(act, act_order)
            act.dma_start(col[:], cols).then_inc(consts_landed, 16)
            act.dma_start(row[:], rows.partition_broadcast(P)).then_inc(consts_landed, 16)
            act.dma_start(cb[:], c_row.partition_broadcast(P)).then_inc(cb_landed, 16)

            def params_in_place():
                act.wait_ge(consts_landed, 32)

            def upper(g, i=None, per=0):
                if g >= G:
                    return
                for half in range(2):
                    h = 2 * g + half
                    if half == 0:
                        act.wait_ge(raw_landed[g % 4], at(16 * (g // 4 + 1), i, 4 * per))
                    if h >= 4:
                        act.wait_ge(weights_used, at(h - 3, i, 2 * per))
                    act.activation(whi[:, h % 4], raw[g % 4][:, 1024 * half:1024 * half + 1024], ACT.Copy)\
                       .then_inc(hi_ready, 1)

            def x_upper(n):
                for b in range(8):
                    act.wait_ge(xT_done, 8 * n + b + 1)
                    act.activation(xhi[:, 2 * b:2 * b + 2].rearrange("p k t -> p (k t)"), ps[:, b], ACT.Copy)\
                       .then_inc(xhi_ready, 1)

            def x_upper_modulated(n, shift):
                act.wait_ge(mod_ready, n - 3)
                for b in range(8):
                    act.wait_ge(xT_done, 8 * n + b + 1)
                    if b >= 2:
                        act.wait_ge(xlo_ready, 8 * n + b - 1)
                    for f in range(2):
                        k = 2 * b + f
                        order.mark(act.activation(modulated[:, b % 2, S * f:S * f + S], ps[:, b, S * f:S * f + S], ACT.Identity,
                                                  bias=mod[:, shift + k:shift + k + 1], scale=scale_col[:, k:k + 1]))
                    order.wait()
                    act.activation(xhi[:, 2 * b:2 * b + 2].rearrange("p k t -> p (k t)"), modulated[:, b % 2], ACT.Copy)\
                       .then_inc(xhi_ready, 1)

            def read_out(c, g, dst, func=ACT.Copy, half=2, i=None, per=0):
                act.wait_ge(weights_used, at(through(g, half), i, 2 * per))
                if i is not None:
                    params_in_place()
                act.activation(dst, pair(c), func).then_inc(pair_read[c % 2], 1)

            def read_out_rows(c, g, dst, func=ACT.Copy, half=2):
                act.wait_ge(weights_used, through(g, half))
                act.activation(dst, ps[:, 2 * (c % 2):2 * (c % 2) + 2, :], func).then_inc(pair_read[c % 2], 1)

            def tiles4(tensor, k0):
                return tensor[:, k0:k0 + 4].rearrange("p k t -> p (k t)")

            upper(0)
            x_upper(0)
            for g in range(0, 4):
                upper(g + 1)
            read_out(CH["k_mem"], 3, tiles4(kmT, 0))
            for g in range(4, 8):
                upper(g + 1)
            read_out_rows(CH["v_mem"], 7, vm[:])
            x_upper(1)
            g0 = AT["c_kv"]
            upper(g0 + 1)
            upper(g0 + 2)
            act.wait_ge(pair_read[0], reads(CH["c_kv"]))
            for t in range(T):
                act.activation(idx_r[:, t, 0:LATENT], ckv[:, t], ACT.Square, accum_out=misc(t)).then_inc(ck_squared, 1)
            upper(g0 + 3)
            upper(g0 + 4)
            upper(g0 + 5)
            act.wait_ge(small_T, 1)
            act.activation(ckhi[:].rearrange("p c t -> p (c t)"), ps[:, 4], ACT.Copy).then_inc(ckhi_ready, 1)
            act.wait_ge(small_T, 2)
            act.activation(kiT[:], ps[:, 5, 0:S], ACT.Copy).then_inc(ki_ready, 1)
            for g in range(AT["q_idx"] + 2, AT["q_idx"] + 8):
                upper(g + 1)
                if g in (AT["q_idx"] + 3, AT["q_idx"] + 7):
                    c = CH["q_idx"] + (g > AT["q_idx"] + 3)
                    read_out(c, g, tiles4(qi, 4 * (c - CH["q_idx"])))
            for n in range(8):
                g = AT["v_moba"] + n
                upper(g + 1)
                for h in (2 * n, 2 * n + 1):
                    act.wait_ge(idx_done, h + 1)
                    if h >= 2:
                        act.wait_ge(idx_added, h - 1)
                    act.activation(idx_r[:, h % 2], ps[:, 4 + h % 4], ACT.Relu, scale=IDX_DIM ** -0.5).then_inc(idx_relu, 1)
                if n in (3, 7):
                    c = CH["v_moba"] + n // 4
                    read_out_rows(c, g, vall[:, :, 1024 + 512 * (n // 4):1536 + 512 * (n // 4)])
            g = AT["w_uk"]
            upper(g + 1)
            for n in range(2):
                read_out(CH["w_uk"] + n, g, tiles4(qk, 24 + 4 * n), half=n + 1)
            g = AT["w_uv"]
            upper(g + 1)
            for n in range(2):
                read_out_rows(CH["w_uv"] + n, g, vall[:, :, 512 * n:512 * n + 512], half=n + 1)
            act.wait_ge(cb_landed, 16)
            act.activation(cb[:], cb[:], ACT.Silu).then_inc(cb_ready, 1)
            g0 = AT["qk"]
            with act.Fori(0, 3) as i:
                for s in range(8):
                    upper(g0 + s + 1, i, 8)
                    if s % 4 == 3:
                        read_out(CH["qk"] + s // 4, g0 + s, qk[:, bass.ds(at(s - 3, i, 8), 4)].rearrange("p k t -> p (k t)"),
                                 i=i, per=8)

            with act.Fori(0, HEADS) as i:
                for j in range(2):
                    act.activation(qs[:, j], qk[:, at(8 * j, i, 1)], ACT.Copy).then_inc(qv_ready, 1)
                    act.activation(vs[:, j], vall[:, :, bass.ds(at(1024 * j, i, HD), HD)], ACT.Copy).then_inc(qv_ready, 1)
                for j in range(2):
                    for t, (c0, c1) in enumerate(((0, 128), (128, 384))):
                        act.wait_ge(att_max, at(2 * j + t + 1, i, 4))
                        act.activation(att_e[:, j, c0:c1], att_s[:, j, c0:c1], ACT.Exp, bias=misc(8 + 2 * j + t),
                                       accum_out=misc(12 + 2 * j + t)).then_inc(att_exp, 1)
                for j in range(2):
                    act.wait_ge(att_T, at(j + 1, i, 2))
                    act.activation(att_pT[:, j], ps[:, 6 + j, 0:384], ACT.Copy).then_inc(att_pT_ready, 1)
                act.wait_ge(att_o, at(2, i, 2))

            g0, c0 = AT["gates"], CH["gates"]
            with act.Fori(0, 4) as i:
                for s in range(12):
                    upper(g0 + s + 1, i, 12)
                    if s in (3, 9):
                        n = s // 6
                        act.wait_ge(weights_used, at(through(g0 + s), i, 24))
                        act.wait_ge(pair_read[1], at(reads(c0 + 2 * n - 1), i, 2))
                        params_in_place()
                        for m in range(4):
                            ins = act.activation(sig[:, S * m:S * m + S], pair(c0)[:, S * m:S * m + S], ACT.Sigmoid,
                                                 bias=col[:, bass.ds(at(COL["b_gate"] + KT * n + m, i, 4), 1)])
                        ins.then_inc(pair_read[0], 1)

            def wide_start(name, n_ln=None):
                act.wait_ge(weights_used, through(AT[name] - 1))
                if n_ln is not None:
                    act.dma_start(gamma[:], ln_g[n_ln:n_ln + 1].partition_broadcast(P)).then_inc(ln_landed, 16)
                    act.dma_start(beta[:], ln_b[n_ln:n_ln + 1].partition_broadcast(P)).then_inc(ln_landed, 16)

            def wide_turns(name, src, turns, i0=0):
                g0 = AT[name]

                def turn(i):
                    for s in range(4):
                        act.activation(shi[:, s], src[:, at(s, i, 4)], ACT.Copy).then_inc(shi_ready, 1)
                        upper(g0 + s + 1, i, 4)

                if turns == 1:
                    turn(None)
                else:
                    with act.Fori(0, turns) as i:
                        turn(i)

            def squares(n, src, count, centred):
                for t in range(T):
                    act.wait_ge(mean_ready if centred else res_ready, count + t + 1)
                    bias = misc(2 + t) if centred else 0.0
                    act.activation(ps[:, 4 * t:4 * t + 4].rearrange("p b n -> p (b n)"), src[:, t], ACT.Square, bias=bias,
                                   accum_out=misc(4 + t)).then_inc(sq_ready, 1)

            act.wait_ge(merged_ready, 4)
            act.dma_start(res[:], x.rearrange("(t p) d -> p t d", p=P)).then_inc(x_landed, 16)
            wide_start("out1", 0)
            wide_turns("out1", merged, 4)
            squares(2, res, 0, True)
            x_upper(2)
            g0 = AT["q_mem"]
            for g in range(g0, g0 + 4):
                upper(g + 1)
            read_out(CH["q_mem"], g0 + 3, tiles4(qmT, 0))

            def m_exps(h):
                act.wait_ge(m_max, h + 1)
                for t in range(T):
                    act.activation(mem_p[:, h % 2, S * t:S * t + S], ps[:, 4 + h % 2, S * t:S * t + S], ACT.Exp,
                                   bias=misc(8 + 2 * (h % 2) + t), scale=HD ** -0.5,
                                   accum_out=misc(12 + 2 * (h % 2) + t)).then_inc(m_exp, 1)

            m_exps(0)
            m_exps(1)
            for h in range(HEADS_MEM):
                act.wait_ge(m_T, h + 1)
                act.activation(mem_pT[:, h % 2], ps[:, 6 + h % 2], ACT.Copy).then_inc(m_pT, 1)
                act.wait_ge(m_o, h + 1)
                act.activation(omT[:, h], ps[:, 4 + h % 2, 0:S], ACT.Copy).then_inc(m_out, 1)
                if h + 2 < HEADS_MEM:
                    m_exps(h + 2)
            wide_start("o_mem", 1)
            act.wait_ge(m_out, HEADS_MEM)
            wide_turns("o_mem", omT, 1)
            squares(4, res, 2, True)
            x_upper(3)
            g0, c0 = AT["up1"], CH["up1"]
            with act.Fori(0, FC) as i:
                for s in range(8):
                    upper(g0 + s + 1, i, 8)
                    if s == 3:
                        act.wait_ge(weights_used, at(through(g0 + s), i, 16))
                        act.wait_ge(pair_read[(c0 + 1) % 2], at(reads(c0 - 1), i, 1))
                        act.activation(silu[:], pair(c0), ACT.Silu).then_inc(pair_read[c0 % 2], 1)
            wide_start("down1", 2)
            act.wait_ge(pair_read[(c0 + 1) % 2], reads(c0 + 2 * FC - 1))
            wide_turns("down1", hid, FC)
            squares(6, res, 4, True)
            squares(8, res, 4, False)
            x_upper_modulated(4, 0)
            g0 = AT["lstm_gates"]
            upper(g0 + 1)
            g0 = AT["lstm_q"]
            for g in range(g0, g0 + 4):
                upper(g + 1)
            read_out(CH["lstm_q"], g0 + 3, tiles4(lq, 0))
            act.wait_ge(g_abs, 1)
            act.activation(g_e[:], g_e[:], ACT.Exp, scale=-1.0).then_inc(g_exp, 1)
            g0 = AT["lstm_k"]
            for g in range(g0, g0 + 4):
                upper(g + 1)
            read_out(CH["lstm_k"], g0 + 3, tiles4(lk, 0))
            act.wait_ge(g_one, 1)
            act.activation(g_e[:], g_e[:], ACT.Ln).then_inc(g_ln, 1)
            g0 = AT["lstm_v"]
            for n in range(8):
                upper(g0 + n + 1)
                if n % 4 == 3:
                    c = CH["lstm_v"] + n // 4
                    act.wait_ge(weights_used, through(g0 + n))
                    if n == 3:
                        act.wait_ge(built, 14)
                    for t in range(T):
                        ins = act.activation(lv[:, t, 2 * (n // 4):2 * (n // 4) + 2, 0:DV],
                                             ps[:, 2 * (c % 2) + t].rearrange("p (h v) -> p h v", h=2), ACT.Copy)
                    ins.then_inc(pair_read[c % 2], 1)
            act.wait_ge(g_stab, 1)
            act.activation(g_m[:], g_m[:], ACT.Exp, scale=-1.0).then_inc(g_floor, 1)
            g0 = AT["lstm_o"]
            for n in range(8):
                upper(g0 + n + 1)
                if n % 4 == 3:
                    read_out(CH["lstm_o"] + n // 4, g0 + n, tiles4(so, 4 * (n // 4)), ACT.Sigmoid)
            g0 = AT["fourier"]
            for n in range(8):
                upper(g0 + n + 1)
                if n % 4 == 3:
                    read_out_rows(CH["fourier"] + n // 4, g0 + n, uf[:, :, 512 * (n // 4):512 * (n // 4) + 512])
            for h in range(LH):
                act.wait_ge(l_x, h + 1)
                act.activation(le[:], lx[:], ACT.Exp, scale=-1.0).then_inc(l_e, 1)
                for f in range(2):
                    act.wait_ge(f_first, 2 * h + f + 1)
                    act.activation(fa[:, f], ps[:, 2 + f], ACT.Copy).then_inc(f_copied, 1)
                act.wait_ge(f_second, h + 1)
                act.activation(mixT[:, 2 * h:2 * h + 2].rearrange("p k t -> p (k t)"), ps[:, 2], ACT.Copy).then_inc(mix_f, 1)
                for t in range(T):
                    act.wait_ge(l_h, 2 * h + t + 1)
                    act.activation(lx[:, S * t:S * t + S], lh[:, t], ACT.Square, accum_out=misc(16 + t)).then_inc(l_sq, 1)

            def gate_rows(n):
                act.wait_ge(gate_T, n + 1)
                act.activation(gate_row[:], ps[:, 4:8].rearrange("p b n -> p (b n)"), ACT.Copy).then_inc(gate_ready, 1)

            wide_start("out2")
            gate_rows(0)
            act.wait_ge(mix_m, 2 * LH)
            wide_turns("out2", mixT, 4)
            squares(14, res, 6, False)
            x_upper_modulated(5, 3 * KT)
            g0, c0 = AT["up2"], CH["up2"]
            with act.Fori(0, FC) as i:
                for s in range(8):
                    upper(g0 + s + 1, i, 8)
                    if s % 4 == 3:
                        q = s // 4
                        act.wait_ge(weights_used, at(through(g0 + s), i, 16))
                        if q == 0:
                            act.wait_ge(conv_done, at(1, i, 1))
                        params_in_place()
                        for m in range(4):
                            tap = at(COL["w_conv"] + 2 * FT + FT * q + m, i, 4)
                            bias = at(COL["b_conv"] + FT * q + m, i, 4)
                            ins = act.activation(conv[:, q, S * m:S * m + S], pair(c0 + q)[:, S * m:S * m + S], ACT.Identity,
                                                 bias=col[:, bass.ds(bias, 1)], scale=col[:, bass.ds(tap, 1)])
                        ins.then_inc(conv_mid, 1)
                    if s == 6:
                        act.wait_ge(pair_read[c0 % 2], at(reads(c0), i, 1))
                        act.activation(silu[:], conv[:, 0], ACT.Silu).then_inc(silu_ready, 1)
            wide_start("down2")
            act.dma_start(gamma[:], norm_f.partition_broadcast(P)).then_inc(ln_landed, 16)
            gate_rows(1)
            act.wait_ge(conv_done, FC + 1)
            g0 = AT["down2"]
            with act.Fori(0, FC - 1) as i:
                for s in range(4):
                    act.activation(shi[:, s], hid[:, at(s, i, 4)], ACT.Copy).then_inc(shi_ready, 1)
                    upper(g0 + s + 1, i, 4)
            for s in range(4):
                act.activation(shi[:, s], hid[:, FT - 4 + s], ACT.Copy).then_inc(shi_ready, 1)
                upper(g0 + FT - 4 + s + 1)
            squares(16, res, 8, False)

        @block.vector
        def _(dve):
            order = Order(dve, dve_order)

            def rest(g, i=None, per=0):
                if g >= G:
                    return
                for half in range(2):
                    h = 2 * g + half
                    dve.wait_ge(hi_ready, at(h + 1, i, 2 * per))
                    dve.tensor_tensor(wlo[:, h % 4], raw[g % 4][:, 1024 * half:1024 * half + 1024], whi[:, h % 4].bitcast(F32),
                                      ALU.subtract).then_inc(lo_ready, 1)

            def x_rest(n, src=None):
                for b in range(8):
                    dve.wait_ge(xhi_ready, 8 * n + b + 1)
                    hi = xhi[:, 2 * b:2 * b + 2].rearrange("p k t -> p (k t)")
                    lo = xlo[:, 2 * b:2 * b + 2].rearrange("p k t -> p (k t)")
                    dve.tensor_tensor(lo, ps[:, b] if src is None else src[:, b % 2], hi.bitcast(F32), ALU.subtract)\
                       .then_inc(xlo_ready, 1)

            def modulation(n, i=None, per=0):
                slot = n % 2
                dve.wait_ge(ada_landed[slot], at(16 * (n // 2 + 1), i, 8 * per))
                dve.scalar_tensor_tensor(out=ada[slot][:], in0=ada[slot][:], scalar=1.0, in1=cb[:], op0=ALU.mult, op1=ALU.mult,
                                         accum_out=mod[:, bass.ds(at(n, i, per), 1)]).then_inc(ada_used, 1)

            rest(0)
            x_rest(0)
            for g in range(0, 8):
                rest(g + 1)
            x_rest(1)
            g0 = AT["c_kv"]
            rest(g0 + 1)
            rest(g0 + 2)
            dve.wait_ge(weights_used, through(g0 + 1))
            dve.wait_ge(built, 11)
            dve.tensor_copy(ckv[:], ps[:, 0:2, 0:LATENT]).then_inc(pair_read[0], 1)
            rest(g0 + 3)
            dve.wait_ge(ck_squared, 2)
            dve.tensor_scalar(var(0, 0, 2), misc(0, 2), 1.0 / LATENT, LN_EPS, ALU.mult, ALU.add).then_inc(var_ready, 1)
            dve.wait_ge(weights_used, through(AT["k_idx"]))
            dve.tensor_copy(kw[:], ps[:, 2:4, 0:IDX_DIM + IDX_HEADS]).then_inc(pair_read[1], 1)
            dve.wait_ge(pair_read[1], reads(CH["k_idx"]))
            order.mark(dve.tensor_reduce(misc(2, 2), kw[:, :, 0:IDX_DIM], AX_X, ALU.add))
            order.wait()
            order.mark(dve.tensor_scalar(misc(4, 2), misc(2, 2), -1.0 / IDX_DIM, None, ALU.mult))
            order.wait()
            for t in range(T):
                order.mark(dve.tensor_scalar(kc[:, t], kw[:, t, 0:IDX_DIM], misc(4 + t), None, ALU.add))
            order.wait()
            order.mark(dve.tensor_tensor(ksq[:], kc[:], kc[:], ALU.mult))
            order.wait()
            order.mark(dve.tensor_reduce(misc(6, 2), ksq[:], AX_X, ALU.add))
            order.wait()
            dve.tensor_scalar(var(1, 0, 2), misc(6, 2), 1.0 / IDX_DIM, LN_EPS, ALU.mult, ALU.add).then_inc(var_ready, 1)
            order.mark(dve.tensor_scalar(wi[:], kw[:, :, IDX_DIM:IDX_DIM + IDX_HEADS], IDX_HEADS ** -0.5, None, ALU.mult))
            rest(g0 + 4)
            dve.wait_ge(consts_landed, 32)
            dve.wait_ge(rstd_ready, 1)
            for t in range(T):
                dve.scalar_tensor_tensor(out=ckv[:, t], in0=ckv[:, t], scalar=rstd(0, t), in1=row[:, 0:LATENT],
                                         op0=ALU.mult, op1=ALU.mult).then_inc(ck_ready, 1)
            dve.wait_ge(rstd_ready, 2)
            for t in range(T):
                order.mark(dve.scalar_tensor_tensor(out=kc[:, t], in0=kc[:, t], scalar=rstd(1, t),
                                                    in1=row[:, LATENT:LATENT + IDX_DIM], op0=ALU.mult, op1=ALU.mult))
            order.wait()
            for t in range(T):
                for n in range(2):
                    dve.tensor_tensor(kn[:, t, IDX_DIM * n:IDX_DIM * n + IDX_DIM], kc[:, t],
                                      row[:, LATENT + IDX_DIM:LATENT + 2 * IDX_DIM], ALU.add).then_inc(kn_ready, 1)
            rest(g0 + 5)
            dve.wait_ge(ckhi_ready, 1)
            dve.tensor_tensor(cklo[:].rearrange("p c t -> p (c t)"), ps[:, 4], ckhi[:].rearrange("p c t -> p (c t)").bitcast(F32),
                              ALU.subtract).then_inc(cklo_ready, 1)
            for g in range(AT["q_idx"] + 2, AT["q_idx"] + 8):
                rest(g + 1)
            for n in range(8):
                rest(AT["v_moba"] + n + 1)
                for h in (2 * n, 2 * n + 1):
                    dve.wait_ge(idx_relu, h + 1)
                    for t in range(T):
                        relu = idx_r[:, h % 2, S * t:S * t + S]
                        if h == 0:
                            ins = dve.tensor_scalar(score[:, t], relu, wi[:, t, h:h + 1], None, ALU.mult)
                        else:
                            if t == 0:
                                order.wait()
                            else:
                                dve.wait_ge(idx_added, h)
                            ins = dve.scalar_tensor_tensor(out=score[:, t], in0=relu, scalar=wi[:, t, h:h + 1], in1=score[:, t],
                                                           op0=ALU.mult, op1=ALU.add)
                        if t == 0:
                            order.mark(ins)
                        else:
                            ins.then_inc(idx_added, 1)
            rest(AT["w_uk"] + 1)
            dve.wait_ge(built, 11)
            dve.wait_ge(idx_added, IDX_HEADS)
            seen = [(score[:, 0, 0:128], 0, 128), (score[:, 1, :], 128, 384)]
            for work, c0, c1 in seen:
                order.mark(dve.tensor_tensor(work, work, causal[:, c0:c1], ALU.add))
            for n in range(TOPK // 8):
                order.wait()
                for t, (work, _, _) in enumerate(seen):
                    order.mark(dve.max(best8[:, t], work))
                order.wait()
                for t, (work, _, _) in enumerate(seen):
                    order.mark(dve.match_replace(work, best8[:, t], work, TAKEN))
                if n == 3:
                    rest(AT["w_uv"] + 1)
            order.wait()
            for work, c0, c1 in seen:
                order.mark(dve.tensor_scalar(work, work, TAKEN / 2, OUT_OF_SIGHT, ALU.is_gt, ALU.mult))
            order.wait()
            order.mark(dve.tensor_tensor(chosen[:, 0:128], seen[0][0], causal[:, 0:128], ALU.add))
            dve.tensor_tensor(chosen[:, 128:384], seen[1][0], causal[:, 128:384], ALU.add).then_inc(att_free, 1)
            dve.wait_ge(cb_ready, 1)
            g0 = AT["qk"]
            with dve.Fori(0, 3) as i:
                for s in range(8):
                    rest(g0 + s + 1, i, 8)
                    if s % 4 == 1:
                        modulation(s // 4, i, ADA_QK)

            dve.wait_ge(att_free, 1)
            order.wait()
            dve.wait_ge(pair_read[0], reads(CH["qk"] + 4))
            with dve.Fori(0, HEADS) as i:
                order.enter(i, 6)
                for j, mask in enumerate((chosen, causal)):
                    order.mark(dve.scalar_tensor_tensor(out=att_ab[:, j], in0=dist[:], scalar=col[:, bass.ds(at(COL["slope"], i, 1), 1)],
                                                        in1=mask[:], op0=ALU.mult, op1=ALU.add))
                for j in range(2):
                    dve.wait_ge(att_scores, at(j + 1, i, 2))
                    order.wait()
                    order.mark(dve.scalar_tensor_tensor(out=att_s[:, j], in0=ps[:, 4 + j, 0:384], scalar=HD ** -0.5,
                                                        in1=att_ab[:, j], op0=ALU.mult, op1=ALU.add))
                    order.wait()
                    for t, (c0, c1) in enumerate(((0, 128), (128, 384))):
                        dve.tensor_reduce(misc(8 + 2 * j + t), att_s[:, j, c0:c1], AX_X, ALU.max, negate=True)\
                           .then_inc(att_max, 1)
                for j in range(2):
                    dve.wait_ge(att_exp, at(2 * j + 2, i, 4))
                    order.mark(dve.reciprocal(misc(12 + 2 * j, 2), misc(12 + 2 * j, 2)))
                    order.wait()
                    for t, (c0, c1) in enumerate(((0, 128), (128, 384))):
                        dve.tensor_scalar(att_e[:, j, c0:c1], att_e[:, j, c0:c1], misc(12 + 2 * j + t), None, ALU.mult)\
                           .then_inc(att_p, 1)
                for j in range(2):
                    dve.wait_ge(att_o, at(j + 1, i, 2))
                    dve.tensor_scalar(ohi[:, at(8 * j, i, 1)], ps[:, 4 + j, 0:S], 1.0, None, ALU.mult).then_inc(att_ohi, 1)
                for j in range(2):
                    dve.wait_ge(att_ohi, at(j + 1, i, 2))
                    dve.tensor_tensor(olo[:, at(8 * j, i, 1)], ps[:, 4 + j, 0:S], ohi[:, at(8 * j, i, 1)].bitcast(F32),
                                      ALU.subtract).then_inc(att_free, 1)
                order.leave(HEADS)

            g0, c0, n0 = AT["gates"], CH["gates"], 3 * ADA_QK
            with dve.Fori(0, 4) as i:
                for s in range(12):
                    rest(g0 + s + 1, i, 12)
                    if s in (5, 11):
                        dst = gated_a if s == 5 else gated_b
                        n = s // 6
                        dve.wait_ge(weights_used, at(through(g0 + s), i, 24))
                        dve.wait_ge(pair_read[0], at(reads(c0 + 2 * n), i, 2))
                        dve.tensor_tensor(dst[:], pair(c0 + 1), sig[:], ALU.mult).then_inc(pair_read[1], 1)
                    if s == 11:
                        dve.wait_ge(pair_read[1], at(reads(c0 + 3), i, 2))
                        dve.tensor_tensor(merged[:, bass.ds(at(0, i, 4), 4)].rearrange("p k t -> p (k t)"), gated_a[:], gated_b[:],
                                          ALU.add).then_inc(merged_ready, 1)
                    if s % 2 == 0:
                        modulation(n0 + s // 2, i, ADA_GATES)

            def wide_turns(name, src, turns, ada0=None):
                g0, k0 = AT[name], SRC[name]

                def turn(i):
                    for s in range(4):
                        dve.wait_ge(shi_ready, at(k0 + s + 1, i, 4))
                        dve.tensor_tensor(slo[:, s], src[:, at(s, i, 4)], shi[:, s].bitcast(F32), ALU.subtract)\
                           .then_inc(slo_ready, 1)
                        rest(g0 + s + 1, i, 4)
                        if ada0 is not None and s % 2:
                            modulation(ada0 + s // 2, i, ADA_DOWN)

                if turns == 1:
                    turn(None)
                else:
                    with dve.Fori(0, turns) as i:
                        turn(i)

            def add_and_norm(n, g, job):
                dve.wait_ge(weights_used, through(g))
                for t in range(T):
                    order.mark(dve.scalar_tensor_tensor(out=res[:, t], in0=res[:, t], scalar=ALPHA,
                                                        in1=ps[:, 4 * t:4 * t + 4].rearrange("p b n -> p (b n)"),
                                                        op0=ALU.mult, op1=ALU.add, accum_out=misc(t)))
                    order.wait()
                    dve.tensor_scalar(misc(2 + t), misc(t), -1.0 / D, None, ALU.mult).then_inc(mean_ready, 1)
                dve.wait_ge(ln_landed, 32 * (n + 1))
                for t in range(T):
                    dve.wait_ge(sq_ready, 2 * n + t + 1)
                    dve.tensor_scalar(var(job + t), misc(4 + t), 1.0 / D, LN_EPS, ALU.mult, ALU.add).then_inc(var_ready, 1)
                    order.mark(dve.scalar_tensor_tensor(out=res[:, t], in0=res[:, t], scalar=misc(2 + t), in1=gamma[:],
                                                        op0=ALU.add, op1=ALU.mult))
                order.wait()
                for t in range(T):
                    dve.wait_ge(rstd_ready, job + t + 1)
                    dve.scalar_tensor_tensor(out=res[:, t], in0=res[:, t], scalar=rstd(job + t), in1=beta[:],
                                             op0=ALU.mult, op1=ALU.add).then_inc(res_ready, 1)

            def rms_rows(squared, job, last=False):
                for t in range(T):
                    dve.wait_ge(sq_ready, squared + t + 1)
                    dve.tensor_scalar(var(job + t), misc(4 + t), 1.0 / D, RMS_EPS, ALU.mult, ALU.add).then_inc(var_ready, 1)
                for t in range(T):
                    dve.wait_ge(rstd_ready, job + t + 1)
                    if last:
                        dve.scalar_tensor_tensor(out=xn[:, t], in0=res[:, t], scalar=rstd(job + t), in1=gamma[:],
                                                 op0=ALU.mult, op1=ALU.mult).then_inc(out_ready, 1)
                    else:
                        dve.tensor_scalar(xn[:, t], res[:, t], rstd(job + t), None, ALU.mult).then_inc(xn_ready, 1)

            def scales(first, norm):
                dve.scalar_tensor_tensor(out=scale_col[:], in0=mod[:, first:first + KT], scalar=1.0,
                                         in1=col[:, COL[norm]:COL[norm] + KT], op0=ALU.add, op1=ALU.mult).then_inc(mod_ready, 1)

            def gate_diagonals(first, n):
                for k in range(KT):
                    ins = dve.tensor_scalar(diag[:, k], ident[:], mod[:, first + k:first + k + 1], None, ALU.mult)
                ins.then_inc(diag_ready, 1)

            def add_gated(g):
                dve.wait_ge(weights_used, through(g))
                for t in range(T):
                    order.mark(dve.tensor_tensor(xn[:, t], ps[:, 4 * t:4 * t + 4].rearrange("p b n -> p (b n)"), gate_row[:],
                                                 ALU.mult))
                    order.wait()
                    dve.tensor_tensor(res[:, t], res[:, t], xn[:, t], ALU.add).then_inc(res_ready, 1)

            wide_turns("out1", merged, 4)
            dve.wait_ge(x_landed, 32)
            add_and_norm(0, AT["q_mem"] - 1, 2)
            x_rest(2)
            for g in range(AT["q_mem"], AT["q_mem"] + 4):
                rest(g + 1)

            def m_maxima(h):
                dve.wait_ge(m_scores, h + 1)
                order.mark(dve.tensor_reduce(misc(20 + 2 * (h % 2), 2), ps[:, 4 + h % 2].rearrange("p (t k) -> p t k", t=T), AX_X, ALU.max))
                order.wait()
                dve.tensor_scalar(misc(8 + 2 * (h % 2), 2), misc(20 + 2 * (h % 2), 2), -HD ** -0.5, None, ALU.mult).then_inc(m_max, 1)

            m_maxima(0)
            m_maxima(1)
            for h in range(HEADS_MEM):
                dve.wait_ge(m_exp, 2 * h + 2)
                order.mark(dve.reciprocal(misc(12 + 2 * (h % 2), 2), misc(12 + 2 * (h % 2), 2)))
                order.wait()
                for t in range(T):
                    dve.tensor_scalar(mem_p[:, h % 2, S * t:S * t + S], mem_p[:, h % 2, S * t:S * t + S],
                                      misc(12 + 2 * (h % 2) + t), None, ALU.mult).then_inc(m_p, 1)
                if h + 2 < HEADS_MEM:
                    m_maxima(h + 2)
            dve.wait_ge(m_out, HEADS_MEM)
            wide_turns("o_mem", omT, 1)
            add_and_norm(1, AT["up1"] - 1, 4)
            x_rest(3)
            g0, c0, n0 = AT["up1"], CH["up1"], 3 * ADA_QK + 4 * ADA_GATES
            with dve.Fori(0, FC) as i:
                for s in range(8):
                    rest(g0 + s + 1, i, 8)
                    if s == 7:
                        dve.wait_ge(weights_used, at(through(g0 + s), i, 16))
                        dve.wait_ge(pair_read[c0 % 2], at(reads(c0), i, 1))
                        dve.tensor_tensor(hid[:, bass.ds(at(0, i, 4), 4)].rearrange("p k t -> p (k t)"), pair(c0 + 1), silu[:],
                                          ALU.mult).then_inc(pair_read[(c0 + 1) % 2], 1)
                    if s % 2 == 0:
                        modulation(n0 + s // 2, i, ADA_UP)
            wide_turns("down1", hid, FC, n0 + FC * ADA_UP)
            add_and_norm(2, AT["lstm_gates"] - 1, 6)
            dve.wait_ge(ada_used, ADA)
            order.mark(dve.tensor_tensor(mod[:], mod[:], col[:, COL["b_ada"]:COL["b_ada"] + ADA], ALU.add))
            order.wait()
            scales(KT, "norm1")
            rms_rows(6, 8)
            x_rest(4, modulated)
            rest(AT["lstm_gates"] + 1)
            dve.wait_ge(weights_used, through(AT["lstm_gates"]))
            c = CH["lstm_gates"]
            dve.tensor_copy(gn[:], ps[:, 2 * (c % 2):2 * (c % 2) + 2, 0:16]).then_inc(pair_read[c % 2], 1)
            rest(AT["lstm_gates"] + 2)
            rest(AT["lstm_gates"] + 3)
            dve.wait_ge(late_landed, 32)
            dve.wait_ge(g_rows_T, 1)
            for d in range(2):
                for n, dst in enumerate((g_in, g_fo)):
                    order.mark(dve.tensor_scalar(dst[:, d], ps[0:LH, 4 + d, S * n:S * n + S], gbias[:, 2 * d + n:2 * d + n + 1], None,
                                                 ALU.add))
            order.wait()
            dve.scalar_tensor_tensor(out=g_e[:], in0=g_fo[:], scalar=-1.0, in1=g_fo[:], op0=ALU.mult, op1=ALU.max).then_inc(g_abs, 1)
            rest(AT["lstm_gates"] + 4)
            rest(AT["lstm_gates"] + 5)
            rest(AT["lstm_gates"] + 6)
            dve.wait_ge(g_exp, 1)
            dve.tensor_scalar(g_e[:], g_e[:], 1.0, None, ALU.add).then_inc(g_one, 1)
            for g in range(AT["lstm_k"] + 2, AT["lstm_k"] + 5):
                rest(g)
            rest(AT["lstm_v"] + 1)
            dve.wait_ge(g_ln, 1)
            order.mark(dve.scalar_tensor_tensor(out=g_fo[:], in0=g_fo[:], scalar=0.0, in1=g_e[:], op0=ALU.min, op1=ALU.subtract))
            order.wait()
            ones_row = ones[0:LH, 0:1].to_broadcast([LH, S])
            order.mark(dve.tensor_tensor_scan(g_sum[:, 0], ones_row, g_fo[:, 0], 0.0, ALU.mult, ALU.add))
            order.mark(dve.tensor_tensor_scan(g_sum[:, 1, ::-1], ones_row, g_fo[:, 1, ::-1], 0.0, ALU.mult, ALU.add))
            order.wait()
            order.mark(dve.tensor_tensor(g_a[:], g_in[:], g_sum[:], ALU.subtract))
            order.wait()
            rest(AT["lstm_v"] + 2)
            order.mark(dve.tensor_tensor_scan(g_max[:, 0], g_a[:, 0], g_a[:, 0], -3e38, ALU.max, ALU.max))
            order.mark(dve.tensor_tensor_scan(g_max[:, 1, ::-1], g_a[:, 1, ::-1], g_a[:, 1, ::-1], -3e38, ALU.max, ALU.max))
            order.wait()
            dve.tensor_tensor(g_m[:], g_sum[:], g_max[:], ALU.add).then_inc(g_stab, 1)
            for g in range(AT["lstm_v"] + 3, AT["lstm_o"] + 5):
                rest(g)
            dve.wait_ge(g_cols_T, 1)
            dve.tensor_copy(lcols[:].rearrange("p a n -> p (a n)"), ps[:, 6, 0:32]).then_inc(g_cols, 1)
            for g in range(AT["lstm_o"] + 5, AT["out2"] + 1):
                rest(g)
            dve.wait_ge(g_cols, 1)
            dve.wait_ge(built, 19)
            floors = lcols[:, 1].rearrange("p (n h) -> p n h", h=LH)
            for h in range(LH):
                dve.wait_ge(l_bc, h + 1)
                for d, st, t0, t1, c0 in BLOCKS:
                    n = 8 * d + 4 * st + h
                    ins = dve.tensor_scalar(lx[:, c0:c0 + t1 - t0], ps[:, 0, S * d + t0:S * d + t1], lcols[:, 0, n:n + 1], 0.0,
                                            ALU.subtract, ALU.max)
                ins.then_inc(l_x, 1)
                dve.wait_ge(l_e, h + 1)
                order.mark(dve.tensor_tensor(le[:], le[:], tri[:], ALU.mult))
                order.wait()
                dve.wait_ge(l_st, h + 1)
                for d, st, t0, t1, c0 in BLOCKS:
                    ins = dve.scalar_tensor_tensor(out=lp[:, c0:c0 + t1 - t0], in0=ps[:, 1, S * st + t0:S * st + t1],
                                                   scalar=HD ** -0.5, in1=le[:, c0:c0 + t1 - t0], op0=ALU.mult, op1=ALU.mult)
                ins.then_inc(l_p, 1)
                dve.wait_ge(l_num, h + 1)
                order.mark(dve.tensor_copy(misc(24, 4), ps[:, 4:8, DV]))
                order.wait()
                order.mark(dve.scalar_tensor_tensor(out=misc(28, 4), in0=misc(24, 4), scalar=-1.0, in1=misc(24, 4), op0=ALU.mult,
                                                    op1=ALU.max))
                order.wait()
                order.mark(dve.tensor_tensor(misc(32, 4), misc(28, 4), floors[:, :, h], ALU.max))
                order.wait()
                order.mark(dve.reciprocal(misc(36, 4), misc(32, 4)))
                order.wait()
                for t in range(T):
                    order.mark(dve.tensor_scalar(lh[:, t], ps[:, 4 + t, 0:DV], misc(36 + t), None, ALU.mult))
                order.wait()
                for t in range(T):
                    dve.scalar_tensor_tensor(out=lh[:, t], in0=ps[:, 6 + t, 0:DV], scalar=misc(38 + t), in1=lh[:, t], op0=ALU.mult,
                                             op1=ALU.add).then_inc(l_h, 1)
                dve.wait_ge(l_sq, 2 * h + 2)
                dve.tensor_scalar(var(10 + h, 0, 2), misc(16, 2), 1.0 / DV, RMS_EPS, ALU.mult, ALU.add).then_inc(var_ready, 1)
                dve.wait_ge(rstd_ready, 11 + h)
                for t in range(T):
                    dve.tensor_scalar(lh[:, t], lh[:, t], rstd(10 + h, t), None, ALU.mult).then_inc(l_hn, 1)
                dve.wait_ge(l_hT, h + 1)
                for v in range(2):
                    k = 2 * h + v
                    dve.scalar_tensor_tensor(out=mixT[:, 8 + k], in0=ps[:, 0, S * v:S * v + S],
                                             scalar=col[:, COL["norm_m"] + k:COL["norm_m"] + k + 1], in1=so[:, k], op0=ALU.mult,
                                             op1=ALU.mult).then_inc(mix_m, 1)
            gate_diagonals(2 * KT, 0)
            dve.wait_ge(mix_f, LH)
            wide_turns("out2", mixT, 4)
            dve.wait_ge(gate_ready, 1)
            add_gated(AT["up2"] - 1)
            scales(4 * KT, "norm2")
            rms_rows(8, 14)
            dve.wait_ge(xn_ready, 4)
            x_rest(5, modulated)
            dve.memset(misc(40), 0.0).then_inc(conv_done, 1)
            g0, c0 = AT["up2"], CH["up2"]
            with dve.Fori(0, FC) as i:
                order.enter(i, 8)
                for s in range(8):
                    rest(g0 + s + 1, i, 8)
                    if s % 4 == 3:
                        q = s // 4
                        dve.wait_ge(conv_mid, at(q + 1, i, 2))
                        bank = pair(c0 + q)
                        for m in range(4):
                            tap = at(COL["w_conv"] + FT * q + m, i, 4)
                            order.mark(dve.scalar_tensor_tensor(
                                out=conv[:, q, S * m + 1:S * m + S], in0=bank[:, S * m:S * m + S - 1], scalar=col[:, bass.ds(tap, 1)],
                                in1=conv[:, q, S * m + 1:S * m + S], op0=ALU.mult, op1=ALU.add))
                        order.wait()
                        for m in range(4):
                            tap = at(COL["w_conv"] + 4 * FT + FT * q + m, i, 4)
                            ins = dve.scalar_tensor_tensor(
                                out=conv[:, q, S * m:S * m + S - 1], in0=bank[:, S * m + 1:S * m + S], scalar=col[:, bass.ds(tap, 1)],
                                in1=conv[:, q, S * m:S * m + S - 1], op0=ALU.mult, op1=ALU.add)
                        ins.then_inc(pair_read[(c0 + q) % 2], 1)
                    if s == 7:
                        dve.wait_ge(silu_ready, at(1, i, 1))
                        dve.wait_ge(pair_read[(c0 + 1) % 2], at(reads(c0 + 1), i, 1))
                        dve.tensor_tensor(hid[:, bass.ds(at(0, i, 4), 4)].rearrange("p k t -> p (k t)"), conv[:, 1], silu[:],
                                          ALU.mult).then_inc(conv_done, 1)
                order.leave(FC)
            gate_diagonals(5 * KT, 1)
            g0, k0 = AT["down2"], SRC["down2"]
            with dve.Fori(0, FC - 1) as i:
                for s in range(4):
                    dve.wait_ge(shi_ready, at(k0 + s + 1, i, 4))
                    dve.tensor_tensor(slo[:, s], hid[:, at(s, i, 4)], shi[:, s].bitcast(F32), ALU.subtract).then_inc(slo_ready, 1)
                    rest(g0 + s + 1, i, 4)
            for s in range(FT - 4, FT):
                dve.wait_ge(shi_ready, k0 + s + 1)
                dve.tensor_tensor(slo[:, s % 4], hid[:, s], shi[:, s % 4].bitcast(F32), ALU.subtract).then_inc(slo_ready, 1)
                rest(g0 + s + 1)
            dve.wait_ge(gate_ready, 2)
            add_gated(G - 1)
            dve.wait_ge(ln_landed, 32 * 3 + 16)
            rms_rows(10, 16, last=True)

        @block.tensor
        def _(pe):
            def transpose_rows(n, src):
                for b in range(8):
                    for f in range(2):
                        for t in range(T):
                            k = 2 * b + f
                            ins = pe.transpose(ps[:, b, S * f + P * t:S * f + P * t + P], src[:, t, P * k:P * k + P], ident[:])
                    ins.then_inc(xT_done, 1)

            def bank_pair(c, i=None, per=0):
                if c >= 2:
                    pe.wait_ge(pair_read[c % 2], at(c // 2, i, per))

            def product(g, half, c, form, left, k0, ks, width, first, last, i=None, per=0):
                h = 2 * g + half
                pe.wait_ge(lo_ready, at(h + 1, i, 2 * per))
                hi, lo = (w[:, h % 4, 0:ks * width].rearrange("p (k n) -> p k n", k=ks) for w in (whi, wlo))
                lhi, llo = left
                for k in range(ks):
                    kt = k0 + k
                    begins, ends = first and k == 0, last and k == ks - 1
                    for m in range(width // P if form == "T" else T):
                        for n, (w, a) in enumerate(((hi, lhi), (hi, llo), (lo, lhi))):
                            if form == "T":
                                o = ps[:, 2 * (c % 2) + m // 2, S * (m % 2):S * (m % 2) + S]
                                ins = pe.matmul(o, w[:, k, P * m:P * m + P], a[:, kt], start=begins and n == 0 and m % 2 == 0,
                                                stop=ends and n == 2, skip_group_check=True)
                            else:
                                o = ps[:, 2 * (c % 2) + m, 0:width]
                                ins = pe.matmul(o, a[:, kt, P * m:P * m + P], w[:, k, :], start=begins and n == 0,
                                                stop=ends and n == 2, skip_group_check=True)
                ins.then_inc(weights_used, 1)

            def chunk(g0, c, form, left=(xhi, xlo), tiles=4, k0=0, i=None, per=0, chunks=0):
                bank_pair(c, i, chunks)
                for s in range(tiles):
                    for half in range(2):
                        product(g0 + s, half, c, form, left, k0 + 4 * s + 2 * half, 2, 512, s == 0 and half == 0,
                                s == tiles - 1 and half == 1, i, per)

            def wide_open():
                for b in range(8):
                    pe.matmul(ps[:, b], zeros[:, 0:P], zeros[:], start=True, stop=False, skip_group_check=True)

            def wide_tile(g, k, s, i=None):
                for half in range(2):
                    h = 2 * g + half
                    pe.wait_ge(lo_ready, at(h + 1, i, 8))
                    if half == 0:
                        pe.wait_ge(slo_ready, at(k + 1, i, 4))
                    for t in range(T):
                        for a, w in ((shi, whi), (shi, wlo), (slo, whi)):
                            for n in range(2):
                                ins = pe.matmul(ps[:, 4 * t + 2 * half + n], a[:, s, P * t:P * t + P],
                                                w[:, h % 4, 512 * n:512 * n + 512], start=False, stop=False, skip_group_check=True)
                    ins.then_inc(weights_used, 1)

            def wide(name, turns):
                wide_open()
                g0, k0 = AT[name], SRC[name]
                if turns == 1:
                    for s in range(4):
                        wide_tile(g0 + s, k0 + s, s)
                else:
                    with pe.Fori(0, turns) as i:
                        for s in range(4):
                            wide_tile(g0 + s, k0 + s, s, i)

            pe.wait_ge(built, 6)
            pe.wait_ge(mem_landed, 16)
            transpose_rows(0, mem_nat)
            pe.wait_ge(xlo_ready, 8)
            chunk(AT["k_mem"], CH["k_mem"], "T")
            chunk(AT["v_mem"], CH["v_mem"], "N")
            pe.wait_ge(x_landed, 16)
            pe.wait_ge(pair_read[0], 1)
            pe.wait_ge(pair_read[1], 1)
            transpose_rows(1, res)
            pe.wait_ge(xlo_ready, 16)
            g, c = AT["c_kv"], CH["c_kv"]
            for n in range(4):
                product(g + n // 2, n % 2, c, "N", (xhi, xlo), 4 * n, 4, LATENT, n == 0, n == 3)
            g, c = AT["k_idx"], CH["k_idx"]
            for half in range(2):
                product(g, half, c, "N", (xhi, xlo), 8 * half, 8, IDX_DIM + IDX_HEADS, half == 0, half == 1)
            g, c = AT["q_idx"], CH["q_idx"]
            bank_pair(c)
            for s in range(4):
                for half in range(2):
                    product(g + s, half, c, "T", (xhi, xlo), 4 * s + 2 * half, 2, 512, s == 0 and half == 0, s == 3 and half == 1)
                if s == 1:
                    pe.wait_ge(ck_ready, 2)
                    for k in range(2):
                        for t in range(T):
                            ins = pe.transpose(ps[:, 4, S * k + P * t:S * k + P * t + P], ckv[:, t, P * k:P * k + P], ident[:])
                    ins.then_inc(small_T, 1)
                    pe.wait_ge(kn_ready, 4)
                    for t in range(T):
                        ins = pe.transpose(ps[:, 5, P * t:P * t + P], kn[:, t], ident[:])
                    ins.then_inc(small_T, 1)
            chunk(g + 4, c + 1, "T")
            g, c = AT["v_moba"], CH["v_moba"]
            pe.wait_ge(cklo_ready, 1)
            pe.wait_ge(ki_ready, 1)
            for s in range(8):
                if s % 4 == 0:
                    bank_pair(c + s // 4)
                for half in range(2):
                    h = 2 * s + half
                    pe.wait_ge(pair_read[(CH["q_idx"] + h // 8) % 2], reads(CH["q_idx"] + h // 8))
                    if h >= 4:
                        pe.wait_ge(idx_relu, h - 3)
                    r0 = IDX_DIM * (h % 2)
                    for t in range(T):
                        ins = pe.matmul(ps[:, 4 + h % 4, S * t:S * t + S], qi[r0:r0 + IDX_DIM, h // 2, P * t:P * t + P],
                                        kiT[r0:r0 + IDX_DIM, :], start=True, stop=True, skip_group_check=True)
                    ins.then_inc(idx_done, 1)
                    product(g + s, half, c + s // 4, "N", (xhi, xlo), 4 * (s % 4) + 2 * half, 2, 512, s % 4 == 0 and half == 0,
                            s % 4 == 3 and half == 1)
            for name, form in (("w_uk", "T"), ("w_uv", "N")):
                for half in range(2):
                    bank_pair(CH[name] + half)
                    product(AT[name], half, CH[name] + half, form, (ckhi, cklo), 0, 2, 512, True, True)
            with pe.Fori(0, 3) as i:
                for q in range(2):
                    chunk(AT["qk"] + 4 * q, CH["qk"] + q, "T", i=i, per=8, chunks=1)

            pe.wait_ge(idx_relu, IDX_HEADS)
            with pe.Fori(0, HEADS) as i:
                pe.wait_ge(qv_ready, at(4, i, 4))
                pe.wait_ge(att_free, at(1, i, 2))
                for j, k0 in enumerate((24, 16)):
                    key = qk[:, at(k0, i, 1)]
                    pe.matmul(ps[:, 4 + j, 0:128], qs[:, j, 0:128], key[:, 0:128], start=True, stop=True, skip_group_check=True)
                    pe.matmul(ps[:, 4 + j, 128:384], qs[:, j, 128:256], key, start=True, stop=True, skip_group_check=True)\
                      .then_inc(att_scores, 1)
                for j in range(2):
                    pe.wait_ge(att_p, at(2 * j + 2, i, 4))
                    for n in range(3):
                        ins = pe.transpose(ps[:, 6 + j, 128 * n:128 * n + 128], att_e[:, j, 128 * n:128 * n + 128], ident[:])
                    ins.then_inc(att_T, 1)
                for j in range(2):
                    pe.wait_ge(att_pT_ready, at(j + 1, i, 2))
                    pe.matmul(ps[:, 4 + j, 0:S], vs[:, j, 0], att_pT[:, j, 0:256], start=True, stop=False, skip_group_check=True)
                    pe.matmul(ps[:, 4 + j, P:S], vs[:, j, 1], att_pT[:, j, 256:384], start=False, stop=True,
                              skip_group_check=True).then_inc(att_o, 1)

            pe.wait_ge(att_free, 1 + 2 * HEADS)
            g0, c0 = AT["gates"], CH["gates"]
            with pe.Fori(0, 4) as i:
                chunk(g0, c0, "T", i=i, per=12, chunks=2)
                chunk(g0 + 4, c0 + 1, "T", (ohi, olo), 2, 0, i, 12, 2)
                chunk(g0 + 6, c0 + 2, "T", i=i, per=12, chunks=2)
                chunk(g0 + 10, c0 + 3, "T", (ohi, olo), 2, 8, i, 12, 2)
            for c in (c0 + 14, c0 + 15):
                pe.wait_ge(pair_read[c % 2], reads(c))
            wide("out1", 4)
            pe.wait_ge(res_ready, 2)
            transpose_rows(2, res)
            pe.wait_ge(xlo_ready, 24)
            chunk(AT["q_mem"], CH["q_mem"], "T")

            def m_score(h):
                for t in range(T):
                    ins = pe.matmul(ps[:, 4 + h % 2, S * t:S * t + S], qmT[:, h, P * t:P * t + P], kmT[:, h], start=True, stop=True,
                                    skip_group_check=True)
                ins.then_inc(m_scores, 1)

            c = CH["q_mem"]
            pe.wait_ge(pair_read[c % 2], reads(c))
            m_score(0)
            m_score(1)
            for h in range(HEADS_MEM):
                pe.wait_ge(m_p, 2 * h + 2)
                for k in range(2):
                    for t in range(T):
                        ins = pe.transpose(ps[:, 6 + h % 2, S * k + P * t:S * k + P * t + P],
                                           mem_p[:, h % 2, S * t + P * k:S * t + P * k + P], ident[:])
                ins.then_inc(m_T, 1)
                pe.wait_ge(m_pT, h + 1)
                for k in range(2):
                    ins = pe.matmul(ps[:, 4 + h % 2, 0:S], vm[:, k, HD * h:HD * h + HD], mem_pT[:, h % 2, S * k:S * k + S],
                                    start=k == 0, stop=k == 1, skip_group_check=True)
                ins.then_inc(m_o, 1)
                if h + 2 < HEADS_MEM:
                    pe.wait_ge(m_out, h + 1)
                    m_score(h + 2)
            pe.wait_ge(m_out, HEADS_MEM)
            wide("o_mem", 1)
            pe.wait_ge(res_ready, 4)
            transpose_rows(3, res)
            pe.wait_ge(xlo_ready, 32)
            with pe.Fori(0, FC) as i:
                for q in range(2):
                    chunk(AT["up1"] + 4 * q, CH["up1"] + q, "T", i=i, per=8, chunks=1)
            for c in (CH["up1"] + 2 * FC - 2, CH["up1"] + 2 * FC - 1):
                pe.wait_ge(pair_read[c % 2], reads(c))
            wide("down1", FC)
            pe.wait_ge(xn_ready, 2)
            transpose_rows(4, xn)
            pe.wait_ge(xlo_ready, 40)
            g, c = AT["lstm_gates"], CH["lstm_gates"]
            for half in range(2):
                product(g, half, c, "N", (xhi, xlo), 8 * half, 8, 16, half == 0, half == 1)
            g, c = AT["lstm_q"], CH["lstm_q"]
            bank_pair(c)
            for s in range(4):
                for half in range(2):
                    product(g + s, half, c, "T", (xhi, xlo), 4 * s + 2 * half, 2, 512, s == 0 and half == 0, s == 3 and half == 1)
                if s == 0:
                    pe.wait_ge(pair_read[CH["lstm_gates"] % 2], reads(CH["lstm_gates"]))
                    for d in range(2):
                        for n in range(2):
                            for t in range(T):
                                q = 8 * d + 4 * n
                                ins = pe.transpose(ps[0:LH, 4 + d, S * n + P * t:S * n + P * t + P], gn[:, t, q:q + LH], ident[:])
                    ins.then_inc(g_rows_T, 1)
            chunk(AT["lstm_k"], CH["lstm_k"], "T")
            chunk(AT["lstm_v"], CH["lstm_v"], "N")
            chunk(AT["lstm_v"] + 4, CH["lstm_v"] + 1, "N")
            pe.wait_ge(g_floor, 1)
            for n, src in enumerate((g_a, g_m)):
                for d in range(2):
                    for t in range(T):
                        q = 16 * n + 8 * d + 4 * t
                        ins = pe.transpose(ps[:, 6, q:q + LH], src[:, d, P * t:P * t + P], ident[0:LH, 0:LH])
            ins.then_inc(g_cols_T, 1)
            for q in range(2):
                chunk(AT["lstm_o"] + 4 * q, CH["lstm_o"] + q, "T")
            for q in range(2):
                chunk(AT["fourier"] + 4 * q, CH["fourier"] + q, "N")
            for c in (CH["fourier"], CH["fourier"] + 1):
                pe.wait_ge(pair_read[c % 2], reads(c))
            pe.wait_ge(g_cols, 1)
            pe.wait_ge(built, 19)
            pe.wait_ge(late_landed, 32)
            for h in range(LH):
                if h >= 1:
                    pe.wait_ge(mix_m, 2 * h)
                pe.matmul(ps[:, 0], sel[:, h], g_max[:].rearrange("h d t -> h (d t)"), start=True, stop=True,
                          skip_group_check=True).then_inc(l_bc, 1)
                for st in range(T):
                    ins = pe.matmul(ps[:, 1, S * st:S * st + S], lk[:, h, P * st:P * st + P], lq[:, h], start=True, stop=True,
                                    skip_group_check=True)
                ins.then_inc(l_st, 1)
                if h >= 1:
                    pe.wait_ge(mix_f, h)
                for f in range(2):
                    for st in range(T):
                        ins = pe.matmul(ps[:, 2 + f], uf[:, st, S * h + P * f:S * h + P * f + P], dftc[:, st, 0:512], start=st == 0,
                                        stop=st == 1, skip_group_check=True)
                    ins.then_inc(f_first, 1)
                pe.wait_ge(l_p, h + 1)
                for d in range(2):
                    for t in range(T):
                        mine = [b for b in BLOCKS if b[0] == d and b[2] <= P * t < b[3]]
                        for n, (_, st, t0, _, c0) in enumerate(mine):
                            q = c0 + P * t - t0
                            ins = pe.matmul(ps[:, 4 + 2 * d + t, 0:DV + 1], lp[:, q:q + P], lv[:, st, h, 0:DV + 1], start=n == 0,
                                            stop=n == len(mine) - 1, skip_group_check=True)
                ins.then_inc(l_num, 1)
                pe.wait_ge(f_copied, 2 * h + 2)
                for fo in range(2):
                    for n in range(4):
                        fi, part = n // 2, n % 2
                        ins = pe.matmul(ps[:, 2, S * fo:S * fo + S], dftc[:, fi, 512 * part + P * fo:512 * part + P * fo + P],
                                        fa[:, fi, S * part:S * part + S], start=n == 0 and fo == 0, stop=n == 3,
                                        skip_group_check=True)
                ins.then_inc(f_second, 1)
                pe.wait_ge(l_hn, 2 * h + 2)
                for v in range(2):
                    for t in range(T):
                        ins = pe.transpose(ps[:, 0, S * v + P * t:S * v + P * t + P], lh[:, t, P * v:P * v + P], ident[:])
                ins.then_inc(l_hT, 1)

            def gate_rows(n):
                pe.wait_ge(diag_ready, n + 1)
                for k in range(KT):
                    ins = pe.matmul(ps[:, 4 + k // 4, P * (k % 4):P * (k % 4) + P], ones[:], diag[:, k], start=True, stop=True,
                                    skip_group_check=True)
                ins.then_inc(gate_T, 1)
                pe.wait_ge(gate_ready, n + 1)

            gate_rows(0)
            pe.wait_ge(mix_f, LH)
            wide("out2", 4)
            pe.wait_ge(xn_ready, 4)
            transpose_rows(5, xn)
            pe.wait_ge(xlo_ready, 48)
            with pe.Fori(0, FC) as i:
                for q in range(2):
                    chunk(AT["up2"] + 4 * q, CH["up2"] + q, "T", i=i, per=8, chunks=1)
            for c in (CH["up2"] + 2 * FC - 2, CH["up2"] + 2 * FC - 1):
                pe.wait_ge(pair_read[c % 2], reads(c))
            gate_rows(1)
            wide("down2", FC)


def tiles_by_chunk(w):
    k, n = w.shape
    return w.reshape(k // 512, 4, P, n // 512, 512).transpose(3, 0, 2, 1, 4).reshape(n // 512, k // 512, P, D)


def tiles_of_latent(w):
    return w.reshape(2, P, 2, 512).transpose(1, 2, 0, 3).reshape(1, P, D)


def tile_of_few(w):
    n = w.shape[1]
    out = np.zeros((P, 2, 1024), w.dtype)
    out[:, :, :8 * n] = w.reshape(2, 8, P, n).transpose(2, 0, 1, 3).reshape(P, 2, 8 * n)
    return out.reshape(1, P, D)


def weight_stream(a):
    flat = lambda w: w.reshape(-1, P, D)
    w_in, w_in2 = a["w_in"][0], a["w_in_2"]
    kv = tiles_by_chunk(a["w_kv_mem"][0])
    o = {}
    n = 0
    for name, width in (("q_dsa", 1024), ("c_kv", 256), ("q_idx", 1024), ("k_idx", 80), ("q_m", 1024), ("k_m", 1024),
                        ("v_m", 1024), ("ga", D), ("gb", D)):
        o[name] = w_in[:, n:n + width]
        n += width
    side = [tiles_by_chunk(w) for w in (o["ga"], a["w_o_dsa"][0], o["gb"], a["w_o_moba"][0])]
    gates = np.concatenate(side, axis=1)
    up1 = tiles_by_chunk(a["w_ffn_in"][0])
    up1 = np.concatenate([up1[:FC], up1[FC:]], axis=1)
    up2 = tiles_by_chunk(a["w_up_2"])
    up2 = np.concatenate([up2[:FC], up2[FC:]], axis=1)
    ckv = o["c_kv"].reshape(2, 8, P, LATENT).transpose(0, 2, 1, 3)
    parts = [
        flat(kv), flat(ckv), tile_of_few(o["k_idx"]), flat(tiles_by_chunk(o["q_idx"])), flat(tiles_by_chunk(o["v_m"])),
        tiles_of_latent(a["w_uk"][0].transpose(2, 0, 1).reshape(LATENT, 1024)),
        tiles_of_latent(a["w_uv"][0].transpose(1, 0, 2).reshape(LATENT, 1024)),
        flat(tiles_by_chunk(o["q_dsa"])), flat(tiles_by_chunk(o["q_m"])), flat(tiles_by_chunk(o["k_m"])),
        flat(gates), flat(a["w_out"][0]), flat(tiles_by_chunk(a["w_q_mem"][0])), flat(a["w_o_mem"][0]), flat(up1),
        flat(a["w_ffn_out"][0]), tile_of_few(w_in2[:, 4096:4112]), flat(tiles_by_chunk(w_in2[:, 1024:4096])),
        flat(tiles_by_chunk(w_in2[:, 0:1024])), flat(a["w_out_2"]), flat(up2), flat(a["w_down_2"]),
    ]
    return np.concatenate(parts, axis=0)


def kernel(**inputs):
    import concourse.bacc as bacc
    from concourse.bass_utils import run_bass_kernel_spmd

    a = {k: np.asarray(v) for k, v in inputs.items()}

    def columns(v):
        return v.reshape(-1, P).T

    slopes = np.array([2.0 ** (-8.0 * (n + 1) / HEADS) for n in range(HEADS)], np.float32)
    turn = np.arange(S)
    angle = 2 * np.pi * (np.outer(turn, turn) % S) / S
    root = S ** 0.5
    wave = np.concatenate([np.cos(angle), np.sin(angle), -np.sin(angle)], axis=1) / root
    arrays = {
        "x": a["x"][0],
        "mem": a["mem"][0],
        "stream": weight_stream(a),
        "w_ada": np.ascontiguousarray(a["w_ada_2"].T).reshape(ADA, P, D),
        "cols": np.concatenate(
            [columns(a["b_gate"][0]), columns(a["b_ada_2"]), columns(a["norm1_w_2"]), columns(a["norm2_w_2"]),
             columns(a["mlstm_norm_w_2"]), columns(a["w_conv_2"]), columns(a["b_conv_2"]),
             np.broadcast_to(slopes, (P, HEADS))], axis=1),
        "rows": np.concatenate([a["kv_norm_g"], a["idx_k_norm_g"], a["idx_k_norm_b"]], axis=1),
        "ln_g": a["ln_g"][0],
        "ln_b": a["ln_b"][0],
        "norm_f": a["norm_f_w_2"].reshape(1, D),
        "c_row": a["c_2"],
        "gate_bias": a["b_gates_2"].reshape(4, LH).T,
        "dft": wave.astype(np.float32),
    }
    arrays = {k: np.ascontiguousarray(v) for k, v in arrays.items()}
    assert arrays["stream"].shape[0] == G, (arrays["stream"].shape, G)
    nc = bacc.Bacc("TRN2", target_bir_lowering=False, num_devices=1)
    args = [nc.dram_tensor(f"in_{k}", v.shape, F32, kind="ExternalInput").ap() for k, v in arrays.items()]
    out = nc.dram_tensor("out_0", (S, D), F32, kind="ExternalOutput").ap()
    two_blocks(nc, *args, out)
    r = run_bass_kernel_spmd(nc, [{f"in_{k}": v for k, v in arrays.items()}], core_ids=[0])
    return r.results[0]["out_0"].reshape(1, S, D)
```

```python
from contextlib import ExitStack

import numpy as np
import concourse.bass as bass
from concourse import mybir

F32 = mybir.dt.float32
F32R = mybir.dt.float32r
BF16 = mybir.dt.bfloat16
I32 = mybir.dt.int32
ALU = mybir.AluOpType
ACT = mybir.ActivationFunctionType
AX_X = mybir.AxisListType.X

P = 128
S = 256
T = S // P
D = 2048
KT = D // P
HD = 128
HEADS = 8
HEADS_MEM = 4
LATENT = 256
IDX_HEADS = 16
IDX_DIM = 64
TOPK = min(256, S // 4)
FF = 5632
FT = FF // P
FC = FF // 512
LH = 4
DV = 256
ADA = 6 * D // P
ALPHA = 2.0 ** 0.25
LN_EPS = 1e-5
RMS_EPS = 1e-6
OUT_OF_SIGHT = -1e30
TAKEN = -3e38

TILES = [("k_mem", 4), ("v_mem", 4), ("latent", 3), ("q_idx", 8), ("v_moba", 8), ("w_uk", 1), ("w_uv", 1),
         ("qk", 24), ("gate_a", 16), ("gates", 32), ("out1", 16), ("q_mem", 4), ("o_mem", 4), ("up1", 8 * FC), ("down1", FT),
         ("lstm_gates", 1), ("lstm_q", 4), ("lstm_k", 4), ("lstm_v", 8), ("lstm_o", 8), ("fourier", 8), ("out2", 16),
         ("up2", 8 * FC), ("down2", FT)]
CHUNKS = [("k_mem", 1), ("v_mem", 1), ("latent", 1), ("q_idx", 2), ("v_moba", 2), ("w_uk", 2), ("w_uv", 2),
          ("qk", 6), ("gate_a", 4), ("gates", 12), ("q_mem", 1), ("up1", 2 * FC), ("lstm_gates", 1), ("lstm_q", 1), ("lstm_k", 1),
          ("lstm_v", 2), ("lstm_o", 2), ("fourier", 2), ("up2", 2 * FC)]
WIDE = [("out1", 16), ("o_mem", 4), ("down1", FT), ("out2", 16), ("down2", FT)]
COLS = [("b_gate", 2 * KT), ("b_ada", ADA), ("norm1", KT), ("norm2", KT), ("norm_m", 8), ("w_conv", 3 * 2 * FT),
        ("b_conv", 2 * FT), ("slope", HEADS)]


def starts(parts):
    found, n = {}, 0
    for name, size in parts:
        found[name] = n
        n += size
    return found, n


AT, G = starts(TILES)
CH, _ = starts(CHUNKS)
SRC, _ = starts(WIDE)
COL, NCOL = starts(COLS)
ADA_OUT, ADA_UP, ADA_DOWN = 2, 6, 2
assert 4 * ADA_OUT + FC * ADA_UP + (FT // 4) * ADA_DOWN == ADA
BLOCKS = [(0, 0, 0, 256, 0), (0, 1, 128, 256, 256), (1, 0, 0, 128, 384), (1, 1, 0, 256, 512)]


class Order:

    def __init__(self, eng, sem):
        self.eng, self.sem, self.n, self.i, self.per = eng, sem, 0, None, 0

    def mark(self, ins):
        ins.then_inc(self.sem, 1)
        self.n += 1

    def wait(self):
        self.eng.wait_ge(self.sem, at(self.n, self.i, self.per))

    def enter(self, i, per):
        self.i, self.per, self.n0 = i, per, self.n

    def leave(self, turns):
        assert self.n - self.n0 == self.per, (self.n - self.n0, self.per)
        self.i, self.n = None, self.n0 + turns * self.per


def at(first, i=None, per=0):
    return first if i is None else i * per + first


def two_blocks(nc, x, mem, stream, w_ada, cols, rows, ln_g, ln_b, norm_f, c_row, gate_bias, dft, out):
    with ExitStack() as ctx:
        def sem(name):
            return ctx.enter_context(nc.semaphore(name))

        place = [16512]

        def sb(name, shape, dt=F32, offset=None):
            here = place[0] if offset is None else offset
            if offset is None:
                size = int(np.prod(shape[1:])) * (2 if dt == BF16 else 4)
                place[0] += -(-size // 32) * 32
            return nc.alloc_sbuf_tensor_at(name, shape, dt, offset=here)

        raw = [sb(f"raw{s}", [P, D]) for s in range(4)]
        whi = sb("whi", [P, 4, 1024], F32R)
        wlo = sb("wlo", [P, 4, 1024], F32R)
        at_xhi = place[0]
        xhi = sb("xhi", [P, KT, S], F32R)
        at_xlo = place[0]
        xlo = sb("xlo", [P, KT, S], F32R)
        at_res = place[0]
        res = sb("res", [P, T, D])
        ident = sb("ident", [P, P])
        ones = sb("ones", [P, P])
        zeros = sb("zeros", [P, 512], BF16)
        dist = sb("dist", [P, 384])
        causal = sb("causal", [P, 384])
        chosen = sb("chosen", [P, 384])
        col = sb("col", [P, NCOL])
        row = sb("row", [P, LATENT + 2 * IDX_DIM])
        mod = sb("mod", [P, ADA])
        scale_col = sb("scale_col", [P, KT])
        expo = sb("expo", [P, 4])
        small = sb("small", [P, 128])
        at_pool = place[0]
        at_pool2 = at_pool + 49152
        shi = sb("shi", [P, 4, S], F32R, at_xhi)
        slo = sb("slo", [P, 4, S], F32R, at_xhi + 4096)
        gate_row = sb("gate_row", [P, D], F32, at_xhi + 8192)
        gamma = sb("gamma", [P, D], F32, at_xlo)
        beta = sb("beta", [P, D], F32, at_xlo + 8192)
        qk = sb("qk", [P, 32, S], F32, at_pool)
        ohi = sb("ohi", [P, 16, S], F32R, at_pool)
        olo = sb("olo", [P, 16, S], F32R, at_pool + 16384)
        vall = sb("vall", [P, T, D], F32, at_pool + 32768)
        mem_nat = sb("mem_nat", [P, T, D], F32, at_pool + 32768)
        merged = sb("merged", [P, KT, S], F32, at_pool + 32768)
        ckv = sb("ckv", [P, T, LATENT], F32, at_pool)
        kw = sb("kw", [P, T, IDX_DIM + IDX_HEADS], F32, at_pool + 2048)
        kn = sb("kn", [P, T, 2 * IDX_DIM], F32, at_pool + 3072)
        kc = sb("kc", [P, T, IDX_DIM], F32, at_pool + 4096)
        ksq = sb("ksq", [P, T, IDX_DIM], F32, at_pool + 4608)
        qi = sb("qi", [P, 8, S], F32, at_res)
        idx_r = sb("idx_r", [P, 2, 512], F32, at_res + 8192)
        score = sb("score", [P, T, S], F32, at_res + 12288)
        best8 = sb("best8", [P, T, 8], F32, at_res + 14336)
        wi = sb("wi", [P, T, IDX_HEADS], F32, at_res + 14400)
        kiT = sb("kiT", [P, S], F32, at_res + 14592)
        qs = sb("qs", [P, 2, S], F32, at_res)
        vs = sb("vs", [P, 2, T, HD], F32, at_res + 2048)
        att_ab = sb("att_ab", [P, 2, 384], F32, at_res + 4096)
        att_s = sb("att_s", [P, 2, 384], F32, at_res + 7168)
        att_e = sb("att_e", [P, 2, 384], F32, at_res + 10240)
        att_pT = sb("att_pT", [P, 2, 384], F32, at_res + 13312)
        sig = sb("sig", [P, 2, 1024], F32, at_res)
        gated_a = sb("gated_a", [P, 1024], F32, at_res + 8192)
        gated_b = sb("gated_b", [P, 1024], F32, at_res + 12288)
        place[0] = at_pool2
        kmT = sb("kmT", [P, HEADS_MEM, S])
        vm = sb("vm", [P, T, HEADS_MEM * HD])
        cb = sb("cb", [P, D])
        ada = [sb(f"ada{s}", [P, D]) for s in range(2)]
        gate_a = sb("gate_a", [P, KT, S], F32, place[0] - 2 * 4 * D)
        at_end = place[0]
        assert at_end <= 229344, at_end
        ckhi = sb("ckhi", [P, 2, S], F32R, at_pool + 8192)
        cklo = sb("cklo", [P, 2, S], F32R, at_pool + 10240)
        qmT = sb("qmT", [P, HEADS_MEM, S], F32, at_pool)
        omT = sb("omT", [P, HEADS_MEM, S], F32, at_pool + 4096)
        mem_p = sb("mem_p", [P, 2, T * S], F32, at_pool + 8192)
        mem_pT = sb("mem_pT", [P, 2, T * S], F32, at_pool + 12288)
        hid = sb("hid", [P, FT, S], F32, at_pool)
        silu = sb("silu", [P, 1024], F32, at_pool2)
        conv = sb("conv", [P, 2, 1024], F32, at_pool2 + 4096)
        diag = sb("diag", [P, KT, P], F32, at_pool2 + 12288)
        xn = sb("xn", [P, T, D], F32, at_pool)
        modulated = sb("modulated", [P, 2, 512], F32, at_pool + 16384)
        so = sb("so", [P, 8, S], F32, at_pool + 16384)
        lq = sb("lq", [P, LH, S], F32, at_pool + 24576)
        lk = sb("lk", [P, LH, S], F32, at_pool + 28672)
        mixT = sb("mixT", [P, KT, S], F32, at_pool + 32768)
        uf = sb("uf", [P, T, 1024], F32, at_pool2)
        lv = sb("lv", [P, T, LH, DV + 2], F32, at_pool2 + 8192)
        dftc = sb("dftc", [P, T, 768], F32, at_pool2 + 16448)
        fa = sb("fa", [P, 2, 512], F32, at_pool2 + 22592)
        tri = sb("tri", [P, 768], F32, at_pool2 + 26688)
        sel = sb("sel", [LH, LH, P], F32, at_pool2 + 29760)
        lcols = sb("lcols", [P, 2, 16], F32, at_pool2 + 31808)
        gbias = sb("gbias", [P, 1], F32, at_pool2 + 31936)
        lx = sb("lx", [P, 768], F32, at_pool)
        le = sb("le", [P, 768], F32, at_pool + 3072)
        lp = sb("lp", [P, 768], F32, at_pool + 6144)
        lh = sb("lh", [P, T, DV], F32, at_pool + 9216)
        g_in = sb("g_in", [LH, 2, S], F32, at_pool)
        g_fo = sb("g_fo", [LH, 2, S], F32, at_pool + 2048)
        g_e = sb("g_e", [LH, 2, S], F32, at_pool + 4096)
        g_sum = sb("g_sum", [LH, 2, S], F32, at_pool + 6144)
        g_a = sb("g_a", [LH, 2, S], F32, at_pool + 8192)
        g_max = sb("g_max", [LH, 2, S], F32, at_pool + 11264)
        g_m = sb("g_m", [LH, 2, S], F32, at_pool + 13312)
        iota_i = sb("iota_i", [P, 384], I32, at_pool)

        ps = ctx.enter_context(nc.psum_tensor("ps", [P, 8, 512], F32))

        def var(n, t=0, w=1):
            return small[:, 2 * n + t:2 * n + t + w]

        def rstd(n, t=0, w=1):
            return small[:, 40 + 2 * n + t:40 + 2 * n + t + w]

        def misc(n, w=1):
            return small[:, 80 + n:80 + n + w]

        raw_landed = [sem(f"raw_landed{s}") for s in range(4)]
        hi_ready = sem("hi_ready")
        lo_ready = sem("lo_ready")
        weights_used = sem("weights_used")
        pair_read = [sem(f"pair_read{p}") for p in range(2)]
        x_landed = sem("x_landed")
        mem_landed = sem("mem_landed")
        consts_landed = sem("consts_landed")
        late_landed = sem("late_landed")
        cb_landed = sem("cb_landed")
        cb_ready = sem("cb_ready")
        ln_landed = sem("ln_landed")
        ada_landed = [sem(f"ada_landed{s}") for s in range(2)]
        ada_used = sem("ada_used")
        built = sem("built")
        xT_done = sem("xT_done")
        xhi_ready = sem("xhi_ready")
        xlo_ready = sem("xlo_ready")
        shi_ready = sem("shi_ready")
        slo_ready = sem("slo_ready")
        var_ready = sem("var_ready")
        rstd_ready = sem("rstd_ready")
        mean_ready = sem("mean_ready")
        sq_ready = sem("sq_ready")
        res_ready = sem("res_ready")
        xn_ready = sem("xn_ready")
        mod_ready = sem("mod_ready")
        ck_squared = sem("ck_squared")
        ck_ready = sem("ck_ready")
        kn_ready = sem("kn_ready")
        small_T = sem("small_T")
        ckhi_ready = sem("ckhi_ready")
        cklo_ready = sem("cklo_ready")
        ki_ready = sem("ki_ready")
        idx_done = sem("idx_done")
        idx_relu = sem("idx_relu")
        idx_added = sem("idx_added")
        qv_ready = sem("qv_ready")
        att_free = sem("att_free")
        att_scores = sem("att_scores")
        att_max = sem("att_max")
        att_exp = sem("att_exp")
        att_p = sem("att_p")
        att_T = sem("att_T")
        att_pT_ready = sem("att_pT_ready")
        att_o = sem("att_o")
        att_ohi = sem("att_ohi")
        sig_ready = sem("sig_ready")
        merged_ready = sem("merged_ready")
        m_scores = sem("m_scores")
        m_max = sem("m_max")
        m_exp = sem("m_exp")
        m_p = sem("m_p")
        m_T = sem("m_T")
        m_pT = sem("m_pT")
        m_o = sem("m_o")
        m_out = sem("m_out")
        conv_mid = sem("conv_mid")
        conv_done = sem("conv_done")
        silu_ready = sem("silu_ready")
        g_copied = sem("g_copied")
        g_abs = sem("g_abs")
        g_exp = sem("g_exp")
        g_one = sem("g_one")
        g_ln = sem("g_ln")
        g_stab = sem("g_stab")
        g_floor = sem("g_floor")
        g_cols_T = sem("g_cols_T")
        g_cols = sem("g_cols")
        l_bc = sem("l_bc")
        l_x = sem("l_x")
        l_e = sem("l_e")
        l_st = sem("l_st")
        l_p = sem("l_p")
        l_num = sem("l_num")
        l_h = sem("l_h")
        l_sq = sem("l_sq")
        l_hn = sem("l_hn")
        l_hT = sem("l_hT")
        mix_m = sem("mix_m")
        f_first = sem("f_first")
        f_copied = sem("f_copied")
        f_second = sem("f_second")
        mix_f = sem("mix_f")
        diag_ready = sem("diag_ready")
        gate_T = sem("gate_T")
        gate_ready = sem("gate_ready")
        out_ready = sem("out_ready")
        out_landed = sem("out_landed")
        act_order = sem("act_order")
        dve_order = sem("dve_order")

        def through(g, half=2):
            return 2 * g + half

        def pair(c):
            return ps[:, 2 * (c % 2):2 * (c % 2) + 2, :].rearrange("p b n -> p (b n)")

        def reads(c):
            return c // 2 + 1

        block = ctx.enter_context(nc.Block())

        @block.sync
        def _(sp):
            sp.dma_start(mem_nat[:], mem.rearrange("(t p) d -> p t d", p=P)).then_inc(mem_landed, 16)
            for s in range(4):
                sp.dma_start(raw[s][:], stream[s]).then_inc(raw_landed[s], 16)
            sp.dma_start(res[:], x.rearrange("(t p) d -> p t d", p=P)).then_inc(x_landed, 16)
            with sp.Fori(1, G // 4) as i:
                for s in range(4):
                    sp.wait_ge(lo_ready, at(2 * s - 6, i, 8))
                    sp.dma_start(raw[s][:], stream[at(s, i, 4)]).then_inc(raw_landed[s], 16)
            for g in range(G // 4 * 4, G):
                sp.wait_ge(lo_ready, 2 * (g - 4) + 2)
                sp.dma_start(raw[g % 4][:], stream[g]).then_inc(raw_landed[g % 4], 16)
            for t in range(T):
                sp.wait_ge(out_ready, t + 1)
                sp.dma_start(out[t * P:(t + 1) * P, :], xn[:, t]).then_inc(out_landed, 16)
            sp.wait_ge(out_landed, 16 * T)

        @block.gpsimd
        def _(pool):
            pool.memset(ident[:], 0.0).then_inc(built, 1)
            pool.memset(ones[:], 1.0).then_inc(built, 1)
            pool.memset(zeros[:], 0.0).then_inc(built, 1)
            pool.memset(expo[:], -0.5).then_inc(built, 1)
            pool.memset(causal[:], 0.0).then_inc(built, 1)
            pool.wait_ge(built, 5)
            pool.affine_select(out=ident[:], in_=ident[:], compare_op=ALU.not_equal, fill=1.0, base=0,
                               pattern=[[-1, P]], channel_multiplier=1).then_inc(built, 1)
            for q0, c0, c1 in ((0, 0, 128), (128, 128, 384)):
                pool.affine_select(out=causal[:, c0:c1], in_=causal[:, c0:c1], compare_op=ALU.is_ge, fill=OUT_OF_SIGHT,
                                   base=q0, pattern=[[-1, c1 - c0]], channel_multiplier=1).then_inc(built, 1)
                pool.iota(iota_i[:, c0:c1], pattern=[[1, c1 - c0]], base=-q0, channel_multiplier=-1).then_inc(built, 1)
            pool.wait_ge(built, 10)
            pool.tensor_copy(dist[:], iota_i[:]).then_inc(built, 1)

            def power(n, w):
                pool.wait_ge(var_ready, n + 1)
                pool.tensor_tensor(rstd(n, 0, w), var(n, 0, w), expo[:, 0:w], ALU.pow).then_inc(rstd_ready, 1)

            power(0, 2)
            power(1, 2)
            pool.wait_ge(merged_ready, 4)
            for n in range(2):
                pool.dma_start(ada[n][:], w_ada[n]).then_inc(ada_landed[n], 16)

            def ada_turns(n0, turns, per):
                with pool.Fori(0, turns) as i:
                    for s in range(per):
                        pool.wait_ge(ada_used, at(n0 + s - 1, i, per))
                        pool.wait_ge(built, 11)
                        pool.dma_start(ada[s % 2][:], w_ada[at(n0 + s, i, per)]).then_inc(ada_landed[s % 2], 16)

            first = 4 * ADA_OUT
            ada_turns(2, first // 2, 2)
            power(2, 1)
            power(3, 1)
            power(4, 1)
            power(5, 1)
            ada_turns(first + 2, (ADA - first - 2) // 2, 2)
            pool.wait_ge(ada_used, ADA)
            pool.dma_start(dftc[:], dft.rearrange("(t p) n -> p t n", p=P)).then_inc(late_landed, 16)
            pool.dma_start(gbias[:], gate_bias).then_inc(late_landed, 16)
            pool.memset(tri[:], 1.0).then_inc(built, 1)
            pool.memset(sel[:], 0.0).then_inc(built, 1)
            pool.memset(lv[:, :, :, DV:DV + 2], 1.0).then_inc(built, 1)
            pool.wait_ge(built, 14)
            for d, st, t0, t1, c0 in BLOCKS:
                sign = 1 if d == 0 else -1
                pool.affine_select(out=tri[:, c0:c0 + t1 - t0], in_=tri[:, c0:c0 + t1 - t0], compare_op=ALU.is_ge,
                                   fill=0.0, base=sign * (t0 - P * st), pattern=[[sign, t1 - t0]],
                                   channel_multiplier=-sign).then_inc(built, 1)
            pool.affine_select(out=sel[:], in_=sel[:], compare_op=ALU.not_equal, fill=1.0, base=0,
                               pattern=[[-1, LH], [0, P]], channel_multiplier=1).then_inc(built, 1)
            for n, w in [(6, 1), (7, 1), (8, 1), (9, 1), (10, 2), (11, 2), (12, 2), (13, 2), (14, 1), (15, 1), (16, 1), (17, 1)]:
                power(n, w)

        @block.scalar
        def _(act):
            order = Order(act, act_order)
            act.dma_start(col[:], cols).then_inc(consts_landed, 16)
            act.dma_start(row[:], rows.partition_broadcast(P)).then_inc(consts_landed, 16)
            act.dma_start(cb[:], c_row.partition_broadcast(P)).then_inc(cb_landed, 16)

            def params_in_place():
                act.wait_ge(consts_landed, 32)

            def upper(g, i=None, per=0):
                if g >= G:
                    return
                for half in range(2):
                    h = 2 * g + half
                    if half == 0:
                        act.wait_ge(raw_landed[g % 4], at(16 * (g // 4 + 1), i, 4 * per))
                    if h >= 4:
                        act.wait_ge(weights_used, at(h - 3, i, 2 * per))
                    act.activation(whi[:, h % 4], raw[g % 4][:, 1024 * half:1024 * half + 1024], ACT.Copy)\
                       .then_inc(hi_ready, 1)

            def x_upper(n):
                for b in range(8):
                    act.wait_ge(xT_done, 8 * n + b + 1)
                    act.activation(xhi[:, 2 * b:2 * b + 2].rearrange("p k t -> p (k t)"), ps[:, b], ACT.Copy)\
                       .then_inc(xhi_ready, 1)

            def x_upper_modulated(n, shift):
                act.wait_ge(mod_ready, n - 3)
                for b in range(8):
                    act.wait_ge(xT_done, 8 * n + b + 1)
                    if b >= 2:
                        act.wait_ge(xlo_ready, 8 * n + b - 1)
                    for f in range(2):
                        k = 2 * b + f
                        order.mark(act.activation(modulated[:, b % 2, S * f:S * f + S], ps[:, b, S * f:S * f + S], ACT.Identity,
                                                  bias=mod[:, shift + k:shift + k + 1], scale=scale_col[:, k:k + 1]))
                    order.wait()
                    act.activation(xhi[:, 2 * b:2 * b + 2].rearrange("p k t -> p (k t)"), modulated[:, b % 2], ACT.Copy)\
                       .then_inc(xhi_ready, 1)

            def read_out(c, g, dst, func=ACT.Copy, half=2, i=None, per=0):
                act.wait_ge(weights_used, at(through(g, half), i, 2 * per))
                if i is not None:
                    params_in_place()
                act.activation(dst, pair(c), func).then_inc(pair_read[c % 2], 1)

            def read_out_rows(c, g, dst, func=ACT.Copy, half=2):
                act.wait_ge(weights_used, through(g, half))
                act.activation(dst, ps[:, 2 * (c % 2):2 * (c % 2) + 2, :], func).then_inc(pair_read[c % 2], 1)

            def tiles4(tensor, k0):
                return tensor[:, k0:k0 + 4].rearrange("p k t -> p (k t)")

            upper(0)
            x_upper(0)
            for g in range(0, 4):
                upper(g + 1)
            read_out(CH["k_mem"], 3, tiles4(kmT, 0))
            for g in range(4, 8):
                upper(g + 1)
            read_out_rows(CH["v_mem"], 7, vm[:])
            x_upper(1)
            g0 = AT["latent"]
            for g in range(g0, g0 + 3):
                upper(g + 1)
            act.wait_ge(pair_read[CH["latent"] % 2], reads(CH["latent"]))
            for t in range(T):
                act.activation(idx_r[:, t, 0:LATENT], ckv[:, t], ACT.Square, accum_out=misc(t)).then_inc(ck_squared, 1)
            upper(g0 + 4)
            upper(g0 + 5)
            act.wait_ge(small_T, 1)
            act.activation(ckhi[:].rearrange("p c t -> p (c t)"), ps[:, 4], ACT.Copy).then_inc(ckhi_ready, 1)
            act.wait_ge(small_T, 2)
            act.activation(kiT[:], ps[:, 5, 0:S], ACT.Copy).then_inc(ki_ready, 1)
            for g in range(AT["q_idx"] + 2, AT["q_idx"] + 8):
                upper(g + 1)
                if g in (AT["q_idx"] + 3, AT["q_idx"] + 7):
                    c = CH["q_idx"] + (g > AT["q_idx"] + 3)
                    read_out(c, g, tiles4(qi, 4 * (c - CH["q_idx"])))
            for n in range(8):
                g = AT["v_moba"] + n
                upper(g + 1)
                for h in (2 * n, 2 * n + 1):
                    act.wait_ge(idx_done, h + 1)
                    if h >= 2:
                        act.wait_ge(idx_added, h - 1)
                    act.activation(idx_r[:, h % 2], ps[:, 4 + h % 4], ACT.Relu, scale=IDX_DIM ** -0.5).then_inc(idx_relu, 1)
                if n in (3, 7):
                    c = CH["v_moba"] + n // 4
                    read_out_rows(c, g, vall[:, :, 1024 + 512 * (n // 4):1536 + 512 * (n // 4)])
            g = AT["w_uk"]
            upper(g + 1)
            for n in range(2):
                read_out(CH["w_uk"] + n, g, tiles4(qk, 24 + 4 * n), half=n + 1)
            g = AT["w_uv"]
            upper(g + 1)
            for n in range(2):
                read_out_rows(CH["w_uv"] + n, g, vall[:, :, 512 * n:512 * n + 512], half=n + 1)
            act.wait_ge(cb_landed, 16)
            act.activation(cb[:], cb[:], ACT.Silu).then_inc(cb_ready, 1)
            g0 = AT["qk"]
            with act.Fori(0, 3) as i:
                for s in range(8):
                    upper(g0 + s + 1, i, 8)
                    if s % 4 == 3:
                        read_out(CH["qk"] + s // 4, g0 + s, qk[:, bass.ds(at(s - 3, i, 8), 4)].rearrange("p k t -> p (k t)"),
                                 i=i, per=8)

            g0, c0 = AT["gate_a"], CH["gate_a"]
            with act.Fori(0, 2) as i:
                for q in range(4):
                    g = g0 + 2 * q
                    for j in range(2):
                        act.activation(qs[:, j], qk[:, at(8 * j + q, i, 4)], ACT.Copy).then_inc(qv_ready, 1)
                        act.activation(vs[:, j], vall[:, :, bass.ds(at(1024 * j + HD * q, i, 4 * HD), HD)], ACT.Copy)\
                           .then_inc(qv_ready, 1)
                    upper(g + 1, i, 8)
                    for j in range(2):
                        for t, (k0, k1) in enumerate(((0, 128), (128, 384))):
                            act.wait_ge(att_max, at(4 * q + 2 * j + t + 1, i, 16))
                            act.activation(att_e[:, j, k0:k1], att_s[:, j, k0:k1], ACT.Exp, bias=misc(8 + 2 * j + t),
                                           accum_out=misc(12 + 2 * j + t)).then_inc(att_exp, 1)
                    upper(g + 2, i, 8)
                    for j in range(2):
                        act.wait_ge(att_T, at(2 * q + j + 1, i, 8))
                        act.activation(att_pT[:, j], ps[:, 6 + j, 0:384], ACT.Copy).then_inc(att_pT_ready, 1)
                    if q % 2 == 1:
                        c = c0 + q // 2
                        read_out(c, g + 1, gate_a[:, bass.ds(at(2 * q - 2, i, 8), 4)].rearrange("p k t -> p (k t)"), i=i, per=8)
                    act.wait_ge(att_o, at(2 * q + 2, i, 8))

            g0, c0 = AT["gates"], CH["gates"]

            def gate(n, src, c, i):
                act.wait_ge(pair_read[c % 2], at(reads(c), i, 3))
                params_in_place()
                u = 4 * unit
                for m in range(4):
                    ins = act.activation(sig[:, n, S * m:S * m + S], src(m), ACT.Sigmoid,
                                         bias=col[:, bass.ds(at(COL["b_gate"] + KT * n + u + m, i, 8), 1)])
                return ins

            with act.Fori(0, 2) as i:
                for unit in range(2):
                    g, c = g0 + 8 * unit, c0 + 3 * unit
                    gate(0, lambda m: gate_a[:, at(4 * unit + m, i, 8)], c - 3, i).then_inc(sig_ready, 1)
                    for s in range(8):
                        upper(g + s + 1, i, 16)
                        if s == 5:
                            act.wait_ge(weights_used, at(through(g + s), i, 32))
                            gate(1, lambda m: pair(c + 1)[:, S * m:S * m + S], c - 1, i).then_inc(pair_read[(c + 1) % 2], 1)

            def wide_start(name, n_ln=None):
                act.wait_ge(weights_used, through(AT[name] - 1))
                if n_ln is not None:
                    act.dma_start(gamma[:], ln_g[n_ln:n_ln + 1].partition_broadcast(P)).then_inc(ln_landed, 16)
                    act.dma_start(beta[:], ln_b[n_ln:n_ln + 1].partition_broadcast(P)).then_inc(ln_landed, 16)

            def wide_turns(name, src, turns, i0=0):
                g0 = AT[name]

                def turn(i):
                    for s in range(4):
                        act.activation(shi[:, s], src[:, at(s, i, 4)], ACT.Copy).then_inc(shi_ready, 1)
                        upper(g0 + s + 1, i, 4)

                if turns == 1:
                    turn(None)
                else:
                    with act.Fori(0, turns) as i:
                        turn(i)

            def squares(n, src, count, centred):
                for t in range(T):
                    act.wait_ge(mean_ready if centred else res_ready, count + t + 1)
                    bias = misc(2 + t) if centred else 0.0
                    act.activation(ps[:, 4 * t:4 * t + 4].rearrange("p b n -> p (b n)"), src[:, t], ACT.Square, bias=bias,
                                   accum_out=misc(4 + t)).then_inc(sq_ready, 1)

            act.wait_ge(merged_ready, 4)
            act.dma_start(res[:], x.rearrange("(t p) d -> p t d", p=P)).then_inc(x_landed, 16)
            wide_start("out1", 0)
            wide_turns("out1", merged, 4)
            squares(2, res, 0, True)
            x_upper(2)
            g0 = AT["q_mem"]
            for g in range(g0, g0 + 4):
                upper(g + 1)
            read_out(CH["q_mem"], g0 + 3, tiles4(qmT, 0))

            def m_exps(h):
                act.wait_ge(m_max, h + 1)
                for t in range(T):
                    act.activation(mem_p[:, h % 2, S * t:S * t + S], ps[:, 4 + h % 2, S * t:S * t + S], ACT.Exp,
                                   bias=misc(8 + 2 * (h % 2) + t), scale=HD ** -0.5,
                                   accum_out=misc(12 + 2 * (h % 2) + t)).then_inc(m_exp, 1)

            m_exps(0)
            m_exps(1)
            for h in range(HEADS_MEM):
                act.wait_ge(m_T, h + 1)
                act.activation(mem_pT[:, h % 2], ps[:, 6 + h % 2], ACT.Copy).then_inc(m_pT, 1)
                act.wait_ge(m_o, h + 1)
                act.activation(omT[:, h], ps[:, 4 + h % 2, 0:S], ACT.Copy).then_inc(m_out, 1)
                if h + 2 < HEADS_MEM:
                    m_exps(h + 2)
            wide_start("o_mem", 1)
            act.wait_ge(m_out, HEADS_MEM)
            wide_turns("o_mem", omT, 1)
            squares(4, res, 2, True)
            x_upper(3)
            g0, c0 = AT["up1"], CH["up1"]
            with act.Fori(0, FC) as i:
                for s in range(8):
                    upper(g0 + s + 1, i, 8)
                    if s == 3:
                        act.wait_ge(weights_used, at(through(g0 + s), i, 16))
                        act.wait_ge(pair_read[(c0 + 1) % 2], at(reads(c0 - 1), i, 1))
                        act.activation(silu[:], pair(c0), ACT.Silu).then_inc(pair_read[c0 % 2], 1)
            wide_start("down1", 2)
            act.wait_ge(pair_read[(c0 + 1) % 2], reads(c0 + 2 * FC - 1))
            wide_turns("down1", hid, FC)
            squares(6, res, 4, True)
            squares(8, res, 4, False)
            x_upper_modulated(4, 0)
            g0 = AT["lstm_gates"]
            upper(g0 + 1)
            g0 = AT["lstm_q"]
            for g in range(g0, g0 + 4):
                upper(g + 1)
            read_out(CH["lstm_q"], g0 + 3, tiles4(lq, 0))
            act.wait_ge(g_abs, 1)
            act.activation(g_e[:], g_e[:], ACT.Exp, scale=-1.0).then_inc(g_exp, 1)
            g0 = AT["lstm_k"]
            for g in range(g0, g0 + 4):
                upper(g + 1)
            read_out(CH["lstm_k"], g0 + 3, tiles4(lk, 0))
            act.wait_ge(g_one, 1)
            act.activation(g_e[:], g_e[:], ACT.Ln).then_inc(g_ln, 1)
            g0 = AT["lstm_v"]
            for n in range(8):
                upper(g0 + n + 1)
                if n % 4 == 3:
                    c = CH["lstm_v"] + n // 4
                    act.wait_ge(weights_used, through(g0 + n))
                    if n == 3:
                        act.wait_ge(built, 14)
                    for t in range(T):
                        ins = act.activation(lv[:, t, 2 * (n // 4):2 * (n // 4) + 2, 0:DV],
                                             ps[:, 2 * (c % 2) + t].rearrange("p (h v) -> p h v", h=2), ACT.Copy)
                    ins.then_inc(pair_read[c % 2], 1)
            act.wait_ge(g_stab, 1)
            act.activation(g_m[:], g_m[:], ACT.Exp, scale=-1.0).then_inc(g_floor, 1)
            g0 = AT["lstm_o"]
            for n in range(8):
                upper(g0 + n + 1)
                if n % 4 == 3:
                    read_out(CH["lstm_o"] + n // 4, g0 + n, tiles4(so, 4 * (n // 4)), ACT.Sigmoid)
            g0 = AT["fourier"]
            for n in range(8):
                upper(g0 + n + 1)
                if n % 4 == 3:
                    read_out_rows(CH["fourier"] + n // 4, g0 + n, uf[:, :, 512 * (n // 4):512 * (n // 4) + 512])
            for h in range(LH):
                act.wait_ge(l_x, h + 1)
                act.activation(le[:], lx[:], ACT.Exp, scale=-1.0).then_inc(l_e, 1)
                for f in range(2):
                    act.wait_ge(f_first, 2 * h + f + 1)
                    act.activation(fa[:, f], ps[:, 2 + f], ACT.Copy).then_inc(f_copied, 1)
                act.wait_ge(f_second, h + 1)
                act.activation(mixT[:, 2 * h:2 * h + 2].rearrange("p k t -> p (k t)"), ps[:, 2], ACT.Copy).then_inc(mix_f, 1)
                for t in range(T):
                    act.wait_ge(l_h, 2 * h + t + 1)
                    act.activation(lx[:, S * t:S * t + S], lh[:, t], ACT.Square, accum_out=misc(16 + t)).then_inc(l_sq, 1)

            def gate_rows(n):
                act.wait_ge(gate_T, n + 1)
                act.activation(gate_row[:], ps[:, 4:8].rearrange("p b n -> p (b n)"), ACT.Copy).then_inc(gate_ready, 1)

            wide_start("out2")
            gate_rows(0)
            act.wait_ge(mix_m, 2 * LH)
            wide_turns("out2", mixT, 4)
            squares(14, res, 6, False)
            x_upper_modulated(5, 3 * KT)
            g0, c0 = AT["up2"], CH["up2"]

            def middle_tap(q, i):
                act.wait_ge(weights_used, at(through(g0 + 4 * q + 3), i, 16))
                if q == 0:
                    act.wait_ge(conv_done, at(1, i, 1))
                params_in_place()
                for m in range(4):
                    tap = at(COL["w_conv"] + 2 * FT + FT * q + m, i, 4)
                    bias = at(COL["b_conv"] + FT * q + m, i, 4)
                    ins = act.activation(conv[:, q, S * m:S * m + S], pair(c0 + q)[:, S * m:S * m + S], ACT.Identity,
                                         bias=col[:, bass.ds(bias, 1)], scale=col[:, bass.ds(tap, 1)])
                ins.then_inc(conv_mid, 1)

            def silu_of_first(i):
                act.wait_ge(pair_read[c0 % 2], at(reads(c0), i, 1))
                act.activation(silu[:], conv[:, 0], ACT.Silu).then_inc(silu_ready, 1)

            for s in range(4):
                upper(g0 + s + 1)
            with act.Fori(0, FC - 1) as i:
                for s in range(8):
                    upper(g0 + 4 + s + 1, i, 8)
                    if s % 4 == 0:
                        middle_tap(s // 4, i)
                    if s == 2:
                        silu_of_first(i)
            for s in range(4):
                upper(AT["down2"] - 4 + s + 1)
                if s == 0:
                    middle_tap(0, FC - 1)
                if s == 2:
                    silu_of_first(FC - 1)
            middle_tap(1, FC - 1)
            wide_start("down2")
            act.dma_start(gamma[:], norm_f.partition_broadcast(P)).then_inc(ln_landed, 16)
            gate_rows(1)
            act.wait_ge(conv_done, FC + 1)
            g0 = AT["down2"]
            with act.Fori(0, FC - 1) as i:
                for s in range(4):
                    act.activation(shi[:, s], hid[:, at(s, i, 4)], ACT.Copy).then_inc(shi_ready, 1)
                    upper(g0 + s + 1, i, 4)
            for s in range(4):
                act.activation(shi[:, s], hid[:, FT - 4 + s], ACT.Copy).then_inc(shi_ready, 1)
                upper(g0 + FT - 4 + s + 1)
            squares(16, res, 8, False)

        @block.vector
        def _(dve):
            order = Order(dve, dve_order)

            def rest(g, i=None, per=0):
                if g >= G:
                    return
                for half in range(2):
                    h = 2 * g + half
                    dve.wait_ge(hi_ready, at(h + 1, i, 2 * per))
                    dve.tensor_tensor(wlo[:, h % 4], raw[g % 4][:, 1024 * half:1024 * half + 1024], whi[:, h % 4].bitcast(F32),
                                      ALU.subtract).then_inc(lo_ready, 1)

            def x_rest(n, src=None):
                for b in range(8):
                    dve.wait_ge(xhi_ready, 8 * n + b + 1)
                    hi = xhi[:, 2 * b:2 * b + 2].rearrange("p k t -> p (k t)")
                    lo = xlo[:, 2 * b:2 * b + 2].rearrange("p k t -> p (k t)")
                    dve.tensor_tensor(lo, ps[:, b] if src is None else src[:, b % 2], hi.bitcast(F32), ALU.subtract)\
                       .then_inc(xlo_ready, 1)

            def modulation(n, i=None, per=0):
                slot = n % 2
                dve.wait_ge(ada_landed[slot], at(16 * (n // 2 + 1), i, 8 * per))
                dve.scalar_tensor_tensor(out=ada[slot][:], in0=ada[slot][:], scalar=1.0, in1=cb[:], op0=ALU.mult, op1=ALU.mult,
                                         accum_out=mod[:, bass.ds(at(n, i, per), 1)]).then_inc(ada_used, 1)

            rest(0)
            x_rest(0)
            for g in range(0, 8):
                rest(g + 1)
            x_rest(1)
            g0, wide_n = AT["latent"], LATENT + IDX_DIM + IDX_HEADS
            for g in range(g0, g0 + 3):
                rest(g + 1)
            dve.wait_ge(weights_used, through(g0 + 2))
            dve.wait_ge(built, 11)
            order.mark(dve.tensor_copy(kw[:], ps[:, 0:2, LATENT:wide_n]))
            dve.tensor_copy(ckv[:], ps[:, 0:2, 0:LATENT]).then_inc(pair_read[0], 1)
            dve.wait_ge(ck_squared, 2)
            dve.tensor_scalar(var(0, 0, 2), misc(0, 2), 1.0 / LATENT, LN_EPS, ALU.mult, ALU.add).then_inc(var_ready, 1)
            order.wait()
            order.mark(dve.tensor_reduce(misc(2, 2), kw[:, :, 0:IDX_DIM], AX_X, ALU.add))
            order.wait()
            order.mark(dve.tensor_scalar(misc(4, 2), misc(2, 2), -1.0 / IDX_DIM, None, ALU.mult))
            order.wait()
            for t in range(T):
                order.mark(dve.tensor_scalar(kc[:, t], kw[:, t, 0:IDX_DIM], misc(4 + t), None, ALU.add))
            order.wait()
            order.mark(dve.tensor_tensor(ksq[:], kc[:], kc[:], ALU.mult))
            order.wait()
            order.mark(dve.tensor_reduce(misc(6, 2), ksq[:], AX_X, ALU.add))
            order.wait()
            dve.tensor_scalar(var(1, 0, 2), misc(6, 2), 1.0 / IDX_DIM, LN_EPS, ALU.mult, ALU.add).then_inc(var_ready, 1)
            order.mark(dve.tensor_scalar(wi[:], kw[:, :, IDX_DIM:IDX_DIM + IDX_HEADS], IDX_HEADS ** -0.5, None, ALU.mult))
            rest(g0 + 4)
            dve.wait_ge(consts_landed, 32)
            dve.wait_ge(rstd_ready, 1)
            for t in range(T):
                dve.scalar_tensor_tensor(out=ckv[:, t], in0=ckv[:, t], scalar=rstd(0, t), in1=row[:, 0:LATENT],
                                         op0=ALU.mult, op1=ALU.mult).then_inc(ck_ready, 1)
            dve.wait_ge(rstd_ready, 2)
            for t in range(T):
                order.mark(dve.scalar_tensor_tensor(out=kc[:, t], in0=kc[:, t], scalar=rstd(1, t),
                                                    in1=row[:, LATENT:LATENT + IDX_DIM], op0=ALU.mult, op1=ALU.mult))
            order.wait()
            for t in range(T):
                for n in range(2):
                    dve.tensor_tensor(kn[:, t, IDX_DIM * n:IDX_DIM * n + IDX_DIM], kc[:, t],
                                      row[:, LATENT + IDX_DIM:LATENT + 2 * IDX_DIM], ALU.add).then_inc(kn_ready, 1)
            rest(g0 + 5)
            dve.wait_ge(ckhi_ready, 1)
            dve.tensor_tensor(cklo[:].rearrange("p c t -> p (c t)"), ps[:, 4], ckhi[:].rearrange("p c t -> p (c t)").bitcast(F32),
                              ALU.subtract).then_inc(cklo_ready, 1)
            for g in range(AT["q_idx"] + 2, AT["q_idx"] + 8):
                rest(g + 1)
            for n in range(8):
                rest(AT["v_moba"] + n + 1)
                for h in (2 * n, 2 * n + 1):
                    dve.wait_ge(idx_relu, h + 1)
                    for t in range(T):
                        relu = idx_r[:, h % 2, S * t:S * t + S]
                        if h == 0:
                            ins = dve.tensor_scalar(score[:, t], relu, wi[:, t, h:h + 1], None, ALU.mult)
                        else:
                            if t == 0:
                                order.wait()
                            else:
                                dve.wait_ge(idx_added, h)
                            ins = dve.scalar_tensor_tensor(out=score[:, t], in0=relu, scalar=wi[:, t, h:h + 1], in1=score[:, t],
                                                           op0=ALU.mult, op1=ALU.add)
                        if t == 0:
                            order.mark(ins)
                        else:
                            ins.then_inc(idx_added, 1)
            rest(AT["w_uk"] + 1)
            dve.wait_ge(built, 11)
            dve.wait_ge(idx_added, IDX_HEADS)
            seen = [(score[:, 0, 0:128], 0, 128), (score[:, 1, :], 128, 384)]
            for work, c0, c1 in seen:
                order.mark(dve.tensor_tensor(work, work, causal[:, c0:c1], ALU.add))
            for n in range(TOPK // 8):
                order.wait()
                for t, (work, _, _) in enumerate(seen):
                    order.mark(dve.max(best8[:, t], work))
                order.wait()
                for t, (work, _, _) in enumerate(seen):
                    order.mark(dve.match_replace(work, best8[:, t], work, TAKEN))
                if n == 3:
                    rest(AT["w_uv"] + 1)
            order.wait()
            for work, c0, c1 in seen:
                order.mark(dve.tensor_scalar(work, work, TAKEN / 2, OUT_OF_SIGHT, ALU.is_gt, ALU.mult))
            order.wait()
            order.mark(dve.tensor_tensor(chosen[:, 0:128], seen[0][0], causal[:, 0:128], ALU.add))
            dve.tensor_tensor(chosen[:, 128:384], seen[1][0], causal[:, 128:384], ALU.add).then_inc(att_free, 1)
            dve.wait_ge(cb_ready, 1)
            g0 = AT["qk"]
            with dve.Fori(0, 3) as i:
                for s in range(8):
                    rest(g0 + s + 1, i, 8)

            dve.wait_ge(att_free, 1)
            order.wait()
            c = CH["qk"] + 4
            dve.wait_ge(pair_read[c % 2], reads(c))
            g0 = AT["gate_a"]
            with dve.Fori(0, 2) as i:
                order.enter(i, 24)
                for q in range(4):
                    g = g0 + 2 * q
                    for j, mask in enumerate((chosen, causal)):
                        order.mark(dve.scalar_tensor_tensor(out=att_ab[:, j], in0=dist[:],
                                                            scalar=col[:, bass.ds(at(COL["slope"] + q, i, 4), 1)],
                                                            in1=mask[:], op0=ALU.mult, op1=ALU.add))
                    rest(g + 1, i, 8)
                    for j in range(2):
                        dve.wait_ge(att_scores, at(2 * q + j + 1, i, 8))
                        order.wait()
                        order.mark(dve.scalar_tensor_tensor(out=att_s[:, j], in0=ps[:, 4 + j, 0:384], scalar=HD ** -0.5,
                                                            in1=att_ab[:, j], op0=ALU.mult, op1=ALU.add))
                        order.wait()
                        for t, (k0, k1) in enumerate(((0, 128), (128, 384))):
                            dve.tensor_reduce(misc(8 + 2 * j + t), att_s[:, j, k0:k1], AX_X, ALU.max, negate=True)\
                               .then_inc(att_max, 1)
                    for j in range(2):
                        dve.wait_ge(att_exp, at(4 * q + 2 * j + 2, i, 16))
                        order.mark(dve.reciprocal(misc(12 + 2 * j, 2), misc(12 + 2 * j, 2)))
                        order.wait()
                        for t, (k0, k1) in enumerate(((0, 128), (128, 384))):
                            dve.tensor_scalar(att_e[:, j, k0:k1], att_e[:, j, k0:k1], misc(12 + 2 * j + t), None, ALU.mult)\
                               .then_inc(att_p, 1)
                    rest(g + 2, i, 8)
                    for j in range(2):
                        dve.wait_ge(att_o, at(2 * q + j + 1, i, 8))
                        dve.tensor_scalar(ohi[:, at(8 * j + q, i, 4)], ps[:, 4 + j, 0:S], 1.0, None, ALU.mult).then_inc(att_ohi, 1)
                    for j in range(2):
                        dve.wait_ge(att_ohi, at(2 * q + j + 1, i, 8))
                        dve.tensor_tensor(olo[:, at(8 * j + q, i, 4)], ps[:, 4 + j, 0:S],
                                          ohi[:, at(8 * j + q, i, 4)].bitcast(F32), ALU.subtract).then_inc(att_free, 1)
                order.leave(2)

            g0, c0 = AT["gates"], CH["gates"]
            with dve.Fori(0, 2) as i:
                for unit in range(2):
                    g, c = g0 + 8 * unit, c0 + 3 * unit
                    for s in range(8):
                        rest(g + s + 1, i, 16)
                        if s == 1:
                            dve.wait_ge(weights_used, at(through(g + s), i, 32))
                            dve.wait_ge(sig_ready, at(unit + 1, i, 2))
                            dve.tensor_tensor(gated_a[:], pair(c), sig[:, 0], ALU.mult).then_inc(pair_read[c % 2], 1)
                        if s == 7:
                            dve.wait_ge(weights_used, at(through(g + s), i, 32))
                            dve.wait_ge(pair_read[(c + 1) % 2], at(reads(c + 1), i, 3))
                            dve.tensor_tensor(gated_b[:], pair(c + 2), sig[:, 1], ALU.mult).then_inc(pair_read[c % 2], 1)
                            dve.wait_ge(pair_read[c % 2], at(reads(c + 2), i, 3))
                            dve.tensor_tensor(merged[:, bass.ds(at(4 * unit, i, 8), 4)].rearrange("p k t -> p (k t)"), gated_a[:],
                                              gated_b[:], ALU.add).then_inc(merged_ready, 1)

            def wide_turns(name, src, turns, ada0=None, ada_per=ADA_DOWN):
                g0, k0 = AT[name], SRC[name]

                def turn(i):
                    for s in range(4):
                        dve.wait_ge(shi_ready, at(k0 + s + 1, i, 4))
                        dve.tensor_tensor(slo[:, s], src[:, at(s, i, 4)], shi[:, s].bitcast(F32), ALU.subtract)\
                           .then_inc(slo_ready, 1)
                        rest(g0 + s + 1, i, 4)
                        if ada0 is not None and s % 2:
                            modulation(ada0 + s // 2, i, ada_per)

                if turns == 1:
                    turn(None)
                else:
                    with dve.Fori(0, turns) as i:
                        turn(i)

            def add_and_norm(n, g, job):
                dve.wait_ge(weights_used, through(g))
                for t in range(T):
                    order.mark(dve.scalar_tensor_tensor(out=res[:, t], in0=res[:, t], scalar=ALPHA,
                                                        in1=ps[:, 4 * t:4 * t + 4].rearrange("p b n -> p (b n)"),
                                                        op0=ALU.mult, op1=ALU.add, accum_out=misc(t)))
                    order.wait()
                    dve.tensor_scalar(misc(2 + t), misc(t), -1.0 / D, None, ALU.mult).then_inc(mean_ready, 1)
                dve.wait_ge(ln_landed, 32 * (n + 1))
                for t in range(T):
                    dve.wait_ge(sq_ready, 2 * n + t + 1)
                    dve.tensor_scalar(var(job + t), misc(4 + t), 1.0 / D, LN_EPS, ALU.mult, ALU.add).then_inc(var_ready, 1)
                    order.mark(dve.scalar_tensor_tensor(out=res[:, t], in0=res[:, t], scalar=misc(2 + t), in1=gamma[:],
                                                        op0=ALU.add, op1=ALU.mult))
                order.wait()
                for t in range(T):
                    dve.wait_ge(rstd_ready, job + t + 1)
                    dve.scalar_tensor_tensor(out=res[:, t], in0=res[:, t], scalar=rstd(job + t), in1=beta[:],
                                             op0=ALU.mult, op1=ALU.add).then_inc(res_ready, 1)

            def rms_rows(squared, job, last=False):
                for t in range(T):
                    dve.wait_ge(sq_ready, squared + t + 1)
                    dve.tensor_scalar(var(job + t), misc(4 + t), 1.0 / D, RMS_EPS, ALU.mult, ALU.add).then_inc(var_ready, 1)
                for t in range(T):
                    dve.wait_ge(rstd_ready, job + t + 1)
                    if last:
                        dve.scalar_tensor_tensor(out=xn[:, t], in0=res[:, t], scalar=rstd(job + t), in1=gamma[:],
                                                 op0=ALU.mult, op1=ALU.mult).then_inc(out_ready, 1)
                    else:
                        dve.tensor_scalar(xn[:, t], res[:, t], rstd(job + t), None, ALU.mult).then_inc(xn_ready, 1)

            def scales(first, norm):
                dve.scalar_tensor_tensor(out=scale_col[:], in0=mod[:, first:first + KT], scalar=1.0,
                                         in1=col[:, COL[norm]:COL[norm] + KT], op0=ALU.add, op1=ALU.mult).then_inc(mod_ready, 1)

            def gate_diagonals(first, n):
                for k in range(KT):
                    ins = dve.tensor_scalar(diag[:, k], ident[:], mod[:, first + k:first + k + 1], None, ALU.mult)
                ins.then_inc(diag_ready, 1)

            def add_gated(g):
                dve.wait_ge(weights_used, through(g))
                for t in range(T):
                    order.mark(dve.tensor_tensor(xn[:, t], ps[:, 4 * t:4 * t + 4].rearrange("p b n -> p (b n)"), gate_row[:],
                                                 ALU.mult))
                    order.wait()
                    dve.tensor_tensor(res[:, t], res[:, t], xn[:, t], ALU.add).then_inc(res_ready, 1)

            wide_turns("out1", merged, 4, 0, ADA_OUT)
            dve.wait_ge(x_landed, 32)
            add_and_norm(0, AT["q_mem"] - 1, 2)
            x_rest(2)
            for g in range(AT["q_mem"], AT["q_mem"] + 4):
                rest(g + 1)

            def m_maxima(h):
                dve.wait_ge(m_scores, h + 1)
                order.mark(dve.tensor_reduce(misc(20 + 2 * (h % 2), 2), ps[:, 4 + h % 2].rearrange("p (t k) -> p t k", t=T), AX_X, ALU.max))
                order.wait()
                dve.tensor_scalar(misc(8 + 2 * (h % 2), 2), misc(20 + 2 * (h % 2), 2), -HD ** -0.5, None, ALU.mult).then_inc(m_max, 1)

            m_maxima(0)
            m_maxima(1)
            for h in range(HEADS_MEM):
                dve.wait_ge(m_exp, 2 * h + 2)
                order.mark(dve.reciprocal(misc(12 + 2 * (h % 2), 2), misc(12 + 2 * (h % 2), 2)))
                order.wait()
                for t in range(T):
                    dve.tensor_scalar(mem_p[:, h % 2, S * t:S * t + S], mem_p[:, h % 2, S * t:S * t + S],
                                      misc(12 + 2 * (h % 2) + t), None, ALU.mult).then_inc(m_p, 1)
                if h + 2 < HEADS_MEM:
                    m_maxima(h + 2)
            dve.wait_ge(m_out, HEADS_MEM)
            wide_turns("o_mem", omT, 1)
            add_and_norm(1, AT["up1"] - 1, 4)
            x_rest(3)
            g0, c0, n0 = AT["up1"], CH["up1"], 4 * ADA_OUT
            with dve.Fori(0, FC) as i:
                for s in range(8):
                    rest(g0 + s + 1, i, 8)
                    if s == 7:
                        dve.wait_ge(weights_used, at(through(g0 + s), i, 16))
                        dve.wait_ge(pair_read[c0 % 2], at(reads(c0), i, 1))
                        dve.tensor_tensor(hid[:, bass.ds(at(0, i, 4), 4)].rearrange("p k t -> p (k t)"), pair(c0 + 1), silu[:],
                                          ALU.mult).then_inc(pair_read[(c0 + 1) % 2], 1)
                    if s % 4 != 3:
                        modulation(n0 + s - s // 4, i, ADA_UP)
            wide_turns("down1", hid, FC, n0 + FC * ADA_UP)
            add_and_norm(2, AT["lstm_gates"] - 1, 6)
            dve.wait_ge(ada_used, ADA)
            order.mark(dve.tensor_tensor(mod[:], mod[:], col[:, COL["b_ada"]:COL["b_ada"] + ADA], ALU.add))
            order.wait()
            scales(KT, "norm1")
            rms_rows(6, 8)
            x_rest(4, modulated)
            rest(AT["lstm_gates"] + 1)
            rest(AT["lstm_gates"] + 2)
            dve.wait_ge(weights_used, through(AT["lstm_gates"]))
            dve.wait_ge(late_landed, 32)
            c = CH["lstm_gates"]
            for d in range(2):
                for n, dst in enumerate((g_in, g_fo)):
                    q = 32 * (2 * d + n)
                    ins = dve.tensor_scalar(dst[:, d], ps[q:q + LH, 2 * (c % 2), 0:S], gbias[q:q + LH, :], None, ALU.add)
            ins.then_inc(pair_read[c % 2], 1)
            dve.wait_ge(pair_read[c % 2], reads(c))
            rest(AT["lstm_gates"] + 3)
            dve.scalar_tensor_tensor(out=g_e[:], in0=g_fo[:], scalar=-1.0, in1=g_fo[:], op0=ALU.mult, op1=ALU.max).then_inc(g_abs, 1)
            rest(AT["lstm_gates"] + 4)
            rest(AT["lstm_gates"] + 5)
            rest(AT["lstm_gates"] + 6)
            dve.wait_ge(g_exp, 1)
            dve.tensor_scalar(g_e[:], g_e[:], 1.0, None, ALU.add).then_inc(g_one, 1)
            for g in range(AT["lstm_k"] + 2, AT["lstm_k"] + 5):
                rest(g)
            rest(AT["lstm_v"] + 1)
            dve.wait_ge(g_ln, 1)
            order.mark(dve.scalar_tensor_tensor(out=g_fo[:], in0=g_fo[:], scalar=0.0, in1=g_e[:], op0=ALU.min, op1=ALU.subtract))
            order.wait()
            ones_row = ones[0:LH, 0:1].to_broadcast([LH, S])
            order.mark(dve.tensor_tensor_scan(g_sum[:, 0], ones_row, g_fo[:, 0], 0.0, ALU.mult, ALU.add))
            order.mark(dve.tensor_tensor_scan(g_sum[:, 1, ::-1], ones_row, g_fo[:, 1, ::-1], 0.0, ALU.mult, ALU.add))
            order.wait()
            order.mark(dve.tensor_tensor(g_a[:], g_in[:], g_sum[:], ALU.subtract))
            order.wait()
            rest(AT["lstm_v"] + 2)
            order.mark(dve.tensor_tensor_scan(g_max[:, 0], g_a[:, 0], g_a[:, 0], -3e38, ALU.max, ALU.max))
            order.mark(dve.tensor_tensor_scan(g_max[:, 1, ::-1], g_a[:, 1, ::-1], g_a[:, 1, ::-1], -3e38, ALU.max, ALU.max))
            order.wait()
            dve.tensor_tensor(g_m[:], g_sum[:], g_max[:], ALU.add).then_inc(g_stab, 1)
            for g in range(AT["lstm_v"] + 3, AT["lstm_o"] + 5):
                rest(g)
            dve.wait_ge(g_cols_T, 1)
            dve.tensor_copy(lcols[:].rearrange("p a n -> p (a n)"), ps[:, 6, 0:32]).then_inc(g_cols, 1)
            for g in range(AT["lstm_o"] + 5, AT["out2"] + 1):
                rest(g)
            dve.wait_ge(g_cols, 1)
            dve.wait_ge(built, 19)
            floors = lcols[:, 1].rearrange("p (n h) -> p n h", h=LH)
            for h in range(LH):
                dve.wait_ge(l_bc, h + 1)
                for d, st, t0, t1, c0 in BLOCKS:
                    n = 8 * d + 4 * st + h
                    ins = dve.tensor_scalar(lx[:, c0:c0 + t1 - t0], ps[:, 0, S * d + t0:S * d + t1], lcols[:, 0, n:n + 1], 0.0,
                                            ALU.subtract, ALU.max)
                ins.then_inc(l_x, 1)
                dve.wait_ge(l_e, h + 1)
                order.mark(dve.tensor_tensor(le[:], le[:], tri[:], ALU.mult))
                order.wait()
                dve.wait_ge(l_st, h + 1)
                for d, st, t0, t1, c0 in BLOCKS:
                    ins = dve.scalar_tensor_tensor(out=lp[:, c0:c0 + t1 - t0], in0=ps[:, 1, S * st + t0:S * st + t1],
                                                   scalar=HD ** -0.5, in1=le[:, c0:c0 + t1 - t0], op0=ALU.mult, op1=ALU.mult)
                ins.then_inc(l_p, 1)
                dve.wait_ge(l_num, h + 1)
                order.mark(dve.tensor_copy(misc(24, 4), ps[:, 4:8, DV]))
                order.wait()
                order.mark(dve.scalar_tensor_tensor(out=misc(28, 4), in0=misc(24, 4), scalar=-1.0, in1=misc(24, 4), op0=ALU.mult,
                                                    op1=ALU.max))
                order.wait()
                order.mark(dve.tensor_tensor(misc(32, 4), misc(28, 4), floors[:, :, h], ALU.max))
                order.wait()
                order.mark(dve.reciprocal(misc(36, 4), misc(32, 4)))
                order.wait()
                for t in range(T):
                    order.mark(dve.tensor_scalar(lh[:, t], ps[:, 4 + t, 0:DV], misc(36 + t), None, ALU.mult))
                order.wait()
                for t in range(T):
                    dve.scalar_tensor_tensor(out=lh[:, t], in0=ps[:, 6 + t, 0:DV], scalar=misc(38 + t), in1=lh[:, t], op0=ALU.mult,
                                             op1=ALU.add).then_inc(l_h, 1)
                dve.wait_ge(l_sq, 2 * h + 2)
                dve.tensor_scalar(var(10 + h, 0, 2), misc(16, 2), 1.0 / DV, RMS_EPS, ALU.mult, ALU.add).then_inc(var_ready, 1)
                dve.wait_ge(rstd_ready, 11 + h)
                for t in range(T):
                    dve.tensor_scalar(lh[:, t], lh[:, t], rstd(10 + h, t), None, ALU.mult).then_inc(l_hn, 1)
                dve.wait_ge(l_hT, h + 1)
                for v in range(2):
                    k = 2 * h + v
                    dve.scalar_tensor_tensor(out=mixT[:, 8 + k], in0=ps[:, 0, S * v:S * v + S],
                                             scalar=col[:, COL["norm_m"] + k:COL["norm_m"] + k + 1], in1=so[:, k], op0=ALU.mult,
                                             op1=ALU.mult).then_inc(mix_m, 1)
            gate_diagonals(2 * KT, 0)
            dve.wait_ge(mix_f, LH)
            wide_turns("out2", mixT, 4)
            dve.wait_ge(gate_ready, 1)
            add_gated(AT["up2"] - 1)
            scales(4 * KT, "norm2")
            rms_rows(8, 14)
            dve.wait_ge(xn_ready, 4)
            x_rest(5, modulated)
            dve.memset(misc(40), 0.0).then_inc(conv_done, 1)
            g0, c0 = AT["up2"], CH["up2"]

            def side_taps(q, side, i):
                if side == 0:
                    dve.wait_ge(conv_mid, at(q + 1, i, 2))
                else:
                    order.wait()
                bank = pair(c0 + q)
                to, fro = (1, 0) if side == 0 else (0, 1)
                for m in range(4):
                    tap = at(COL["w_conv"] + 4 * FT * side + FT * q + m, i, 4)
                    ins = dve.scalar_tensor_tensor(
                        out=conv[:, q, S * m + to:S * m + to + S - 1], in0=bank[:, S * m + fro:S * m + fro + S - 1],
                        scalar=col[:, bass.ds(tap, 1)], in1=conv[:, q, S * m + to:S * m + to + S - 1], op0=ALU.mult, op1=ALU.add)
                    if side == 0:
                        order.mark(ins)
                if side == 1:
                    ins.then_inc(pair_read[(c0 + q) % 2], 1)

            def beside(s, i):
                if s % 4 < 2:
                    side_taps(s // 4, s % 4, i)
                if s == 6:
                    dve.wait_ge(silu_ready, at(1, i, 1))
                    dve.wait_ge(pair_read[(c0 + 1) % 2], at(reads(c0 + 1), i, 1))
                    dve.tensor_tensor(hid[:, bass.ds(at(0, i, 4), 4)].rearrange("p k t -> p (k t)"), conv[:, 1], silu[:],
                                      ALU.mult).then_inc(conv_done, 1)

            for s in range(4):
                rest(g0 + s + 1)
            with dve.Fori(0, FC - 1) as i:
                order.enter(i, 8)
                for s in range(8):
                    rest(g0 + 4 + s + 1, i, 8)
                    beside(s, i)
                order.leave(FC - 1)
            for s in range(4):
                rest(AT["down2"] - 4 + s + 1)
                beside(s, FC - 1)
            for s in range(4, 8):
                beside(s, FC - 1)
            gate_diagonals(5 * KT, 1)
            g0, k0 = AT["down2"], SRC["down2"]
            with dve.Fori(0, FC - 1) as i:
                for s in range(4):
                    dve.wait_ge(shi_ready, at(k0 + s + 1, i, 4))
                    dve.tensor_tensor(slo[:, s], hid[:, at(s, i, 4)], shi[:, s].bitcast(F32), ALU.subtract).then_inc(slo_ready, 1)
                    rest(g0 + s + 1, i, 4)
            for s in range(FT - 4, FT):
                dve.wait_ge(shi_ready, k0 + s + 1)
                dve.tensor_tensor(slo[:, s % 4], hid[:, s], shi[:, s % 4].bitcast(F32), ALU.subtract).then_inc(slo_ready, 1)
                rest(g0 + s + 1)
            dve.wait_ge(gate_ready, 2)
            add_gated(G - 1)
            dve.wait_ge(ln_landed, 32 * 3 + 16)
            rms_rows(10, 16, last=True)

        @block.tensor
        def _(pe):
            def transpose_rows(n, src):
                for b in range(8):
                    for f in range(2):
                        for t in range(T):
                            k = 2 * b + f
                            ins = pe.transpose(ps[:, b, S * f + P * t:S * f + P * t + P], src[:, t, P * k:P * k + P], ident[:])
                    ins.then_inc(xT_done, 1)

            def bank_pair(c, i=None, per=0):
                if c >= 2:
                    pe.wait_ge(pair_read[c % 2], at(c // 2, i, per))

            def product(g, half, c, form, left, k0, ks, width, first, last, i=None, per=0, fresh=None):
                h = 2 * g + half
                if fresh is not None:
                    pe.wait_ge(xlo_ready, 8 * fresh + max(4, (k0 + ks + 1) // 2))
                pe.wait_ge(lo_ready, at(h + 1, i, 2 * per))
                hi, lo = (w[:, h % 4, 0:ks * width].rearrange("p (k n) -> p k n", k=ks) for w in (whi, wlo))
                lhi, llo = left
                for k in range(ks):
                    kt = k0 + k
                    begins, ends = first and k == 0, last and k == ks - 1
                    for m in range(width // P if form == "T" else T):
                        for n, (w, a) in enumerate(((hi, lhi), (hi, llo), (lo, lhi))):
                            if form == "T":
                                o = ps[:, 2 * (c % 2) + m // 2, S * (m % 2):S * (m % 2) + S]
                                ins = pe.matmul(o, w[:, k, P * m:P * m + P], a[:, kt], start=begins and n == 0 and m % 2 == 0,
                                                stop=ends and n == 2, skip_group_check=True)
                            else:
                                o = ps[:, 2 * (c % 2) + m, 0:width]
                                ins = pe.matmul(o, a[:, kt, P * m:P * m + P], w[:, k, :], start=begins and n == 0,
                                                stop=ends and n == 2, skip_group_check=True)
                ins.then_inc(weights_used, 1)

            def chunk(g0, c, form, left=(xhi, xlo), tiles=4, k0=0, i=None, per=0, chunks=0, fresh=None):
                bank_pair(c, i, chunks)
                for s in range(tiles):
                    for half in range(2):
                        product(g0 + s, half, c, form, left, k0 + 4 * s + 2 * half, 2, 512, s == 0 and half == 0,
                                s == tiles - 1 and half == 1, i, per, fresh)

            def wide_open():
                for b in range(8):
                    pe.matmul(ps[:, b], zeros[:, 0:P], zeros[:], start=True, stop=False, skip_group_check=True)

            def wide_tile(g, k, s, i=None):
                for half in range(2):
                    h = 2 * g + half
                    pe.wait_ge(lo_ready, at(h + 1, i, 8))
                    if half == 0:
                        pe.wait_ge(slo_ready, at(k + 1, i, 4))
                    for t in range(T):
                        for a, w in ((shi, whi), (shi, wlo), (slo, whi)):
                            for n in range(2):
                                ins = pe.matmul(ps[:, 4 * t + 2 * half + n], a[:, s, P * t:P * t + P],
                                                w[:, h % 4, 512 * n:512 * n + 512], start=False, stop=False, skip_group_check=True)
                    ins.then_inc(weights_used, 1)

            def wide(name, turns):
                wide_open()
                g0, k0 = AT[name], SRC[name]
                if turns == 1:
                    for s in range(4):
                        wide_tile(g0 + s, k0 + s, s)
                else:
                    with pe.Fori(0, turns) as i:
                        for s in range(4):
                            wide_tile(g0 + s, k0 + s, s, i)

            pe.wait_ge(built, 6)
            pe.wait_ge(mem_landed, 16)
            transpose_rows(0, mem_nat)
            chunk(AT["k_mem"], CH["k_mem"], "T", fresh=0)
            chunk(AT["v_mem"], CH["v_mem"], "N")
            pe.wait_ge(x_landed, 16)
            for c in (CH["k_mem"], CH["v_mem"]):
                pe.wait_ge(pair_read[c % 2], reads(c))
            transpose_rows(1, res)
            g, c = AT["latent"], CH["latent"]
            for n in range(6):
                product(g + n // 2, n % 2, c, "N", (xhi, xlo), 3 * n, min(3, KT - 3 * n), LATENT + IDX_DIM + IDX_HEADS, n == 0,
                        n == 5, fresh=1)
            g, c = AT["q_idx"], CH["q_idx"]
            bank_pair(c)
            for s in range(4):
                for half in range(2):
                    product(g + s, half, c, "T", (xhi, xlo), 4 * s + 2 * half, 2, 512, s == 0 and half == 0, s == 3 and half == 1)
                if s == 2:
                    pe.wait_ge(ck_ready, 2)
                    for k in range(2):
                        for t in range(T):
                            ins = pe.transpose(ps[:, 4, S * k + P * t:S * k + P * t + P], ckv[:, t, P * k:P * k + P], ident[:])
                    ins.then_inc(small_T, 1)
                    pe.wait_ge(kn_ready, 4)
                    for t in range(T):
                        ins = pe.transpose(ps[:, 5, P * t:P * t + P], kn[:, t], ident[:])
                    ins.then_inc(small_T, 1)
            chunk(g + 4, c + 1, "T")
            g, c = AT["v_moba"], CH["v_moba"]
            pe.wait_ge(cklo_ready, 1)
            pe.wait_ge(ki_ready, 1)
            for s in range(8):
                if s % 4 == 0:
                    bank_pair(c + s // 4)
                for half in range(2):
                    h = 2 * s + half
                    pe.wait_ge(pair_read[(CH["q_idx"] + h // 8) % 2], reads(CH["q_idx"] + h // 8))
                    if h >= 4:
                        pe.wait_ge(idx_relu, h - 3)
                    r0 = IDX_DIM * (h % 2)
                    for t in range(T):
                        ins = pe.matmul(ps[:, 4 + h % 4, S * t:S * t + S], qi[r0:r0 + IDX_DIM, h // 2, P * t:P * t + P],
                                        kiT[r0:r0 + IDX_DIM, :], start=True, stop=True, skip_group_check=True)
                    ins.then_inc(idx_done, 1)
                    product(g + s, half, c + s // 4, "N", (xhi, xlo), 4 * (s % 4) + 2 * half, 2, 512, s % 4 == 0 and half == 0,
                            s % 4 == 3 and half == 1)
            for name, form in (("w_uk", "T"), ("w_uv", "N")):
                for half in range(2):
                    bank_pair(CH[name] + half)
                    product(AT[name], half, CH[name] + half, form, (ckhi, cklo), 0, 2, 512, True, True)
            with pe.Fori(0, 3) as i:
                for q in range(2):
                    chunk(AT["qk"] + 4 * q, CH["qk"] + q, "T", i=i, per=8, chunks=1)

            pe.wait_ge(idx_relu, IDX_HEADS)
            g0, c0 = AT["gate_a"], CH["gate_a"]
            with pe.Fori(0, 2) as i:
                for q in range(4):
                    c = c0 + q // 2
                    if q % 2 == 0:
                        bank_pair(c, i, 1)
                    for n in range(4):
                        product(g0 + 2 * q + n // 2, n % 2, c, "T", (xhi, xlo), 8 * (q % 2) + 2 * n, 2, 512, q % 2 == 0 and n == 0,
                                q % 2 == 1 and n == 3, i, 8)
                        if n == 0:
                            pe.wait_ge(qv_ready, at(4 * q + 4, i, 16))
                            pe.wait_ge(att_free, at(2 * q + 1, i, 8))
                            for j, k0 in enumerate((24, 16)):
                                key = qk[:, at(k0 + q, i, 4)]
                                pe.matmul(ps[:, 4 + j, 0:128], qs[:, j, 0:128], key[:, 0:128], start=True, stop=True,
                                          skip_group_check=True)
                                pe.matmul(ps[:, 4 + j, 128:384], qs[:, j, 128:256], key, start=True, stop=True,
                                          skip_group_check=True).then_inc(att_scores, 1)
                        if n == 2:
                            for j in range(2):
                                pe.wait_ge(att_p, at(4 * q + 2 * j + 2, i, 16))
                                for b in range(3):
                                    ins = pe.transpose(ps[:, 6 + j, 128 * b:128 * b + 128], att_e[:, j, 128 * b:128 * b + 128],
                                                       ident[:])
                                ins.then_inc(att_T, 1)
                        if n == 3:
                            for j in range(2):
                                pe.wait_ge(att_pT_ready, at(2 * q + j + 1, i, 8))
                                pe.matmul(ps[:, 4 + j, 0:S], vs[:, j, 0], att_pT[:, j, 0:256], start=True, stop=False,
                                          skip_group_check=True)
                                pe.matmul(ps[:, 4 + j, P:S], vs[:, j, 1], att_pT[:, j, 256:384], start=False, stop=True,
                                          skip_group_check=True).then_inc(att_o, 1)

            pe.wait_ge(att_free, 1 + 2 * HEADS)
            g0, c0 = AT["gates"], CH["gates"]
            with pe.Fori(0, 2) as i:
                for unit in range(2):
                    g, c = g0 + 8 * unit, c0 + 3 * unit
                    chunk(g, c, "T", (ohi, olo), 2, 0, i, 16, 3)
                    chunk(g + 2, c + 1, "T", i=i, per=16, chunks=3)
                    chunk(g + 6, c + 2, "T", (ohi, olo), 2, 8, i, 16, 3)
            for c in (c0 + 10, c0 + 11):
                pe.wait_ge(pair_read[c % 2], reads(c))
            wide("out1", 4)
            pe.wait_ge(res_ready, 2)
            transpose_rows(2, res)
            chunk(AT["q_mem"], CH["q_mem"], "T", fresh=2)

            def m_score(h):
                for t in range(T):
                    ins = pe.matmul(ps[:, 4 + h % 2, S * t:S * t + S], qmT[:, h, P * t:P * t + P], kmT[:, h], start=True, stop=True,
                                    skip_group_check=True)
                ins.then_inc(m_scores, 1)

            c = CH["q_mem"]
            pe.wait_ge(pair_read[c % 2], reads(c))
            m_score(0)
            m_score(1)
            for h in range(HEADS_MEM):
                pe.wait_ge(m_p, 2 * h + 2)
                for k in range(2):
                    for t in range(T):
                        ins = pe.transpose(ps[:, 6 + h % 2, S * k + P * t:S * k + P * t + P],
                                           mem_p[:, h % 2, S * t + P * k:S * t + P * k + P], ident[:])
                ins.then_inc(m_T, 1)
                pe.wait_ge(m_pT, h + 1)
                for k in range(2):
                    ins = pe.matmul(ps[:, 4 + h % 2, 0:S], vm[:, k, HD * h:HD * h + HD], mem_pT[:, h % 2, S * k:S * k + S],
                                    start=k == 0, stop=k == 1, skip_group_check=True)
                ins.then_inc(m_o, 1)
                if h + 2 < HEADS_MEM:
                    pe.wait_ge(m_out, h + 1)
                    m_score(h + 2)
            pe.wait_ge(m_out, HEADS_MEM)
            wide("o_mem", 1)
            pe.wait_ge(res_ready, 4)
            transpose_rows(3, res)
            with pe.Fori(0, FC) as i:
                for q in range(2):
                    chunk(AT["up1"] + 4 * q, CH["up1"] + q, "T", i=i, per=8, chunks=1, fresh=3 if q == 0 else None)
            for c in (CH["up1"] + 2 * FC - 2, CH["up1"] + 2 * FC - 1):
                pe.wait_ge(pair_read[c % 2], reads(c))
            wide("down1", FC)
            pe.wait_ge(xn_ready, 2)
            transpose_rows(4, xn)
            g, c = AT["lstm_gates"], CH["lstm_gates"]
            for half in range(2):
                product(g, half, c, "T", (xhi, xlo), 8 * half, 8, P, half == 0, half == 1, fresh=4)
            chunk(AT["lstm_q"], CH["lstm_q"], "T")
            chunk(AT["lstm_k"], CH["lstm_k"], "T")
            chunk(AT["lstm_v"], CH["lstm_v"], "N")
            chunk(AT["lstm_v"] + 4, CH["lstm_v"] + 1, "N")
            pe.wait_ge(g_floor, 1)
            for n, src in enumerate((g_a, g_m)):
                for d in range(2):
                    for t in range(T):
                        q = 16 * n + 8 * d + 4 * t
                        ins = pe.transpose(ps[:, 6, q:q + LH], src[:, d, P * t:P * t + P], ident[0:LH, 0:LH])
            ins.then_inc(g_cols_T, 1)
            for q in range(2):
                chunk(AT["lstm_o"] + 4 * q, CH["lstm_o"] + q, "T")
            for q in range(2):
                chunk(AT["fourier"] + 4 * q, CH["fourier"] + q, "N")
            for c in (CH["fourier"], CH["fourier"] + 1):
                pe.wait_ge(pair_read[c % 2], reads(c))
            pe.wait_ge(g_cols, 1)
            pe.wait_ge(built, 19)
            pe.wait_ge(late_landed, 32)
            for h in range(LH):
                if h >= 1:
                    pe.wait_ge(mix_m, 2 * h)
                pe.matmul(ps[:, 0], sel[:, h], g_max[:].rearrange("h d t -> h (d t)"), start=True, stop=True,
                          skip_group_check=True).then_inc(l_bc, 1)
                for st in range(T):
                    ins = pe.matmul(ps[:, 1, S * st:S * st + S], lk[:, h, P * st:P * st + P], lq[:, h], start=True, stop=True,
                                    skip_group_check=True)
                ins.then_inc(l_st, 1)
                if h >= 1:
                    pe.wait_ge(mix_f, h)
                for f in range(2):
                    for st in range(T):
                        ins = pe.matmul(ps[:, 2 + f], uf[:, st, S * h + P * f:S * h + P * f + P], dftc[:, st, 0:512], start=st == 0,
                                        stop=st == 1, skip_group_check=True)
                    ins.then_inc(f_first, 1)
                pe.wait_ge(l_p, h + 1)
                for d in range(2):
                    for t in range(T):
                        mine = [b for b in BLOCKS if b[0] == d and b[2] <= P * t < b[3]]
                        for n, (_, st, t0, _, c0) in enumerate(mine):
                            q = c0 + P * t - t0
                            ins = pe.matmul(ps[:, 4 + 2 * d + t, 0:DV + 1], lp[:, q:q + P], lv[:, st, h, 0:DV + 1], start=n == 0,
                                            stop=n == len(mine) - 1, skip_group_check=True)
                ins.then_inc(l_num, 1)
                pe.wait_ge(f_copied, 2 * h + 2)
                for fo in range(2):
                    for n in range(4):
                        fi, part = n // 2, n % 2
                        ins = pe.matmul(ps[:, 2, S * fo:S * fo + S], dftc[:, fi, 512 * part + P * fo:512 * part + P * fo + P],
                                        fa[:, fi, S * part:S * part + S], start=n == 0 and fo == 0, stop=n == 3,
                                        skip_group_check=True)
                ins.then_inc(f_second, 1)
                pe.wait_ge(l_hn, 2 * h + 2)
                for v in range(2):
                    for t in range(T):
                        ins = pe.transpose(ps[:, 0, S * v + P * t:S * v + P * t + P], lh[:, t, P * v:P * v + P], ident[:])
                ins.then_inc(l_hT, 1)

            def gate_rows(n):
                pe.wait_ge(diag_ready, n + 1)
                for k in range(KT):
                    ins = pe.matmul(ps[:, 4 + k // 4, P * (k % 4):P * (k % 4) + P], ones[:], diag[:, k], start=True, stop=True,
                                    skip_group_check=True)
                ins.then_inc(gate_T, 1)
                pe.wait_ge(gate_ready, n + 1)

            gate_rows(0)
            pe.wait_ge(mix_f, LH)
            wide("out2", 4)
            pe.wait_ge(xn_ready, 4)
            transpose_rows(5, xn)
            with pe.Fori(0, FC) as i:
                for q in range(2):
                    chunk(AT["up2"] + 4 * q, CH["up2"] + q, "T", i=i, per=8, chunks=1, fresh=5 if q == 0 else None)
            for c in (CH["up2"] + 2 * FC - 2, CH["up2"] + 2 * FC - 1):
                pe.wait_ge(pair_read[c % 2], reads(c))
            gate_rows(1)
            wide("down2", FC)


def tiles_by_chunk(w):
    k, n = w.shape
    return w.reshape(k // 512, 4, P, n // 512, 512).transpose(3, 0, 2, 1, 4).reshape(n // 512, k // 512, P, D)


def tiles_of_latent(w):
    return w.reshape(2, P, 2, 512).transpose(1, 2, 0, 3).reshape(1, P, D)


def tile_of_gates(w):
    out = np.zeros((P, KT, 4, 32), w.dtype)
    out[..., 0:LH] = w.reshape(KT, P, 4, LH).transpose(1, 0, 2, 3)
    return out.reshape(1, P, D)


def weight_stream(a):
    flat = lambda w: w.reshape(-1, P, D)
    w_in, w_in2 = a["w_in"][0], a["w_in_2"]
    kv = tiles_by_chunk(a["w_kv_mem"][0])
    o = {}
    n = 0
    for name, width in (("q_dsa", 1024), ("c_kv", 256), ("q_idx", 1024), ("k_idx", 80), ("q_m", 1024), ("k_m", 1024),
                        ("v_m", 1024), ("ga", D), ("gb", D)):
        o[name] = w_in[:, n:n + width]
        n += width
    side = [tiles_by_chunk(w) for w in (a["w_o_dsa"][0], o["gb"], a["w_o_moba"][0])]
    gates = np.concatenate(side, axis=1)
    up1 = tiles_by_chunk(a["w_ffn_in"][0])
    up1 = np.concatenate([up1[:FC], up1[FC:]], axis=1)
    up2 = tiles_by_chunk(a["w_up_2"])
    up2 = np.concatenate([up2[:FC], up2[FC:]], axis=1)
    few = LATENT + IDX_DIM + IDX_HEADS
    latent = np.zeros((6, P, 1024), w_in.dtype)
    rows = np.concatenate([o["c_kv"], o["k_idx"]], axis=1).reshape(KT, P, few)
    for k in range(KT):
        latent[k // 3, :, few * (k % 3):few * (k % 3) + few] = rows[k]
    latent = latent.reshape(3, 2, P, 1024).transpose(0, 2, 1, 3)
    parts = [
        flat(kv), flat(latent), flat(tiles_by_chunk(o["q_idx"])), flat(tiles_by_chunk(o["v_m"])),
        tiles_of_latent(a["w_uk"][0].transpose(2, 0, 1).reshape(LATENT, 1024)),
        tiles_of_latent(a["w_uv"][0].transpose(1, 0, 2).reshape(LATENT, 1024)),
        flat(tiles_by_chunk(o["q_dsa"])), flat(tiles_by_chunk(o["q_m"])), flat(tiles_by_chunk(o["k_m"])),
        flat(tiles_by_chunk(o["ga"])), flat(gates), flat(a["w_out"][0]), flat(tiles_by_chunk(a["w_q_mem"][0])), flat(a["w_o_mem"][0]), flat(up1),
        flat(a["w_ffn_out"][0]), tile_of_gates(w_in2[:, 4096:4112]), flat(tiles_by_chunk(w_in2[:, 1024:4096])),
        flat(tiles_by_chunk(w_in2[:, 0:1024])), flat(a["w_out_2"]), flat(up2), flat(a["w_down_2"]),
    ]
    return np.concatenate(parts, axis=0)


def kernel(**inputs):
    import concourse.bacc as bacc
    from concourse.bass_utils import run_bass_kernel_spmd

    a = {k: np.asarray(v) for k, v in inputs.items()}

    def columns(v):
        return v.reshape(-1, P).T

    slopes = np.array([2.0 ** (-8.0 * (n + 1) / HEADS) for n in range(HEADS)], np.float32)
    turn = np.arange(S)
    angle = 2 * np.pi * (np.outer(turn, turn) % S) / S
    root = S ** 0.5
    wave = np.concatenate([np.cos(angle), np.sin(angle), -np.sin(angle)], axis=1) / root
    gate_bias = np.zeros((4, 32, 1), np.float32)
    gate_bias[:, 0:LH, 0] = a["b_gates_2"].reshape(4, LH)
    gate_bias = gate_bias.reshape(P, 1)
    arrays = {
        "x": a["x"][0],
        "mem": a["mem"][0],
        "stream": weight_stream(a),
        "w_ada": np.ascontiguousarray(a["w_ada_2"].T).reshape(ADA, P, D),
        "cols": np.concatenate(
            [columns(a["b_gate"][0]), columns(a["b_ada_2"]), columns(a["norm1_w_2"]), columns(a["norm2_w_2"]),
             columns(a["mlstm_norm_w_2"]), columns(a["w_conv_2"]), columns(a["b_conv_2"]),
             np.broadcast_to(slopes, (P, HEADS))], axis=1),
        "rows": np.concatenate([a["kv_norm_g"], a["idx_k_norm_g"], a["idx_k_norm_b"]], axis=1),
        "ln_g": a["ln_g"][0],
        "ln_b": a["ln_b"][0],
        "norm_f": a["norm_f_w_2"].reshape(1, D),
        "c_row": a["c_2"],
        "gate_bias": gate_bias,
        "dft": wave.astype(np.float32),
    }
    arrays = {k: np.ascontiguousarray(v) for k, v in arrays.items()}
    assert arrays["stream"].shape[0] == G, (arrays["stream"].shape, G)
    nc = bacc.Bacc("TRN2", target_bir_lowering=False, num_devices=1)
    args = [nc.dram_tensor(f"in_{k}", v.shape, F32, kind="ExternalInput").ap() for k, v in arrays.items()]
    out = nc.dram_tensor("out_0", (S, D), F32, kind="ExternalOutput").ap()
    two_blocks(nc, *args, out)
    r = run_bass_kernel_spmd(nc, [{f"in_{k}": v for k, v in arrays.items()}], core_ids=[0])
    return r.results[0]["out_0"].reshape(1, S, D)
```

```python
from contextlib import ExitStack

import numpy as np
import concourse.bass as bass
from concourse import mybir

F32 = mybir.dt.float32
F32R = mybir.dt.float32r
BF16 = mybir.dt.bfloat16
I32 = mybir.dt.int32
ALU = mybir.AluOpType
ACT = mybir.ActivationFunctionType
AX_X = mybir.AxisListType.X

P = 128
S = 256
T = S // P
D = 2048
KT = D // P
HD = 128
HEADS = 8
HEADS_MEM = 4
LATENT = 256
IDX_HEADS = 16
IDX_DIM = 64
TOPK = min(256, S // 4)
FF = 5632
FT = FF // P
FC = FF // 512
LH = 4
DV = 256
ADA = 6 * D // P
ALPHA = 2.0 ** 0.25
LN_EPS = 1e-5
RMS_EPS = 1e-6
OUT_OF_SIGHT = -1e30
TAKEN = -3e38

TILES = [("k_mem", 4), ("v_mem", 4), ("latent", 3), ("q_idx", 8), ("v_moba", 8), ("w_uk", 1), ("w_uv", 1),
         ("qk", 24), ("gate_a", 16), ("gates", 32), ("out1", 16), ("q_mem", 4), ("o_mem", 4), ("up1", 8 * FC), ("down1", FT),
         ("lstm_gates", 1), ("lstm_q", 4), ("lstm_k", 4), ("lstm_v", 8), ("lstm_o", 8), ("fourier", 8), ("out2", 16),
         ("up2", 8 * FC), ("down2", FT)]
CHUNKS = [("k_mem", 1), ("v_mem", 1), ("latent", 1), ("q_idx", 2), ("v_moba", 2), ("w_uk", 2), ("w_uv", 2),
          ("qk", 6), ("gate_a", 4), ("gates", 12), ("q_mem", 1), ("up1", 2 * FC), ("lstm_gates", 1), ("lstm_q", 1), ("lstm_k", 1),
          ("lstm_v", 2), ("lstm_o", 2), ("fourier", 2), ("up2", 2 * FC)]
WIDE = [("out1", 16), ("o_mem", 4), ("down1", FT), ("out2", 16), ("down2", FT)]
COLS = [("b_gate", 2 * KT), ("b_ada", ADA), ("norm1", KT), ("norm2", KT), ("norm_m", 8), ("w_conv", 3 * 2 * FT),
        ("b_conv", 2 * FT), ("slope", HEADS)]


def starts(parts):
    found, n = {}, 0
    for name, size in parts:
        found[name] = n
        n += size
    return found, n


AT, G = starts(TILES)
CH, _ = starts(CHUNKS)
SRC, _ = starts(WIDE)
COL, NCOL = starts(COLS)
TURNS_DONE = [(SRC[name] + size) // 4 for name, size in WIDE]
ADA_OUT, ADA_UP, ADA_DOWN = 2, 6, 2
assert 4 * ADA_OUT + FC * ADA_UP + (FT // 4) * ADA_DOWN == ADA
BLOCKS = [(0, 0, 0, 256, 0), (0, 1, 128, 256, 256), (1, 0, 0, 128, 384), (1, 1, 0, 256, 512)]


class Order:

    def __init__(self, eng, sem):
        self.eng, self.sem, self.n, self.i, self.per = eng, sem, 0, None, 0

    def mark(self, ins):
        ins.then_inc(self.sem, 1)
        self.n += 1

    def wait(self):
        self.eng.wait_ge(self.sem, at(self.n, self.i, self.per))

    def enter(self, i, per):
        self.i, self.per, self.n0 = i, per, self.n

    def leave(self, turns):
        assert self.n - self.n0 == self.per, (self.n - self.n0, self.per)
        self.i, self.n = None, self.n0 + turns * self.per


def at(first, i=None, per=0):
    return first if i is None else i * per + first


def two_blocks(nc, x, mem, stream, w_ada, cols, rows, ln_g, ln_b, norm_f, c_row, gate_bias, dft, out):
    with ExitStack() as ctx:
        def sem(name):
            return ctx.enter_context(nc.semaphore(name))

        place = [16512]

        def sb(name, shape, dt=F32, offset=None):
            here = place[0] if offset is None else offset
            if offset is None:
                size = int(np.prod(shape[1:])) * (2 if dt == BF16 else 4)
                place[0] += -(-size // 32) * 32
            return nc.alloc_sbuf_tensor_at(name, shape, dt, offset=here)

        raw = [sb(f"raw{s}", [P, D]) for s in range(4)]
        whi = sb("whi", [P, 4, 1024], F32R)
        wlo = sb("wlo", [P, 4, 1024], F32R)
        at_xhi = place[0]
        xhi = sb("xhi", [P, KT, S], F32R)
        at_xlo = place[0]
        xlo = sb("xlo", [P, KT, S], F32R)
        at_res = place[0]
        res = sb("res", [P, T, D])
        ident = sb("ident", [P, P])
        ones = sb("ones", [P, P])
        zeros = sb("zeros", [P, 512], BF16)
        dist = sb("dist", [P, 384])
        causal = sb("causal", [P, 384])
        chosen = sb("chosen", [P, 384])
        col = sb("col", [P, NCOL])
        row = sb("row", [P, LATENT + 2 * IDX_DIM])
        mod = sb("mod", [P, ADA])
        scale_col = sb("scale_col", [P, KT])
        expo = sb("expo", [P, 4])
        small = sb("small", [P, 128])
        at_pool = place[0]
        at_pool2 = at_pool + 49152
        shi = sb("shi", [P, 4, S], F32R, at_xhi)
        slo = sb("slo", [P, 4, S], F32R, at_xhi + 4096)
        gate_row = sb("gate_row", [P, D], F32, at_xhi + 8192)
        gamma = sb("gamma", [P, D], F32, at_xlo)
        beta = sb("beta", [P, D], F32, at_xlo + 8192)
        qk = sb("qk", [P, 32, S], F32, at_pool)
        ohi = sb("ohi", [P, 16, S], F32R, at_pool)
        olo = sb("olo", [P, 16, S], F32R, at_pool + 16384)
        vall = sb("vall", [P, T, D], F32, at_pool + 32768)
        mem_nat = sb("mem_nat", [P, T, D], F32, at_pool + 32768)
        merged = sb("merged", [P, KT, S], F32, at_pool + 32768)
        ckv = sb("ckv", [P, T, LATENT], F32, at_pool)
        kw = sb("kw", [P, T, IDX_DIM + IDX_HEADS], F32, at_pool + 2048)
        kn = sb("kn", [P, T, 2 * IDX_DIM], F32, at_pool + 3072)
        kc = sb("kc", [P, T, IDX_DIM], F32, at_pool + 4096)
        ksq = sb("ksq", [P, T, IDX_DIM], F32, at_pool + 4608)
        qi = sb("qi", [P, 8, S], F32, at_res)
        idx_r = sb("idx_r", [P, 2, 512], F32, at_res + 8192)
        score = sb("score", [P, T, S], F32, at_res + 12288)
        best8 = sb("best8", [P, T, 8], F32, at_res + 14336)
        wi = sb("wi", [P, T, IDX_HEADS], F32, at_res + 14400)
        kiT = sb("kiT", [P, S], F32, at_res + 14592)
        qs = sb("qs", [P, 2, S], F32, at_res)
        vs = sb("vs", [P, 2, T, HD], F32, at_res + 2048)
        att_ab = sb("att_ab", [P, 2, 384], F32, at_res + 4096)
        att_s = sb("att_s", [P, 2, 384], F32, at_res + 7168)
        att_e = sb("att_e", [P, 2, 384], F32, at_res + 10240)
        att_pT = sb("att_pT", [P, 2, 384], F32, at_res + 13312)
        sig = sb("sig", [P, 2, 1024], F32, at_res)
        gated_a = sb("gated_a", [P, 1024], F32, at_res + 8192)
        gated_b = sb("gated_b", [P, 1024], F32, at_res + 12288)
        place[0] = at_pool2
        kmT = sb("kmT", [P, HEADS_MEM, S])
        vm = sb("vm", [P, T, HEADS_MEM * HD])
        cb = sb("cb", [P, D])
        ada = [sb(f"ada{s}", [P, D]) for s in range(2)]
        gate_a = sb("gate_a", [P, KT, S], F32, place[0] - 2 * 4 * D)
        at_end = place[0]
        assert at_end <= 229344, at_end
        ckhi = sb("ckhi", [P, 2, S], F32R, at_pool + 8192)
        cklo = sb("cklo", [P, 2, S], F32R, at_pool + 10240)
        qmT = sb("qmT", [P, HEADS_MEM, S], F32, at_pool)
        omT = sb("omT", [P, HEADS_MEM, S], F32, at_pool + 4096)
        mem_p = sb("mem_p", [P, HEADS_MEM, T * S], F32, at_pool + 8192)
        mem_pT = sb("mem_pT", [P, 2, T * S], F32, at_pool + 16384)
        hid = sb("hid", [P, FT, S], F32, at_pool)
        silu = sb("silu", [P, 1024], F32, at_pool2)
        conv = sb("conv", [P, 2, 1024], F32, at_pool2 + 4096)
        diags = [sb("diag1", [P, KT, P], F32, at_pool2), sb("diag2", [P, KT, P], F32, at_pool2 + 12288)]
        gates_in_rows = [gate_row, sb("gate_row2", [P, D], F32, at_pool2 + 20480)]
        xn = sb("xn", [P, T, D], F32, at_pool)
        modulated = sb("modulated", [P, 2, 512], F32, at_pool + 16384)
        so = sb("so", [P, 8, S], F32, at_pool + 16384)
        lq = sb("lq", [P, LH, S], F32, at_pool + 24576)
        lk = sb("lk", [P, LH, S], F32, at_pool + 28672)
        mixT = sb("mixT", [P, KT, S], F32, at_pool + 32768)
        uf = sb("uf", [P, T, 1024], F32, at_pool2)
        lv = sb("lv", [P, T, LH, DV + 2], F32, at_pool2 + 8192)
        dftc = sb("dftc", [P, T, 768], F32, at_pool2 + 16448)
        fa = [sb(f"fa{h}", [P, 2, S], F32, at_pool2 + 22592 + 2048 * h if h < 2 else at_end + 2048 * (h - 2)) for h in range(4)]
        assert at_end + 4096 <= 229344
        tri = sb("tri", [P, 768], F32, at_pool2 + 26688)
        sel = sb("sel", [LH, LH, P], F32, at_pool2 + 29760)
        lcols = sb("lcols", [P, 2, 16], F32, at_pool2 + 31808)
        gbias = sb("gbias", [P, 1], F32, at_pool2 + 31936)
        lx = sb("lx", [P, 768], F32, at_pool)
        le = sb("le", [P, 768], F32, at_pool + 3072)
        lp = sb("lp", [P, 768], F32, at_pool + 6144)
        lh = sb("lh", [P, T, DV], F32, at_pool + 9216)
        fy = sb("fy", [P, 2, 2 * S], F32, at_pool)
        l_squares = sb("l_squares", [P, DV], F32, at_pool + 13312)
        g_in = sb("g_in", [LH, 2, S], F32, at_pool)
        g_fo = sb("g_fo", [LH, 2, S], F32, at_pool + 2048)
        g_e = sb("g_e", [LH, 2, S], F32, at_pool + 4096)
        g_sum = sb("g_sum", [LH, 2, S], F32, at_pool + 6144)
        g_a = sb("g_a", [LH, 2, S], F32, at_pool + 8192)
        g_max = sb("g_max", [LH, 2, S], F32, at_pool + 11264)
        g_m = sb("g_m", [LH, 2, S], F32, at_pool + 13312)
        iota_i = sb("iota_i", [P, 384], I32, at_pool)

        ps = ctx.enter_context(nc.psum_tensor("ps", [P, 8, 512], F32))

        def var(n, t=0, w=1):
            return small[:, 2 * n + t:2 * n + t + w]

        def rstd(n, t=0, w=1):
            return small[:, 40 + 2 * n + t:40 + 2 * n + t + w]

        def misc(n, w=1):
            return small[:, 80 + n:80 + n + w]

        raw_landed = [sem(f"raw_landed{s}") for s in range(4)]
        hi_ready = sem("hi_ready")
        lo_ready = sem("lo_ready")
        weights_used = sem("weights_used")
        pair_read = [sem(f"pair_read{p}") for p in range(2)]
        x_landed = sem("x_landed")
        mem_landed = [sem(f"mem_landed{t}") for t in range(T)]
        consts_landed = sem("consts_landed")
        late_landed = sem("late_landed")
        cb_landed = sem("cb_landed")
        cb_ready = sem("cb_ready")
        ln_landed = sem("ln_landed")
        ada_landed = [sem(f"ada_landed{s}") for s in range(2)]
        ada_used = sem("ada_used")
        built = sem("built")
        xT_done = sem("xT_done")
        xhi_ready = sem("xhi_ready")
        xlo_ready = sem("xlo_ready")
        shi_ready = sem("shi_ready")
        slo_ready = sem("slo_ready")
        var_ready = sem("var_ready")
        rstd_ready = sem("rstd_ready")
        mean_ready = sem("mean_ready")
        sq_ready = sem("sq_ready")
        res_ready = sem("res_ready")
        xn_ready = sem("xn_ready")
        mod_ready = sem("mod_ready")
        odd_modulated = sem("odd_modulated")
        first_rows_done = sem("first_rows_done")
        ck_squared = sem("ck_squared")
        ck_ready = sem("ck_ready")
        kn_ready = sem("kn_ready")
        small_T = sem("small_T")
        ckhi_ready = sem("ckhi_ready")
        cklo_ready = sem("cklo_ready")
        ki_ready = sem("ki_ready")
        idx_done = sem("idx_done")
        idx_relu = sem("idx_relu")
        idx_added = sem("idx_added")
        qv_ready = sem("qv_ready")
        att_free = sem("att_free")
        att_scores = sem("att_scores")
        att_max = sem("att_max")
        att_exp = sem("att_exp")
        att_p = sem("att_p")
        att_T = sem("att_T")
        att_pT_ready = sem("att_pT_ready")
        att_o = sem("att_o")
        att_ohi = sem("att_ohi")
        sig_ready = sem("sig_ready")
        merged_ready = sem("merged_ready")
        m_scores = sem("m_scores")
        m_max = sem("m_max")
        m_exp = sem("m_exp")
        m_p = sem("m_p")
        m_T = sem("m_T")
        m_pT = sem("m_pT")
        m_o = sem("m_o")
        m_out = sem("m_out")
        conv_mid = sem("conv_mid")
        conv_done = sem("conv_done")
        silu_ready = sem("silu_ready")
        g_abs = sem("g_abs")
        g_exp = sem("g_exp")
        g_one = sem("g_one")
        g_ln = sem("g_ln")
        g_stab = sem("g_stab")
        g_floor = sem("g_floor")
        g_cols_T = sem("g_cols_T")
        g_cols = sem("g_cols")
        l_bc = sem("l_bc")
        l_x = sem("l_x")
        l_e = sem("l_e")
        l_st = sem("l_st")
        l_p = sem("l_p")
        l_num = sem("l_num")
        l_h = sem("l_h")
        l_sq = sem("l_sq")
        l_hn = sem("l_hn")
        l_hT = sem("l_hT")
        mix_m = sem("mix_m")
        f_first = sem("f_first")
        f_copied = sem("f_copied")
        f_second = sem("f_second")
        f_read = sem("f_read")
        mix_f = sem("mix_f")
        diag_ready = sem("diag_ready")
        gate_T = sem("gate_T")
        gate_ready = sem("gate_ready")
        out_ready = sem("out_ready")
        out_landed = sem("out_landed")
        act_order = sem("act_order")
        dve_order = sem("dve_order")

        def through(g, half=2):
            return 2 * g + half

        def pair(c):
            return ps[:, 2 * (c % 2):2 * (c % 2) + 2, :].rearrange("p b n -> p (b n)")

        def reads(c):
            return c // 2 + 1

        block = ctx.enter_context(nc.Block())

        @block.sync
        def _(sp):
            for t in range(T):
                sp.dma_start(mem_nat[:, t], mem[P * t:P * t + P, :]).then_inc(mem_landed[t], 16)
            for s in range(4):
                sp.dma_start(raw[s][:], stream[s]).then_inc(raw_landed[s], 16)
            sp.dma_start(res[:], x.rearrange("(t p) d -> p t d", p=P)).then_inc(x_landed, 16)
            with sp.Fori(0, G // 4 - 1) as i:
                for s in range(4):
                    sp.wait_ge(lo_ready, at(2 * s + 2, i, 8))
                    sp.dma_start(raw[s][:], stream[at(s + 4, i, 4)]).then_inc(raw_landed[s], 16)
            for g in range(G // 4 * 4, G):
                sp.wait_ge(lo_ready, 2 * (g - 4) + 2)
                sp.dma_start(raw[g % 4][:], stream[g]).then_inc(raw_landed[g % 4], 16)
            for n in range(2 * T):
                t, cut = n // 2, slice(D // 2 * (n % 2), D // 2 * (n % 2) + D // 2)
                sp.wait_ge(out_ready, n + 1)
                sp.dma_start(out[t * P:(t + 1) * P, cut], xn[:, t, cut]).then_inc(out_landed, 16)
            sp.wait_ge(out_landed, 16 * 2 * T)

        @block.gpsimd
        def _(pool):
            pool.memset(ident[:], 0.0).then_inc(built, 1)
            pool.memset(ones[:], 1.0).then_inc(built, 1)
            pool.memset(zeros[:], 0.0).then_inc(built, 1)
            pool.memset(expo[:], -0.5).then_inc(built, 1)
            pool.memset(causal[:], 0.0).then_inc(built, 1)
            pool.wait_ge(built, 5)
            pool.affine_select(out=ident[:], in_=ident[:], compare_op=ALU.not_equal, fill=1.0, base=0,
                               pattern=[[-1, P]], channel_multiplier=1).then_inc(built, 1)
            for q0, c0, c1 in ((0, 0, 128), (128, 128, 384)):
                pool.affine_select(out=causal[:, c0:c1], in_=causal[:, c0:c1], compare_op=ALU.is_ge, fill=OUT_OF_SIGHT,
                                   base=q0, pattern=[[-1, c1 - c0]], channel_multiplier=1).then_inc(built, 1)
                pool.iota(iota_i[:, c0:c1], pattern=[[1, c1 - c0]], base=-q0, channel_multiplier=-1).then_inc(built, 1)
            pool.wait_ge(built, 10)
            pool.tensor_copy(dist[:], iota_i[:]).then_inc(built, 1)

            def power(n, w):
                pool.wait_ge(var_ready, n + 1)
                pool.tensor_tensor(rstd(n, 0, w), var(n, 0, w), expo[:, 0:w], ALU.pow).then_inc(rstd_ready, 1)

            power(0, 2)
            power(1, 2)
            pool.wait_ge(merged_ready, 4)
            for n in range(2):
                pool.dma_start(ada[n][:], w_ada[n]).then_inc(ada_landed[n], 16)

            def ada_turns(n0, turns, per):
                with pool.Fori(0, turns) as i:
                    for s in range(per):
                        pool.wait_ge(ada_used, at(n0 + s - 1, i, per))
                        pool.wait_ge(built, 11)
                        pool.dma_start(ada[s % 2][:], w_ada[at(n0 + s, i, per)]).then_inc(ada_landed[s % 2], 16)

            first = 4 * ADA_OUT
            ada_turns(2, first // 2, 2)
            power(2, 1)
            power(3, 1)
            power(4, 1)
            power(5, 1)
            ada_turns(first + 2, (ADA - first - 2) // 2, 2)
            pool.wait_ge(ada_used, ADA)
            pool.dma_start(dftc[:], dft.rearrange("(t p) n -> p t n", p=P)).then_inc(late_landed, 16)
            pool.dma_start(gbias[:], gate_bias).then_inc(late_landed, 16)
            pool.memset(tri[:], 1.0).then_inc(built, 1)
            pool.memset(sel[:], 0.0).then_inc(built, 1)
            pool.memset(lv[:, :, :, DV:DV + 2], 1.0).then_inc(built, 1)
            pool.wait_ge(built, 14)
            for d, st, t0, t1, c0 in BLOCKS:
                sign = 1 if d == 0 else -1
                pool.affine_select(out=tri[:, c0:c0 + t1 - t0], in_=tri[:, c0:c0 + t1 - t0], compare_op=ALU.is_ge,
                                   fill=0.0, base=sign * (t0 - P * st), pattern=[[sign, t1 - t0]],
                                   channel_multiplier=-sign).then_inc(built, 1)
            pool.affine_select(out=sel[:], in_=sel[:], compare_op=ALU.not_equal, fill=1.0, base=0,
                               pattern=[[-1, LH], [0, P]], channel_multiplier=1).then_inc(built, 1)
            def gate_diagonals(n, first):
                gate = mod[:, first:first + KT].rearrange("p (k o) -> p k o", o=1).to_broadcast([P, KT, P])
                pool.affine_select(out=diags[n][:], in_=gate, compare_op=ALU.is_equal, fill=0.0, base=0,
                                   pattern=[[0, KT], [-1, P]], channel_multiplier=1).then_inc(diag_ready, 1)

            for n, w in [(6, 1), (7, 1), (8, 1), (9, 1), (10, 2), (11, 2), (12, 2), (13, 2)]:
                power(n, w)
            pool.wait_ge(f_first, LH)
            gate_diagonals(0, 2 * KT)
            power(14, 1)
            power(15, 1)
            gate_diagonals(1, 5 * KT)
            power(16, 1)
            power(17, 1)

        @block.scalar
        def _(act):
            order = Order(act, act_order)
            act.dma_start(col[:], cols).then_inc(consts_landed, 16)
            act.dma_start(row[:], rows.partition_broadcast(P)).then_inc(consts_landed, 16)

            def params_in_place():
                act.wait_ge(consts_landed, 32)

            def upper(g, i=None, per=0):
                if g >= G:
                    return
                for half in range(2):
                    h = 2 * g + half
                    if half == 0:
                        act.wait_ge(raw_landed[g % 4], at(16 * (g // 4 + 1), i, 4 * per))
                    if h >= 4:
                        act.wait_ge(weights_used, at(h - 3, i, 2 * per))
                    act.activation(whi[:, h % 4], raw[g % 4][:, 1024 * half:1024 * half + 1024], ACT.Copy)\
                       .then_inc(hi_ready, 1)

            def x_upper(n):
                for b in range(8):
                    act.wait_ge(xT_done, 8 * n + b + 1)
                    act.activation(xhi[:, 2 * b:2 * b + 2].rearrange("p k t -> p (k t)"), ps[:, b], ACT.Copy)\
                       .then_inc(xhi_ready, 1)

            def x_upper_modulated(n, shift):
                act.wait_ge(mod_ready, n - 3)
                for b in range(8):
                    if b % 2 == 0:
                        act.wait_ge(xT_done, 8 * n + b + 1)
                        if b >= 2:
                            act.wait_ge(xlo_ready, 8 * n + b - 1)
                        for f in range(2):
                            k = 2 * b + f
                            order.mark(act.activation(modulated[:, 0, S * f:S * f + S], ps[:, b, S * f:S * f + S], ACT.Identity,
                                                      bias=mod[:, shift + k:shift + k + 1], scale=scale_col[:, k:k + 1]))
                        order.wait()
                    else:
                        act.wait_ge(odd_modulated, 4 * (n - 4) + b // 2 + 1)
                    act.activation(xhi[:, 2 * b:2 * b + 2].rearrange("p k t -> p (k t)"), modulated[:, b % 2], ACT.Copy)\
                       .then_inc(xhi_ready, 1)

            def read_out(c, g, dst, func=ACT.Copy, half=2, i=None, per=0):
                act.wait_ge(weights_used, at(through(g, half), i, 2 * per))
                if i is not None:
                    params_in_place()
                act.activation(dst, pair(c), func).then_inc(pair_read[c % 2], 1)

            def read_out_rows(c, g, dst, func=ACT.Copy, half=2):
                act.wait_ge(weights_used, through(g, half))
                act.activation(dst, ps[:, 2 * (c % 2):2 * (c % 2) + 2, :], func).then_inc(pair_read[c % 2], 1)

            def tiles4(tensor, k0):
                return tensor[:, k0:k0 + 4].rearrange("p k t -> p (k t)")

            x_upper(0)
            upper(0)
            for g in range(0, 4):
                upper(g + 1)
            read_out(CH["k_mem"], 3, tiles4(kmT, 0))
            for g in range(4, 8):
                upper(g + 1)
            read_out_rows(CH["v_mem"], 7, vm[:])
            x_upper(1)
            g0 = AT["latent"]
            for g in range(g0, g0 + 3):
                upper(g + 1)
            act.wait_ge(pair_read[CH["latent"] % 2], reads(CH["latent"]))
            for t in range(T):
                act.activation(idx_r[:, t, 0:LATENT], ckv[:, t], ACT.Square, accum_out=misc(t)).then_inc(ck_squared, 1)
            upper(g0 + 4)
            upper(g0 + 5)
            act.wait_ge(small_T, 1)
            act.activation(ckhi[:].rearrange("p c t -> p (c t)"), ps[:, 4], ACT.Copy).then_inc(ckhi_ready, 1)
            act.wait_ge(small_T, 2)
            act.activation(kiT[:], ps[:, 5, 0:S], ACT.Copy).then_inc(ki_ready, 1)
            for g in range(AT["q_idx"] + 2, AT["q_idx"] + 8):
                upper(g + 1)
                if g in (AT["q_idx"] + 3, AT["q_idx"] + 7):
                    c = CH["q_idx"] + (g > AT["q_idx"] + 3)
                    read_out(c, g, tiles4(qi, 4 * (c - CH["q_idx"])))
            act.dma_start(cb[:], c_row.partition_broadcast(P)).then_inc(cb_landed, 16)
            for n in range(8):
                g = AT["v_moba"] + n
                upper(g + 1)
                for h in (2 * n, 2 * n + 1):
                    act.wait_ge(idx_done, h + 1)
                    if h >= 2:
                        act.wait_ge(idx_added, h - 1)
                    act.activation(idx_r[:, h % 2], ps[:, 4 + h % 4], ACT.Relu, scale=IDX_DIM ** -0.5).then_inc(idx_relu, 1)
                if n in (3, 7):
                    c = CH["v_moba"] + n // 4
                    read_out_rows(c, g, vall[:, :, 1024 + 512 * (n // 4):1536 + 512 * (n // 4)])
            g = AT["w_uk"]
            upper(g + 1)
            for n in range(2):
                read_out(CH["w_uk"] + n, g, tiles4(qk, 24 + 4 * n), half=n + 1)
            g = AT["w_uv"]
            upper(g + 1)
            for n in range(2):
                read_out_rows(CH["w_uv"] + n, g, vall[:, :, 512 * n:512 * n + 512], half=n + 1)
            act.wait_ge(cb_landed, 16)
            act.activation(cb[:], cb[:], ACT.Silu).then_inc(cb_ready, 1)
            g0 = AT["qk"]
            with act.Fori(0, 3) as i:
                for s in range(8):
                    upper(g0 + s + 1, i, 8)
                    if s % 4 == 3:
                        read_out(CH["qk"] + s // 4, g0 + s, qk[:, bass.ds(at(s - 3, i, 8), 4)].rearrange("p k t -> p (k t)"),
                                 i=i, per=8)

            g0, c0 = AT["gate_a"], CH["gate_a"]
            with act.Fori(0, 2) as i:
                for q in range(4):
                    g = g0 + 2 * q
                    for j in range(2):
                        act.activation(qs[:, j], qk[:, at(8 * j + q, i, 4)], ACT.Copy).then_inc(qv_ready, 1)
                        act.activation(vs[:, j], vall[:, :, bass.ds(at(1024 * j + HD * q, i, 4 * HD), HD)], ACT.Copy)\
                           .then_inc(qv_ready, 1)
                    upper(g + 1, i, 8)
                    for j in range(2):
                        for t, (k0, k1) in enumerate(((0, 128), (128, 384))):
                            act.wait_ge(att_max, at(4 * q + 2 * j + t + 1, i, 16))
                            act.activation(att_e[:, j, k0:k1], att_s[:, j, k0:k1], ACT.Exp, bias=misc(8 + 2 * j + t),
                                           accum_out=misc(12 + 2 * j + t)).then_inc(att_exp, 1)
                    upper(g + 2, i, 8)
                    for j in range(2):
                        act.wait_ge(att_T, at(2 * q + j + 1, i, 8))
                        act.activation(att_pT[:, j], ps[:, 6 + j, 0:384], ACT.Copy).then_inc(att_pT_ready, 1)
                    if q % 2 == 1:
                        c = c0 + q // 2
                        read_out(c, g + 1, gate_a[:, bass.ds(at(2 * q - 2, i, 8), 4)].rearrange("p k t -> p (k t)"), i=i, per=8)
                    act.wait_ge(att_o, at(2 * q + 2, i, 8))

            g0, c0 = AT["gates"], CH["gates"]

            def gate(n, src, c, i):
                act.wait_ge(pair_read[c % 2], at(reads(c), i, 3))
                params_in_place()
                u = 4 * unit
                for m in range(4):
                    ins = act.activation(sig[:, n, S * m:S * m + S], src(m), ACT.Sigmoid,
                                         bias=col[:, bass.ds(at(COL["b_gate"] + KT * n + u + m, i, 8), 1)])
                return ins

            with act.Fori(0, 2) as i:
                for unit in range(2):
                    g, c = g0 + 8 * unit, c0 + 3 * unit
                    gate(0, lambda m: gate_a[:, at(4 * unit + m, i, 8)], c - 3, i).then_inc(sig_ready, 1)
                    for s in range(8):
                        upper(g + s + 1, i, 16)
                        if s == 5:
                            act.wait_ge(weights_used, at(through(g + s), i, 32))
                            gate(1, lambda m: pair(c + 1)[:, S * m:S * m + S], c - 1, i).then_inc(pair_read[(c + 1) % 2], 1)

            def wide_start(name, n_ln=None):
                act.wait_ge(weights_used, through(AT[name] - 1))
                if n_ln is not None:
                    act.dma_start(gamma[:], ln_g[n_ln:n_ln + 1].partition_broadcast(P)).then_inc(ln_landed, 16)
                    act.dma_start(beta[:], ln_b[n_ln:n_ln + 1].partition_broadcast(P)).then_inc(ln_landed, 16)

            def wide_turns(name, src, turns, i0=0):
                g0 = AT[name]

                def turn(i):
                    for s in range(4):
                        act.activation(shi[:, s], src[:, at(s, i, 4)], ACT.Copy).then_inc(shi_ready, 1)
                        upper(g0 + s + 1, i, 4)

                if turns == 1:
                    turn(None)
                else:
                    with act.Fori(0, turns) as i:
                        turn(i)

            def squares(src, counts, centred):
                for t in range(T):
                    act.wait_ge(mean_ready if centred else res_ready, counts[t])
                    bias = misc(2 + t) if centred else 0.0
                    act.activation(ps[:, 4 * t:4 * t + 4].rearrange("p b n -> p (b n)"), src[:, t], ACT.Square, bias=bias,
                                   accum_out=misc(4 + t)).then_inc(sq_ready, 1)

            act.wait_ge(merged_ready, 4)
            act.dma_start(res[:], x.rearrange("(t p) d -> p t d", p=P)).then_inc(x_landed, 16)
            wide_start("out1", 0)
            wide_turns("out1", merged, 4)
            squares(res, (1, 2), True)
            x_upper(2)
            g0 = AT["q_mem"]
            for g in range(g0, g0 + 4):
                upper(g + 1)
            read_out(CH["q_mem"], g0 + 3, tiles4(qmT, 0))

            for h in range(HEADS_MEM):
                act.wait_ge(m_max, h + 1)
                for t in range(T):
                    act.activation(mem_p[:, h, S * t:S * t + S], ps[:, 4 + h, S * t:S * t + S], ACT.Exp, bias=misc(8 + 2 * h + t),
                                   scale=HD ** -0.5, accum_out=misc(24 + 2 * h + t)).then_inc(m_exp, 1)
            spare = 2 * ((CH["q_mem"] + 1) % 2)
            for h in range(HEADS_MEM + 1):
                if h < HEADS_MEM:
                    act.wait_ge(m_T, h + 1)
                    act.activation(mem_pT[:, h % 2], ps[:, spare + h % 2], ACT.Copy).then_inc(m_pT, 1)
                if h >= 1:
                    act.wait_ge(m_o, h)
                    act.activation(omT[:, h - 1], ps[:, 3 + h, 0:S], ACT.Copy).then_inc(m_out, 1)
            wide_start("o_mem", 1)
            act.wait_ge(m_out, HEADS_MEM)
            wide_turns("o_mem", omT, 1)
            squares(res, (3, 4), True)
            x_upper(3)
            g0, c0 = AT["up1"], CH["up1"]
            with act.Fori(0, FC) as i:
                for s in range(8):
                    upper(g0 + s + 1, i, 8)
                    if s == 3:
                        act.wait_ge(weights_used, at(through(g0 + s), i, 16))
                        act.wait_ge(pair_read[(c0 + 1) % 2], at(reads(c0 - 1), i, 1))
                        act.activation(silu[:], pair(c0), ACT.Silu).then_inc(pair_read[c0 % 2], 1)
            wide_start("down1", 2)
            act.wait_ge(pair_read[(c0 + 1) % 2], reads(c0 + 2 * FC - 1))
            wide_turns("down1", hid, FC)
            squares(res, (5, 6), True)
            squares(res, (7, 9), False)
            x_upper_modulated(4, 0)
            g0 = AT["lstm_gates"]
            upper(g0 + 1)
            g0 = AT["lstm_q"]
            for g in range(g0, g0 + 4):
                upper(g + 1)
            read_out(CH["lstm_q"], g0 + 3, tiles4(lq, 0))
            act.wait_ge(g_abs, 1)
            act.activation(g_e[:], g_e[:], ACT.Exp, scale=-1.0).then_inc(g_exp, 1)
            g0 = AT["lstm_k"]
            for g in range(g0, g0 + 4):
                upper(g + 1)
            read_out(CH["lstm_k"], g0 + 3, tiles4(lk, 0))
            act.wait_ge(g_one, 1)
            act.activation(g_e[:], g_e[:], ACT.Ln).then_inc(g_ln, 1)
            g0 = AT["lstm_v"]
            for n in range(8):
                upper(g0 + n + 1)
                if n % 4 == 3:
                    c = CH["lstm_v"] + n // 4
                    act.wait_ge(weights_used, through(g0 + n))
                    if n == 3:
                        act.wait_ge(built, 14)
                    for t in range(T):
                        ins = act.activation(lv[:, t, 2 * (n // 4):2 * (n // 4) + 2, 0:DV],
                                             ps[:, 2 * (c % 2) + t].rearrange("p (h v) -> p h v", h=2), ACT.Copy)
                    ins.then_inc(pair_read[c % 2], 1)
            act.wait_ge(g_stab, 1)
            act.activation(g_m[:], g_m[:], ACT.Exp, scale=-1.0).then_inc(g_floor, 1)

            def l_squared(h):
                for t in range(T):
                    act.wait_ge(l_h, 2 * h + t + 1)
                    if h + t:
                        act.wait_ge(l_sq, 2 * h + t)
                    act.activation(l_squares[:], lh[:, t], ACT.Square, accum_out=misc(16 + t)).then_inc(l_sq, 1)

            for n in range(4):
                name = "lstm_o" if n < 2 else "fourier"
                g0, c = AT[name] + 4 * (n % 2), CH[name] + n % 2
                upper(g0 + 1)
                upper(g0 + 2)
                if n >= 1:
                    l_squared(n - 1)
                upper(g0 + 3)
                upper(g0 + 4)
                act.wait_ge(l_x, n + 1)
                act.activation(le[:], lx[:], ACT.Exp, scale=-1.0).then_inc(l_e, 1)
                if n < 2:
                    read_out(c, g0 + 3, tiles4(so, 4 * n), ACT.Sigmoid)
                else:
                    read_out_rows(c, g0 + 3, uf[:, :, 512 * (n - 2):512 * (n - 2) + 512])
            for h in range(4):
                act.wait_ge(f_first, h + 1)
                act.activation(fa[h][:].rearrange("p f k -> p (f k)"), ps[:, h], ACT.Copy).then_inc(f_copied, 1)
                if h == 1:
                    l_squared(LH - 1)
            for h in range(4):
                act.wait_ge(f_second, h + 1)
                if h >= 2:
                    act.wait_ge(mix_f, h - 1)
                act.activation(fy[:, h % 2], ps[:, h], ACT.Copy).then_inc(f_read, 1)
                ends = ps[:, h, 0:2 * P + 2].rearrange("p (f k) -> p f k", f=2)[:, :, 0:P + 1:P]
                act.activation(mixT[:, 2 * h:2 * h + 2, 0:P + 1:P], ends, ACT.Copy).then_inc(f_read, 1)

            def gate_rows(n):
                act.wait_ge(gate_T, n + 1)
                act.activation(gates_in_rows[n][:], ps[:, 4:8].rearrange("p b n -> p (b n)"), ACT.Copy).then_inc(gate_ready, 1)

            wide_start("out2")
            gate_rows(0)
            act.wait_ge(mix_f, LH)
            act.wait_ge(mix_m, 2 * LH)
            wide_turns("out2", mixT, 4)
            squares(res, (10, 11), False)
            x_upper_modulated(5, 3 * KT)
            g0, c0 = AT["up2"], CH["up2"]

            def middle_tap(q, i):
                act.wait_ge(weights_used, at(through(g0 + 4 * q + 3), i, 16))
                if q == 0:
                    act.wait_ge(conv_done, at(1, i, 1))
                params_in_place()
                for m in range(4):
                    tap = at(COL["w_conv"] + 2 * FT + FT * q + m, i, 4)
                    bias = at(COL["b_conv"] + FT * q + m, i, 4)
                    ins = act.activation(conv[:, q, S * m:S * m + S], pair(c0 + q)[:, S * m:S * m + S], ACT.Identity,
                                         bias=col[:, bass.ds(bias, 1)], scale=col[:, bass.ds(tap, 1)])
                ins.then_inc(conv_mid, 1)

            def silu_of_first(i):
                act.wait_ge(pair_read[c0 % 2], at(reads(c0), i, 1))
                act.activation(silu[:], conv[:, 0], ACT.Silu).then_inc(silu_ready, 1)

            for s in range(4):
                upper(g0 + s + 1)
            with act.Fori(0, FC - 1) as i:
                for s in range(8):
                    upper(g0 + 4 + s + 1, i, 8)
                    if s % 4 == 0:
                        middle_tap(s // 4, i)
                    if s == 2:
                        silu_of_first(i)
            for s in range(4):
                upper(AT["down2"] - 4 + s + 1)
                if s == 0:
                    middle_tap(0, FC - 1)
                if s == 2:
                    silu_of_first(FC - 1)
            middle_tap(1, FC - 1)
            gate_rows(1)
            wide_start("down2")
            act.dma_start(gamma[:], norm_f.partition_broadcast(P)).then_inc(ln_landed, 16)
            act.wait_ge(conv_done, FC + 1)
            g0 = AT["down2"]
            with act.Fori(0, FC - 1) as i:
                for s in range(4):
                    act.activation(shi[:, s], hid[:, at(s, i, 4)], ACT.Copy).then_inc(shi_ready, 1)
                    upper(g0 + s + 1, i, 4)
            for s in range(4):
                act.activation(shi[:, s], hid[:, FT - 4 + s], ACT.Copy).then_inc(shi_ready, 1)
                upper(g0 + FT - 4 + s + 1)
            squares(res, (12, 13), False)

        @block.vector
        def _(dve):
            order = Order(dve, dve_order)

            def rest(g, i=None, per=0):
                if g >= G:
                    return
                for half in range(2):
                    h = 2 * g + half
                    dve.wait_ge(hi_ready, at(h + 1, i, 2 * per))
                    dve.tensor_tensor(wlo[:, h % 4], raw[g % 4][:, 1024 * half:1024 * half + 1024], whi[:, h % 4].bitcast(F32),
                                      ALU.subtract).then_inc(lo_ready, 1)

            def x_rest(n, src=None, shift=None):
                for b in range(8):
                    if src is not None and b % 2 == 0:
                        odd = b + 1
                        dve.wait_ge(xT_done, 8 * n + odd + 1)
                        if b >= 2:
                            dve.wait_ge(xlo_ready, 8 * n + b)
                        for f in range(2):
                            k = 2 * odd + f
                            ins = dve.tensor_scalar(modulated[:, 1, S * f:S * f + S], ps[:, odd, S * f:S * f + S],
                                                    scale_col[:, k:k + 1], mod[:, shift + k:shift + k + 1], ALU.mult, ALU.add)
                        ins.then_inc(odd_modulated, 1)
                    dve.wait_ge(xhi_ready, 8 * n + b + 1)
                    hi = xhi[:, 2 * b:2 * b + 2].rearrange("p k t -> p (k t)")
                    lo = xlo[:, 2 * b:2 * b + 2].rearrange("p k t -> p (k t)")
                    dve.tensor_tensor(lo, ps[:, b] if src is None else src[:, b % 2], hi.bitcast(F32), ALU.subtract)\
                       .then_inc(xlo_ready, 1)

            def modulation(n, i=None, per=0):
                slot = n % 2
                dve.wait_ge(ada_landed[slot], at(16 * (n // 2 + 1), i, 8 * per))
                dve.scalar_tensor_tensor(out=ada[slot][:], in0=ada[slot][:], scalar=1.0, in1=cb[:], op0=ALU.mult, op1=ALU.mult,
                                         accum_out=mod[:, bass.ds(at(n, i, per), 1)]).then_inc(ada_used, 1)

            x_rest(0)
            rest(0)
            for g in range(0, 8):
                rest(g + 1)
            x_rest(1)
            g0, wide_n = AT["latent"], LATENT + IDX_DIM + IDX_HEADS
            for g in range(g0, g0 + 3):
                rest(g + 1)
            dve.wait_ge(weights_used, through(g0 + 2))
            dve.wait_ge(built, 11)
            order.mark(dve.tensor_copy(kw[:], ps[:, 0:2, LATENT:wide_n]))
            dve.tensor_copy(ckv[:], ps[:, 0:2, 0:LATENT]).then_inc(pair_read[0], 1)
            dve.wait_ge(ck_squared, 2)
            dve.tensor_scalar(var(0, 0, 2), misc(0, 2), 1.0 / LATENT, LN_EPS, ALU.mult, ALU.add).then_inc(var_ready, 1)
            order.wait()
            order.mark(dve.tensor_reduce(misc(2, 2), kw[:, :, 0:IDX_DIM], AX_X, ALU.add))
            order.wait()
            order.mark(dve.tensor_scalar(misc(4, 2), misc(2, 2), -1.0 / IDX_DIM, None, ALU.mult))
            order.wait()
            for t in range(T):
                order.mark(dve.tensor_scalar(kc[:, t], kw[:, t, 0:IDX_DIM], misc(4 + t), None, ALU.add))
            order.wait()
            order.mark(dve.tensor_tensor(ksq[:], kc[:], kc[:], ALU.mult))
            order.wait()
            order.mark(dve.tensor_reduce(misc(6, 2), ksq[:], AX_X, ALU.add))
            order.wait()
            dve.tensor_scalar(var(1, 0, 2), misc(6, 2), 1.0 / IDX_DIM, LN_EPS, ALU.mult, ALU.add).then_inc(var_ready, 1)
            order.mark(dve.tensor_scalar(wi[:], kw[:, :, IDX_DIM:IDX_DIM + IDX_HEADS], IDX_HEADS ** -0.5, None, ALU.mult))
            rest(g0 + 4)
            dve.wait_ge(consts_landed, 32)
            dve.wait_ge(rstd_ready, 1)
            for t in range(T):
                dve.scalar_tensor_tensor(out=ckv[:, t], in0=ckv[:, t], scalar=rstd(0, t), in1=row[:, 0:LATENT],
                                         op0=ALU.mult, op1=ALU.mult).then_inc(ck_ready, 1)
            dve.wait_ge(rstd_ready, 2)
            for t in range(T):
                order.mark(dve.scalar_tensor_tensor(out=kc[:, t], in0=kc[:, t], scalar=rstd(1, t),
                                                    in1=row[:, LATENT:LATENT + IDX_DIM], op0=ALU.mult, op1=ALU.mult))
            order.wait()
            for t in range(T):
                for n in range(2):
                    dve.tensor_tensor(kn[:, t, IDX_DIM * n:IDX_DIM * n + IDX_DIM], kc[:, t],
                                      row[:, LATENT + IDX_DIM:LATENT + 2 * IDX_DIM], ALU.add).then_inc(kn_ready, 1)
            rest(g0 + 5)
            dve.wait_ge(ckhi_ready, 1)
            dve.tensor_tensor(cklo[:].rearrange("p c t -> p (c t)"), ps[:, 4], ckhi[:].rearrange("p c t -> p (c t)").bitcast(F32),
                              ALU.subtract).then_inc(cklo_ready, 1)
            for g in range(AT["q_idx"] + 2, AT["q_idx"] + 8):
                rest(g + 1)
            for n in range(8):
                rest(AT["v_moba"] + n + 1)
                for h in (2 * n, 2 * n + 1):
                    dve.wait_ge(idx_relu, h + 1)
                    for t in range(T):
                        relu = idx_r[:, h % 2, S * t:S * t + S]
                        if h == 0:
                            ins = dve.tensor_scalar(score[:, t], relu, wi[:, t, h:h + 1], None, ALU.mult)
                        else:
                            if t == 0:
                                order.wait()
                            else:
                                dve.wait_ge(idx_added, h)
                            ins = dve.scalar_tensor_tensor(out=score[:, t], in0=relu, scalar=wi[:, t, h:h + 1], in1=score[:, t],
                                                           op0=ALU.mult, op1=ALU.add)
                        if t == 0:
                            order.mark(ins)
                        else:
                            ins.then_inc(idx_added, 1)
            rest(AT["w_uk"] + 1)
            dve.wait_ge(built, 11)
            dve.wait_ge(idx_added, IDX_HEADS)
            seen = [(score[:, 0, 0:128], 0, 128), (score[:, 1, :], 128, 384)]
            for work, c0, c1 in seen:
                order.mark(dve.tensor_tensor(work, work, causal[:, c0:c1], ALU.add))
            for n in range(TOPK // 8):
                order.wait()
                for t, (work, _, _) in enumerate(seen):
                    order.mark(dve.max(best8[:, t], work))
                order.wait()
                for t, (work, _, _) in enumerate(seen):
                    order.mark(dve.match_replace(work, best8[:, t], work, TAKEN))
                if n == 3:
                    rest(AT["w_uv"] + 1)
            order.wait()
            for work, c0, c1 in seen:
                order.mark(dve.tensor_scalar(work, work, TAKEN / 2, OUT_OF_SIGHT, ALU.is_gt, ALU.mult))
            order.wait()
            order.mark(dve.tensor_tensor(chosen[:, 0:128], seen[0][0], causal[:, 0:128], ALU.add))
            dve.tensor_tensor(chosen[:, 128:384], seen[1][0], causal[:, 128:384], ALU.add).then_inc(att_free, 1)
            dve.wait_ge(cb_ready, 1)
            g0 = AT["qk"]
            with dve.Fori(0, 3) as i:
                for s in range(8):
                    rest(g0 + s + 1, i, 8)

            dve.wait_ge(att_free, 1)
            order.wait()
            c = CH["qk"] + 4
            dve.wait_ge(pair_read[c % 2], reads(c))
            g0 = AT["gate_a"]
            with dve.Fori(0, 2) as i:
                order.enter(i, 24)
                for q in range(4):
                    g = g0 + 2 * q
                    for j, mask in enumerate((chosen, causal)):
                        order.mark(dve.scalar_tensor_tensor(out=att_ab[:, j], in0=dist[:],
                                                            scalar=col[:, bass.ds(at(COL["slope"] + q, i, 4), 1)],
                                                            in1=mask[:], op0=ALU.mult, op1=ALU.add))
                    rest(g + 1, i, 8)
                    for j in range(2):
                        dve.wait_ge(att_scores, at(2 * q + j + 1, i, 8))
                        order.wait()
                        order.mark(dve.scalar_tensor_tensor(out=att_s[:, j], in0=ps[:, 4 + j, 0:384], scalar=HD ** -0.5,
                                                            in1=att_ab[:, j], op0=ALU.mult, op1=ALU.add))
                        order.wait()
                        for t, (k0, k1) in enumerate(((0, 128), (128, 384))):
                            dve.tensor_reduce(misc(8 + 2 * j + t), att_s[:, j, k0:k1], AX_X, ALU.max, negate=True)\
                               .then_inc(att_max, 1)
                    for j in range(2):
                        dve.wait_ge(att_exp, at(4 * q + 2 * j + 2, i, 16))
                        order.mark(dve.reciprocal(misc(12 + 2 * j, 2), misc(12 + 2 * j, 2)))
                        order.wait()
                        for t, (k0, k1) in enumerate(((0, 128), (128, 384))):
                            dve.tensor_scalar(att_e[:, j, k0:k1], att_e[:, j, k0:k1], misc(12 + 2 * j + t), None, ALU.mult)\
                               .then_inc(att_p, 1)
                    rest(g + 2, i, 8)
                    for j in range(2):
                        dve.wait_ge(att_o, at(2 * q + j + 1, i, 8))
                        dve.tensor_scalar(ohi[:, at(8 * j + q, i, 4)], ps[:, 4 + j, 0:S], 1.0, None, ALU.mult).then_inc(att_ohi, 1)
                    for j in range(2):
                        dve.wait_ge(att_ohi, at(2 * q + j + 1, i, 8))
                        dve.tensor_tensor(olo[:, at(8 * j + q, i, 4)], ps[:, 4 + j, 0:S],
                                          ohi[:, at(8 * j + q, i, 4)].bitcast(F32), ALU.subtract).then_inc(att_free, 1)
                order.leave(2)

            g0, c0 = AT["gates"], CH["gates"]
            with dve.Fori(0, 2) as i:
                for unit in range(2):
                    g, c = g0 + 8 * unit, c0 + 3 * unit
                    for s in range(8):
                        rest(g + s + 1, i, 16)
                        if s == 1:
                            dve.wait_ge(weights_used, at(through(g + s), i, 32))
                            dve.wait_ge(sig_ready, at(unit + 1, i, 2))
                            dve.tensor_tensor(gated_a[:], pair(c), sig[:, 0], ALU.mult).then_inc(pair_read[c % 2], 1)
                        if s == 7:
                            dve.wait_ge(weights_used, at(through(g + s), i, 32))
                            dve.wait_ge(pair_read[(c + 1) % 2], at(reads(c + 1), i, 3))
                            dve.tensor_tensor(gated_b[:], pair(c + 2), sig[:, 1], ALU.mult).then_inc(pair_read[c % 2], 1)
                            dve.wait_ge(pair_read[c % 2], at(reads(c + 2), i, 3))
                            dve.tensor_tensor(merged[:, bass.ds(at(4 * unit, i, 8), 4)].rearrange("p k t -> p (k t)"), gated_a[:],
                                              gated_b[:], ALU.add).then_inc(merged_ready, 1)

            def wide_turns(name, src, turns, ada0=None, ada_per=ADA_DOWN):
                g0, k0 = AT[name], SRC[name]

                def turn(i):
                    for s in range(4):
                        dve.wait_ge(shi_ready, at(k0 + s + 1, i, 4))
                        dve.tensor_tensor(slo[:, s], src[:, at(s, i, 4)], shi[:, s].bitcast(F32), ALU.subtract)\
                           .then_inc(slo_ready, 1)
                        rest(g0 + s + 1, i, 4)
                        if ada0 is not None and s in (1, 2):
                            modulation(ada0 + s - 1, i, ada_per)

                if turns == 1:
                    turn(None)
                else:
                    with dve.Fori(0, turns) as i:
                        turn(i)

            def add_and_norm(n, g, job):
                for t in range(T):
                    if t == 0:
                        dve.wait_ge(first_rows_done, TURNS_DONE[n])
                    else:
                        dve.wait_ge(weights_used, through(g))
                    order.mark(dve.scalar_tensor_tensor(out=res[:, t], in0=res[:, t], scalar=ALPHA,
                                                        in1=ps[:, 4 * t:4 * t + 4].rearrange("p b n -> p (b n)"),
                                                        op0=ALU.mult, op1=ALU.add, accum_out=misc(t)))
                    order.wait()
                    dve.tensor_scalar(misc(2 + t), misc(t), -1.0 / D, None, ALU.mult).then_inc(mean_ready, 1)
                dve.wait_ge(ln_landed, 32 * (n + 1))
                for t in range(T):
                    dve.wait_ge(sq_ready, 2 * n + t + 1)
                    dve.tensor_scalar(var(job + t), misc(4 + t), 1.0 / D, LN_EPS, ALU.mult, ALU.add).then_inc(var_ready, 1)
                    order.mark(dve.scalar_tensor_tensor(out=res[:, t], in0=res[:, t], scalar=misc(2 + t), in1=gamma[:],
                                                        op0=ALU.add, op1=ALU.mult))
                    order.wait()
                    dve.wait_ge(rstd_ready, job + t + 1)
                    for d0, d1 in ((0, D),) if t == 0 else ((0, D // 2), (D // 2, D)):
                        dve.scalar_tensor_tensor(out=res[:, t, d0:d1], in0=res[:, t, d0:d1], scalar=rstd(job + t),
                                                 in1=beta[:, d0:d1], op0=ALU.mult, op1=ALU.add).then_inc(res_ready, 1)

            def rms_rows(squared, job, last=False):
                for t in range(T):
                    dve.wait_ge(sq_ready, squared + t + 1)
                    dve.tensor_scalar(var(job + t), misc(4 + t), 1.0 / D, RMS_EPS, ALU.mult, ALU.add).then_inc(var_ready, 1)
                    dve.wait_ge(rstd_ready, job + t + 1)
                    if last:
                        for d0 in (0, D // 2):
                            cut = slice(d0, d0 + D // 2)
                            dve.scalar_tensor_tensor(out=xn[:, t, cut], in0=res[:, t, cut], scalar=rstd(job + t),
                                                     in1=gamma[:, cut], op0=ALU.mult, op1=ALU.mult).then_inc(out_ready, 1)
                    else:
                        dve.tensor_scalar(xn[:, t], res[:, t], rstd(job + t), None, ALU.mult).then_inc(xn_ready, 1)

            def scales(first, norm):
                dve.scalar_tensor_tensor(out=scale_col[:], in0=mod[:, first:first + KT], scalar=1.0,
                                         in1=col[:, COL[norm]:COL[norm] + KT], op0=ALU.add, op1=ALU.mult).then_inc(mod_ready, 1)

            def add_gated(n, g, gate_row):
                for t in range(T):
                    if t == 0:
                        dve.wait_ge(first_rows_done, TURNS_DONE[n])
                    else:
                        dve.wait_ge(weights_used, through(g))
                    order.mark(dve.tensor_tensor(xn[:, t], ps[:, 4 * t:4 * t + 4].rearrange("p b n -> p (b n)"), gate_row[:],
                                                 ALU.mult))
                    order.wait()
                    dve.tensor_tensor(res[:, t], res[:, t], xn[:, t], ALU.add).then_inc(res_ready, 1)

            wide_turns("out1", merged, 4, 0, ADA_OUT)
            dve.wait_ge(x_landed, 32)
            add_and_norm(0, AT["q_mem"] - 1, 2)
            x_rest(2)
            for g in range(AT["q_mem"], AT["q_mem"] + 4):
                rest(g + 1)

            for h in range(HEADS_MEM):
                dve.wait_ge(m_scores, h + 1)
                order.mark(dve.tensor_reduce(misc(32 + 2 * h, 2), ps[:, 4 + h].rearrange("p (t k) -> p t k", t=T), AX_X, ALU.max))
                order.wait()
                dve.tensor_scalar(misc(8 + 2 * h, 2), misc(32 + 2 * h, 2), -HD ** -0.5, None, ALU.mult).then_inc(m_max, 1)
            for h in range(HEADS_MEM):
                dve.wait_ge(m_exp, 2 * h + 2)
                order.mark(dve.reciprocal(misc(24 + 2 * h, 2), misc(24 + 2 * h, 2)))
                order.wait()
                for t in range(T):
                    dve.tensor_scalar(mem_p[:, h, S * t:S * t + S], mem_p[:, h, S * t:S * t + S], misc(24 + 2 * h + t), None,
                                      ALU.mult).then_inc(m_p, 1)
            dve.wait_ge(m_out, HEADS_MEM)
            wide_turns("o_mem", omT, 1)
            add_and_norm(1, AT["up1"] - 1, 4)
            x_rest(3)
            g0, c0, n0 = AT["up1"], CH["up1"], 4 * ADA_OUT
            with dve.Fori(0, FC) as i:
                for s in range(8):
                    rest(g0 + s + 1, i, 8)
                    if s == 7:
                        dve.wait_ge(weights_used, at(through(g0 + s), i, 16))
                        dve.wait_ge(pair_read[c0 % 2], at(reads(c0), i, 1))
                        dve.tensor_tensor(hid[:, bass.ds(at(0, i, 4), 4)].rearrange("p k t -> p (k t)"), pair(c0 + 1), silu[:],
                                          ALU.mult).then_inc(pair_read[(c0 + 1) % 2], 1)
                    if s % 4 != 3:
                        modulation(n0 + s - s // 4, i, ADA_UP)
            wide_turns("down1", hid, FC, n0 + FC * ADA_UP)
            add_and_norm(2, AT["lstm_gates"] - 1, 6)
            dve.wait_ge(ada_used, ADA)
            order.mark(dve.tensor_tensor(mod[:], mod[:], col[:, COL["b_ada"]:COL["b_ada"] + ADA], ALU.add))
            order.wait()
            scales(KT, "norm1")
            rms_rows(6, 8)
            x_rest(4, modulated, 0)
            rest(AT["lstm_gates"] + 1)
            rest(AT["lstm_gates"] + 2)
            dve.wait_ge(weights_used, through(AT["lstm_gates"]))
            dve.wait_ge(late_landed, 32)
            c = CH["lstm_gates"]
            for d in range(2):
                for n, dst in enumerate((g_in, g_fo)):
                    q = 32 * (2 * d + n)
                    ins = dve.tensor_scalar(dst[:, d], ps[q:q + LH, 2 * (c % 2), 0:S], gbias[q:q + LH, :], None, ALU.add)
            ins.then_inc(pair_read[c % 2], 1)
            dve.wait_ge(pair_read[c % 2], reads(c))
            rest(AT["lstm_gates"] + 3)
            dve.scalar_tensor_tensor(out=g_e[:], in0=g_fo[:], scalar=-1.0, in1=g_fo[:], op0=ALU.mult, op1=ALU.max).then_inc(g_abs, 1)
            rest(AT["lstm_gates"] + 4)
            rest(AT["lstm_gates"] + 5)
            rest(AT["lstm_gates"] + 6)
            dve.wait_ge(g_exp, 1)
            dve.tensor_scalar(g_e[:], g_e[:], 1.0, None, ALU.add).then_inc(g_one, 1)
            for g in range(AT["lstm_k"] + 2, AT["lstm_k"] + 5):
                rest(g)
            rest(AT["lstm_v"] + 1)
            dve.wait_ge(g_ln, 1)
            order.mark(dve.scalar_tensor_tensor(out=g_fo[:], in0=g_fo[:], scalar=0.0, in1=g_e[:], op0=ALU.min, op1=ALU.subtract))
            order.wait()
            ones_row = ones[0:LH, 0:1].to_broadcast([LH, S])
            order.mark(dve.tensor_tensor_scan(g_sum[:, 0], ones_row, g_fo[:, 0], 0.0, ALU.mult, ALU.add))
            order.mark(dve.tensor_tensor_scan(g_sum[:, 1, ::-1], ones_row, g_fo[:, 1, ::-1], 0.0, ALU.mult, ALU.add))
            order.wait()
            order.mark(dve.tensor_tensor(g_a[:], g_in[:], g_sum[:], ALU.subtract))
            order.wait()
            rest(AT["lstm_v"] + 2)
            order.mark(dve.tensor_tensor_scan(g_max[:, 0], g_a[:, 0], g_a[:, 0], -3e38, ALU.max, ALU.max))
            order.mark(dve.tensor_tensor_scan(g_max[:, 1, ::-1], g_a[:, 1, ::-1], g_a[:, 1, ::-1], -3e38, ALU.max, ALU.max))
            order.wait()
            dve.tensor_tensor(g_m[:], g_sum[:], g_max[:], ALU.add).then_inc(g_stab, 1)
            for g in range(AT["lstm_v"] + 3, AT["lstm_o"] + 1):
                rest(g)
            floors = lcols[:, 1].rearrange("p (n h) -> p n h", h=LH)

            def exponents(h):
                dve.wait_ge(l_bc, h + 1)
                for d, st, t0, t1, c0 in BLOCKS:
                    n = 8 * d + 4 * st + h
                    ins = dve.tensor_scalar(lx[:, c0:c0 + t1 - t0], ps[:, 4, S * d + t0:S * d + t1], lcols[:, 0, n:n + 1], 0.0,
                                            ALU.subtract, ALU.max)
                ins.then_inc(l_x, 1)

            def decayed(h):
                dve.wait_ge(l_e, h + 1)
                order.mark(dve.tensor_tensor(le[:], le[:], tri[:], ALU.mult))
                order.wait()
                dve.wait_ge(l_st, h + 1)
                for d, st, t0, t1, c0 in BLOCKS:
                    ins = dve.scalar_tensor_tensor(out=lp[:, c0:c0 + t1 - t0], in0=ps[:, 5, S * st + t0:S * st + t1],
                                                   scalar=HD ** -0.5, in1=le[:, c0:c0 + t1 - t0], op0=ALU.mult, op1=ALU.mult)
                ins.then_inc(l_p, 1)

            def head_sums(h):
                dve.wait_ge(l_num, h + 1)
                order.mark(dve.tensor_copy(misc(24, 4), ps[:, 4, 0:4]))
                order.wait()
                order.mark(dve.scalar_tensor_tensor(out=misc(28, 4), in0=misc(24, 4), scalar=-1.0, in1=misc(24, 4), op0=ALU.mult,
                                                    op1=ALU.max))
                order.wait()
                order.mark(dve.tensor_tensor(misc(32, 4), misc(28, 4), floors[:, :, h], ALU.max))
                order.wait()
                order.mark(dve.reciprocal(misc(36, 4), misc(32, 4)))
                order.wait()
                for t in range(T):
                    order.mark(dve.tensor_scalar(lh[:, t], ps[:, 6, S * t:S * t + DV], misc(36 + t), None, ALU.mult))
                order.wait()
                for t in range(T):
                    dve.scalar_tensor_tensor(out=lh[:, t], in0=ps[:, 7, S * t:S * t + DV], scalar=misc(38 + t), in1=lh[:, t],
                                             op0=ALU.mult, op1=ALU.add).then_inc(l_h, 1)

            def head_norm(h):
                dve.wait_ge(l_sq, 2 * h + 2)
                dve.tensor_scalar(var(10 + h, 0, 2), misc(16, 2), 1.0 / DV, RMS_EPS, ALU.mult, ALU.add).then_inc(var_ready, 1)
                dve.wait_ge(rstd_ready, 11 + h)
                for t in range(T):
                    dve.tensor_scalar(lh[:, t], lh[:, t], rstd(10 + h, t), None, ALU.mult).then_inc(l_hn, 1)

            def head_gated(h):
                c = CH["lstm_o"] + h // 2
                dve.wait_ge(pair_read[c % 2], reads(c))
                dve.wait_ge(l_hT, h + 1)
                for v in range(2):
                    k = 2 * h + v
                    dve.scalar_tensor_tensor(out=mixT[:, 8 + k], in0=ps[:, 5, S * v:S * v + S],
                                             scalar=col[:, COL["norm_m"] + k:COL["norm_m"] + k + 1], in1=so[:, k], op0=ALU.mult,
                                             op1=ALU.mult).then_inc(mix_m, 1)

            def mirrored(h):
                dve.wait_ge(f_read, 2 * h + 2)
                cosines = fy[:, h % 2, 0:2 * P + 2].rearrange("p (f k) -> p f k", f=2)[:, :, 1:P]
                sines = fy[:, h % 2, 2 * P + 2:2 * S].rearrange("p (f k) -> p f k", f=2)
                dve.tensor_tensor(mixT[:, 2 * h:2 * h + 2, 1:P], cosines, sines, ALU.subtract)
                dve.tensor_tensor(mixT[:, 2 * h:2 * h + 2, S - 1:P:-1], cosines, sines, ALU.add).then_inc(mix_f, 1)

            for n in range(4):
                g = AT["lstm_o"] + 4 * n
                rest(g + 1)
                if n == 0:
                    dve.wait_ge(g_cols_T, 1)
                    dve.tensor_copy(lcols[:].rearrange("p a n -> p (a n)"), ps[:, 6, 0:32]).then_inc(g_cols, 1)
                    dve.wait_ge(g_cols, 1)
                    dve.wait_ge(built, 19)
                else:
                    head_sums(n - 1)
                rest(g + 2)
                if n >= 1:
                    head_norm(n - 1)
                rest(g + 3)
                if n >= 1:
                    head_gated(n - 1)
                rest(g + 4)
                exponents(n)
                decayed(n)
            head_sums(LH - 1)
            head_norm(LH - 1)
            mirrored(0)
            mirrored(1)
            head_gated(LH - 1)
            mirrored(2)
            mirrored(3)
            dve.wait_ge(mix_f, LH)
            wide_turns("out2", mixT, 4)
            dve.wait_ge(gate_ready, 1)
            add_gated(3, AT["up2"] - 1, gates_in_rows[0])
            scales(4 * KT, "norm2")
            rms_rows(8, 14)
            dve.wait_ge(xn_ready, 4)
            x_rest(5, modulated, 3 * KT)
            dve.memset(misc(40), 0.0).then_inc(conv_done, 1)
            g0, c0 = AT["up2"], CH["up2"]

            def side_taps(q, side, i):
                if side == 0:
                    dve.wait_ge(conv_mid, at(q + 1, i, 2))
                else:
                    order.wait()
                bank = pair(c0 + q)
                to, fro = (1, 0) if side == 0 else (0, 1)
                for m in range(4):
                    tap = at(COL["w_conv"] + 4 * FT * side + FT * q + m, i, 4)
                    ins = dve.scalar_tensor_tensor(
                        out=conv[:, q, S * m + to:S * m + to + S - 1], in0=bank[:, S * m + fro:S * m + fro + S - 1],
                        scalar=col[:, bass.ds(tap, 1)], in1=conv[:, q, S * m + to:S * m + to + S - 1], op0=ALU.mult, op1=ALU.add)
                    if side == 0:
                        order.mark(ins)
                if side == 1:
                    ins.then_inc(pair_read[(c0 + q) % 2], 1)

            def beside(s, i):
                if s % 4 < 2:
                    side_taps(s // 4, s % 4, i)
                if s == 6:
                    dve.wait_ge(silu_ready, at(1, i, 1))
                    dve.wait_ge(pair_read[(c0 + 1) % 2], at(reads(c0 + 1), i, 1))
                    dve.tensor_tensor(hid[:, bass.ds(at(0, i, 4), 4)].rearrange("p k t -> p (k t)"), conv[:, 1], silu[:],
                                      ALU.mult).then_inc(conv_done, 1)

            for s in range(4):
                rest(g0 + s + 1)
            with dve.Fori(0, FC - 1) as i:
                order.enter(i, 8)
                for s in range(8):
                    rest(g0 + 4 + s + 1, i, 8)
                    beside(s, i)
                order.leave(FC - 1)
            for s in range(4):
                rest(AT["down2"] - 4 + s + 1)
                beside(s, FC - 1)
            for s in range(4, 8):
                beside(s, FC - 1)
            g0, k0 = AT["down2"], SRC["down2"]
            with dve.Fori(0, FC - 1) as i:
                for s in range(4):
                    dve.wait_ge(shi_ready, at(k0 + s + 1, i, 4))
                    dve.tensor_tensor(slo[:, s], hid[:, at(s, i, 4)], shi[:, s].bitcast(F32), ALU.subtract).then_inc(slo_ready, 1)
                    rest(g0 + s + 1, i, 4)
            for s in range(FT - 4, FT):
                dve.wait_ge(shi_ready, k0 + s + 1)
                dve.tensor_tensor(slo[:, s % 4], hid[:, s], shi[:, s % 4].bitcast(F32), ALU.subtract).then_inc(slo_ready, 1)
                rest(g0 + s + 1)
            dve.wait_ge(gate_ready, 2)
            add_gated(4, G - 1, gates_in_rows[1])
            dve.wait_ge(ln_landed, 32 * 3 + 16)
            rms_rows(10, 16, last=True)

        @block.tensor
        def _(pe):
            def transpose_rows(n, src, ready=None, counts=None):
                for t in range(T):
                    for b in range(8):
                        if counts is not None and b == 0:
                            pe.wait_ge(ready[t] if len(counts) == T else ready, counts[t])
                        if counts is not None and len(counts) > T and (t, b) == (1, 4):
                            pe.wait_ge(ready, counts[2])
                        for f in range(2):
                            k = 2 * b + f
                            ins = pe.transpose(ps[:, b, S * f + P * t:S * f + P * t + P], src[:, t, P * k:P * k + P], ident[:])
                        if t == T - 1:
                            ins.then_inc(xT_done, 1)

            def bank_pair(c, i=None, per=0):
                if c >= 2:
                    pe.wait_ge(pair_read[c % 2], at(c // 2, i, per))

            def product(g, half, c, form, left, k0, ks, width, first, last, i=None, per=0, fresh=None):
                h = 2 * g + half
                if fresh is not None:
                    pe.wait_ge(xlo_ready, 8 * fresh + max(2 + 2 * (c % 2), (k0 + ks + 1) // 2))
                pe.wait_ge(lo_ready, at(h + 1, i, 2 * per))
                hi, lo = (w[:, h % 4, 0:ks * width].rearrange("p (k n) -> p k n", k=ks) for w in (whi, wlo))
                lhi, llo = left
                for k in range(ks):
                    kt = k0 + k
                    begins, ends = first and k == 0, last and k == ks - 1
                    for m in range(width // P if form == "T" else T):
                        for n, (w, a) in enumerate(((hi, lhi), (hi, llo), (lo, lhi))):
                            if form == "T":
                                o = ps[:, 2 * (c % 2) + m // 2, S * (m % 2):S * (m % 2) + S]
                                ins = pe.matmul(o, w[:, k, P * m:P * m + P], a[:, kt], start=begins and n == 0 and m % 2 == 0,
                                                stop=ends and n == 2, skip_group_check=True)
                            else:
                                o = ps[:, 2 * (c % 2) + m, 0:width]
                                ins = pe.matmul(o, a[:, kt, P * m:P * m + P], w[:, k, :], start=begins and n == 0,
                                                stop=ends and n == 2, skip_group_check=True)
                ins.then_inc(weights_used, 1)

            def chunk(g0, c, form, left=(xhi, xlo), tiles=4, k0=0, i=None, per=0, chunks=0, fresh=None, beside=None):
                bank_pair(c, i, chunks)
                for s in range(tiles):
                    for half in range(2):
                        product(g0 + s, half, c, form, left, k0 + 4 * s + 2 * half, 2, 512, s == 0 and half == 0,
                                s == tiles - 1 and half == 1, i, per, fresh)
                        if beside is not None:
                            beside(2 * s + half)

            def wide_open():
                for b in range(8):
                    pe.matmul(ps[:, b], zeros[:, 0:P], zeros[:], start=True, stop=False, skip_group_check=True)

            def wide_tile(g, k, s, i=None):
                steps = [(half, t) for half in range(2) for t in range(T)]
                if s == 3:
                    steps.sort(key=lambda step: step[1])
                pe.wait_ge(slo_ready, at(k + 1, i, 4))
                for half, t in steps:
                    h = 2 * g + half
                    if t == 0:
                        pe.wait_ge(lo_ready, at(h + 1, i, 8))
                    for a, w in ((shi, whi), (shi, wlo), (slo, whi)):
                        for n in range(2):
                            ins = pe.matmul(ps[:, 4 * t + 2 * half + n], a[:, s, P * t:P * t + P],
                                            w[:, h % 4, 512 * n:512 * n + 512], start=False, stop=False, skip_group_check=True)
                    if t == T - 1:
                        ins.then_inc(weights_used, 1)
                    elif s == 3 and half == 1:
                        ins.then_inc(first_rows_done, 1)

            def wide(name, turns):
                wide_open()
                g0, k0 = AT[name], SRC[name]
                if turns == 1:
                    for s in range(4):
                        wide_tile(g0 + s, k0 + s, s)
                else:
                    with pe.Fori(0, turns) as i:
                        for s in range(4):
                            wide_tile(g0 + s, k0 + s, s, i)

            pe.wait_ge(built, 6)
            transpose_rows(0, mem_nat, mem_landed, (16, 16))
            chunk(AT["k_mem"], CH["k_mem"], "T", fresh=0)
            chunk(AT["v_mem"], CH["v_mem"], "N")
            pe.wait_ge(x_landed, 16)
            for c in (CH["k_mem"], CH["v_mem"]):
                pe.wait_ge(pair_read[c % 2], reads(c))
            transpose_rows(1, res)
            g, c = AT["latent"], CH["latent"]
            for n in range(6):
                product(g + n // 2, n % 2, c, "N", (xhi, xlo), 3 * n, min(3, KT - 3 * n), LATENT + IDX_DIM + IDX_HEADS, n == 0,
                        n == 5, fresh=1)
            g, c = AT["q_idx"], CH["q_idx"]
            bank_pair(c)
            for s in range(4):
                for half in range(2):
                    product(g + s, half, c, "T", (xhi, xlo), 4 * s + 2 * half, 2, 512, s == 0 and half == 0, s == 3 and half == 1)
                if s == 2:
                    pe.wait_ge(ck_ready, 2)
                    for k in range(2):
                        for t in range(T):
                            ins = pe.transpose(ps[:, 4, S * k + P * t:S * k + P * t + P], ckv[:, t, P * k:P * k + P], ident[:])
                    ins.then_inc(small_T, 1)
                    pe.wait_ge(kn_ready, 4)
                    for t in range(T):
                        ins = pe.transpose(ps[:, 5, P * t:P * t + P], kn[:, t], ident[:])
                    ins.then_inc(small_T, 1)
            chunk(g + 4, c + 1, "T")
            g, c = AT["v_moba"], CH["v_moba"]
            pe.wait_ge(cklo_ready, 1)
            pe.wait_ge(ki_ready, 1)
            for s in range(8):
                if s % 4 == 0:
                    bank_pair(c + s // 4)
                for half in range(2):
                    h = 2 * s + half
                    pe.wait_ge(pair_read[(CH["q_idx"] + h // 8) % 2], reads(CH["q_idx"] + h // 8))
                    if h >= 4:
                        pe.wait_ge(idx_relu, h - 3)
                    r0 = IDX_DIM * (h % 2)
                    for t in range(T):
                        ins = pe.matmul(ps[:, 4 + h % 4, S * t:S * t + S], qi[r0:r0 + IDX_DIM, h // 2, P * t:P * t + P],
                                        kiT[r0:r0 + IDX_DIM, :], start=True, stop=True, skip_group_check=True)
                    ins.then_inc(idx_done, 1)
                    product(g + s, half, c + s // 4, "N", (xhi, xlo), 4 * (s % 4) + 2 * half, 2, 512, s % 4 == 0 and half == 0,
                            s % 4 == 3 and half == 1)
            for name, form in (("w_uk", "T"), ("w_uv", "N")):
                for half in range(2):
                    bank_pair(CH[name] + half)
                    product(AT[name], half, CH[name] + half, form, (ckhi, cklo), 0, 2, 512, True, True)
            with pe.Fori(0, 3) as i:
                for q in range(2):
                    chunk(AT["qk"] + 4 * q, CH["qk"] + q, "T", i=i, per=8, chunks=1)

            pe.wait_ge(idx_relu, IDX_HEADS)
            g0, c0 = AT["gate_a"], CH["gate_a"]
            with pe.Fori(0, 2) as i:
                for q in range(4):
                    c = c0 + q // 2
                    if q % 2 == 0:
                        bank_pair(c, i, 1)
                    for n in range(4):
                        product(g0 + 2 * q + n // 2, n % 2, c, "T", (xhi, xlo), 8 * (q % 2) + 2 * n, 2, 512, q % 2 == 0 and n == 0,
                                q % 2 == 1 and n == 3, i, 8)
                        if n == 0:
                            pe.wait_ge(qv_ready, at(4 * q + 4, i, 16))
                            pe.wait_ge(att_free, at(2 * q + 1, i, 8))
                            for j, k0 in enumerate((24, 16)):
                                key = qk[:, at(k0 + q, i, 4)]
                                pe.matmul(ps[:, 4 + j, 0:128], qs[:, j, 0:128], key[:, 0:128], start=True, stop=True,
                                          skip_group_check=True)
                                pe.matmul(ps[:, 4 + j, 128:384], qs[:, j, 128:256], key, start=True, stop=True,
                                          skip_group_check=True).then_inc(att_scores, 1)
                        if n == 2:
                            for j in range(2):
                                pe.wait_ge(att_p, at(4 * q + 2 * j + 2, i, 16))
                                for b in range(3):
                                    ins = pe.transpose(ps[:, 6 + j, 128 * b:128 * b + 128], att_e[:, j, 128 * b:128 * b + 128],
                                                       ident[:])
                                ins.then_inc(att_T, 1)
                        if n == 3:
                            for j in range(2):
                                pe.wait_ge(att_pT_ready, at(2 * q + j + 1, i, 8))
                                pe.matmul(ps[:, 4 + j, 0:S], vs[:, j, 0], att_pT[:, j, 0:256], start=True, stop=False,
                                          skip_group_check=True)
                                pe.matmul(ps[:, 4 + j, P:S], vs[:, j, 1], att_pT[:, j, 256:384], start=False, stop=True,
                                          skip_group_check=True).then_inc(att_o, 1)

            pe.wait_ge(att_free, 1 + 2 * HEADS)
            g0, c0 = AT["gates"], CH["gates"]
            with pe.Fori(0, 2) as i:
                for unit in range(2):
                    g, c = g0 + 8 * unit, c0 + 3 * unit
                    chunk(g, c, "T", (ohi, olo), 2, 0, i, 16, 3)
                    chunk(g + 2, c + 1, "T", i=i, per=16, chunks=3)
                    chunk(g + 6, c + 2, "T", (ohi, olo), 2, 8, i, 16, 3)
            for c in (c0 + 10, c0 + 11):
                pe.wait_ge(pair_read[c % 2], reads(c))
            wide("out1", 4)
            pe.wait_ge(sq_ready, 2)
            transpose_rows(2, res, res_ready, (1, 2, 3))
            chunk(AT["q_mem"], CH["q_mem"], "T", fresh=2)

            c = CH["q_mem"]
            pe.wait_ge(pair_read[c % 2], reads(c))
            spare = 2 * ((c + 1) % 2)
            for h in range(HEADS_MEM):
                for t in range(T):
                    ins = pe.matmul(ps[:, 4 + h, S * t:S * t + S], qmT[:, h, P * t:P * t + P], kmT[:, h], start=True, stop=True,
                                    skip_group_check=True)
                ins.then_inc(m_scores, 1)
            for h in range(HEADS_MEM + 1):
                if h < HEADS_MEM:
                    pe.wait_ge(m_p, 2 * h + 2)
                    for k in range(2):
                        for t in range(T):
                            ins = pe.transpose(ps[:, spare + h % 2, S * k + P * t:S * k + P * t + P],
                                               mem_p[:, h, S * t + P * k:S * t + P * k + P], ident[:])
                    ins.then_inc(m_T, 1)
                if h >= 1:
                    pe.wait_ge(m_pT, h)
                    for k in range(2):
                        ins = pe.matmul(ps[:, 3 + h, 0:S], vm[:, k, HD * (h - 1):HD * h], mem_pT[:, (h - 1) % 2, S * k:S * k + S],
                                        start=k == 0, stop=k == 1, skip_group_check=True)
                    ins.then_inc(m_o, 1)
            pe.wait_ge(m_out, HEADS_MEM)
            wide("o_mem", 1)
            pe.wait_ge(sq_ready, 4)
            transpose_rows(3, res, res_ready, (4, 5, 6))
            with pe.Fori(0, FC) as i:
                for q in range(2):
                    chunk(AT["up1"] + 4 * q, CH["up1"] + q, "T", i=i, per=8, chunks=1, fresh=3 if q == 0 else None)
            for c in (CH["up1"] + 2 * FC - 2, CH["up1"] + 2 * FC - 1):
                pe.wait_ge(pair_read[c % 2], reads(c))
            wide("down1", FC)
            pe.wait_ge(sq_ready, 8)
            transpose_rows(4, xn, xn_ready, (1, 2, 2))
            g, c = AT["lstm_gates"], CH["lstm_gates"]
            for half in range(2):
                product(g, half, c, "T", (xhi, xlo), 8 * half, 8, P, half == 0, half == 1, fresh=4)
            chunk(AT["lstm_q"], CH["lstm_q"], "T")
            chunk(AT["lstm_k"], CH["lstm_k"], "T")
            chunk(AT["lstm_v"], CH["lstm_v"], "N")
            chunk(AT["lstm_v"] + 4, CH["lstm_v"] + 1, "N")

            def gate_columns():
                pe.wait_ge(g_floor, 1)
                for n, src in enumerate((g_a, g_m)):
                    for d in range(2):
                        for t in range(T):
                            q = 16 * n + 8 * d + 4 * t
                            ins = pe.transpose(ps[:, 6, q:q + LH], src[:, d, P * t:P * t + P], ident[0:LH, 0:LH])
                ins.then_inc(g_cols_T, 1)

            def l_products(h):
                if h == 0:
                    pe.wait_ge(built, 19)
                    pe.wait_ge(late_landed, 32)
                else:
                    pe.wait_ge(mix_m, 2 * h)
                pe.matmul(ps[:, 4], sel[:, h], g_max[:].rearrange("h d t -> h (d t)"), start=True, stop=True,
                          skip_group_check=True).then_inc(l_bc, 1)
                for st in range(T):
                    ins = pe.matmul(ps[:, 5, S * st:S * st + S], lk[:, h, P * st:P * st + P], lq[:, h], start=True, stop=True,
                                    skip_group_check=True)
                ins.then_inc(l_st, 1)

            def l_values(h):
                pe.wait_ge(l_p, h + 1)
                for d in range(2):
                    for t in range(T):
                        mine = [b for b in BLOCKS if b[0] == d and b[2] <= P * t < b[3]]
                        for n, (_, st, t0, _, c0) in enumerate(mine):
                            q = c0 + P * t - t0
                            pe.matmul(ps[:, 6 + d, S * t:S * t + DV], lp[:, q:q + P], lv[:, st, h, 0:DV], start=t == 0 and n == 0,
                                      stop=n == len(mine) - 1, skip_group_check=True)
                            o = 2 * d + t
                            ins = pe.matmul(ps[:, 4, o:o + 1], lp[:, q:q + P], lv[:, st, h, DV:DV + 1], start=o == 0 and n == 0,
                                            stop=n == len(mine) - 1, skip_group_check=True)
                ins.then_inc(l_num, 1)

            def l_transposed(h):
                pe.wait_ge(l_hn, 2 * h + 2)
                for v in range(2):
                    for t in range(T):
                        ins = pe.transpose(ps[:, 5, S * v + P * t:S * v + P * t + P], lh[:, t, P * v:P * v + P], ident[:])
                ins.then_inc(l_hT, 1)

            def heads_beside(n):
                def step(half):
                    if half == 1:
                        gate_columns() if n == 0 else l_values(n - 1)
                    if half == 4 and n >= 1:
                        l_transposed(n - 1)
                    if half == 5:
                        l_products(n)
                return step

            for n in range(4):
                name, form = ("lstm_o", "T") if n < 2 else ("fourier", "N")
                chunk(AT[name] + 4 * (n % 2), CH[name] + n % 2, form, beside=heads_beside(n))

            def f_tokens(h):
                for f in range(2):
                    for st in range(T):
                        ins = pe.matmul(ps[:, h, S * f:S * f + S], uf[:, st, S * h + P * f:S * h + P * f + P],
                                        dftc[:, st, 2 * S:3 * S], start=f == 0 and st == 0, stop=st == 1, skip_group_check=True)
                ins.then_inc(f_first, 1)

            def f_width(h):
                pe.wait_ge(f_copied, h + 1)
                for part, k0, width in ((0, 0, P + 1), (1, P + 1, P - 1)):
                    for fo in range(2):
                        for fi in range(2):
                            o = 2 * (P + 1) * part + width * fo
                            ins = pe.matmul(ps[:, h, o:o + width], dftc[:, fi, S * part + P * fo:S * part + P * fo + P],
                                            fa[h][:, fi, k0:k0 + width], start=part + fo + fi == 0, stop=fi == 1,
                                            skip_group_check=True)
                ins.then_inc(f_second, 1)

            for c in (CH["fourier"], CH["fourier"] + 1):
                pe.wait_ge(pair_read[c % 2], reads(c))
            f_tokens(0)
            f_tokens(1)
            l_values(LH - 1)
            f_tokens(2)
            f_tokens(3)
            f_width(0)
            f_width(1)
            f_width(2)
            l_transposed(LH - 1)
            f_width(3)

            def gate_rows(n):
                pe.wait_ge(diag_ready, n + 1)
                for k in range(KT):
                    ins = pe.matmul(ps[:, 4 + k // 4, P * (k % 4):P * (k % 4) + P], ones[:], diags[n][:, k], start=True, stop=True,
                                    skip_group_check=True)
                ins.then_inc(gate_T, 1)

            pe.wait_ge(mix_m, 2 * LH)
            gate_rows(0)
            pe.wait_ge(gate_ready, 1)
            pe.wait_ge(mix_f, LH)
            wide("out2", 4)
            pe.wait_ge(sq_ready, 10)
            transpose_rows(5, xn, xn_ready, (3, 4, 4))
            with pe.Fori(0, FC) as i:
                for q in range(2):
                    chunk(AT["up2"] + 4 * q, CH["up2"] + q, "T", i=i, per=8, chunks=1, fresh=5 if q == 0 else None)
            gate_rows(1)
            for c in (CH["up2"] + 2 * FC - 2, CH["up2"] + 2 * FC - 1):
                pe.wait_ge(pair_read[c % 2], reads(c))
            pe.wait_ge(gate_ready, 2)
            wide("down2", FC)


def tiles_by_chunk(w):
    k, n = w.shape
    return w.reshape(k // 512, 4, P, n // 512, 512).transpose(3, 0, 2, 1, 4).reshape(n // 512, k // 512, P, D)


def tiles_of_latent(w):
    return w.reshape(2, P, 2, 512).transpose(1, 2, 0, 3).reshape(1, P, D)


def tile_of_gates(w):
    out = np.zeros((P, KT, 4, 32), w.dtype)
    out[..., 0:LH] = w.reshape(KT, P, 4, LH).transpose(1, 0, 2, 3)
    return out.reshape(1, P, D)


def weight_stream(a):
    flat = lambda w: w.reshape(-1, P, D)
    w_in, w_in2 = a["w_in"][0], a["w_in_2"]
    kv = tiles_by_chunk(a["w_kv_mem"][0])
    o = {}
    n = 0
    for name, width in (("q_dsa", 1024), ("c_kv", 256), ("q_idx", 1024), ("k_idx", 80), ("q_m", 1024), ("k_m", 1024),
                        ("v_m", 1024), ("ga", D), ("gb", D)):
        o[name] = w_in[:, n:n + width]
        n += width
    side = [tiles_by_chunk(w) for w in (a["w_o_dsa"][0], o["gb"], a["w_o_moba"][0])]
    gates = np.concatenate(side, axis=1)
    up1 = tiles_by_chunk(a["w_ffn_in"][0])
    up1 = np.concatenate([up1[:FC], up1[FC:]], axis=1)
    up2 = tiles_by_chunk(a["w_up_2"])
    up2 = np.concatenate([up2[:FC], up2[FC:]], axis=1)
    few = LATENT + IDX_DIM + IDX_HEADS
    latent = np.zeros((6, P, 1024), w_in.dtype)
    rows = np.concatenate([o["c_kv"], o["k_idx"]], axis=1).reshape(KT, P, few)
    for k in range(KT):
        latent[k // 3, :, few * (k % 3):few * (k % 3) + few] = rows[k]
    latent = latent.reshape(3, 2, P, 1024).transpose(0, 2, 1, 3)
    parts = [
        flat(kv), flat(latent), flat(tiles_by_chunk(o["q_idx"])), flat(tiles_by_chunk(o["v_m"])),
        tiles_of_latent(a["w_uk"][0].transpose(2, 0, 1).reshape(LATENT, 1024)),
        tiles_of_latent(a["w_uv"][0].transpose(1, 0, 2).reshape(LATENT, 1024)),
        flat(tiles_by_chunk(o["q_dsa"])), flat(tiles_by_chunk(o["q_m"])), flat(tiles_by_chunk(o["k_m"])),
        flat(tiles_by_chunk(o["ga"])), flat(gates), flat(a["w_out"][0]), flat(tiles_by_chunk(a["w_q_mem"][0])), flat(a["w_o_mem"][0]), flat(up1),
        flat(a["w_ffn_out"][0]), tile_of_gates(w_in2[:, 4096:4112]), flat(tiles_by_chunk(w_in2[:, 1024:4096])),
        flat(tiles_by_chunk(w_in2[:, 0:1024])), flat(a["w_out_2"]), flat(up2), flat(a["w_down_2"]),
    ]
    return np.concatenate(parts, axis=0)


def kernel(**inputs):
    import concourse.bacc as bacc
    from concourse.bass_utils import run_bass_kernel_spmd

    a = {k: np.asarray(v) for k, v in inputs.items()}

    def columns(v):
        return v.reshape(-1, P).T

    slopes = np.array([2.0 ** (-8.0 * (n + 1) / HEADS) for n in range(HEADS)], np.float32)
    turn = np.arange(S)
    angle = 2 * np.pi * (np.outer(turn, turn) % S) / S
    root = S ** 0.5
    cosines, sines = np.cos(angle) / root, np.sin(angle) / root
    wave = np.concatenate([cosines, sines, cosines[:, 0:P + 1], sines[:, 1:P]], axis=1)
    gate_bias = np.zeros((4, 32, 1), np.float32)
    gate_bias[:, 0:LH, 0] = a["b_gates_2"].reshape(4, LH)
    gate_bias = gate_bias.reshape(P, 1)
    arrays = {
        "x": a["x"][0],
        "mem": a["mem"][0],
        "stream": weight_stream(a),
        "w_ada": np.ascontiguousarray(a["w_ada_2"].T).reshape(ADA, P, D),
        "cols": np.concatenate(
            [columns(a["b_gate"][0]), columns(a["b_ada_2"]), columns(a["norm1_w_2"]), columns(a["norm2_w_2"]),
             columns(a["mlstm_norm_w_2"]), columns(a["w_conv_2"]), columns(a["b_conv_2"]),
             np.broadcast_to(slopes, (P, HEADS))], axis=1),
        "rows": np.concatenate([a["kv_norm_g"], a["idx_k_norm_g"], a["idx_k_norm_b"]], axis=1),
        "ln_g": a["ln_g"][0],
        "ln_b": a["ln_b"][0],
        "norm_f": a["norm_f_w_2"].reshape(1, D),
        "c_row": a["c_2"],
        "gate_bias": gate_bias,
        "dft": wave.astype(np.float32),
    }
    arrays = {k: np.ascontiguousarray(v) for k, v in arrays.items()}
    assert arrays["stream"].shape[0] == G, (arrays["stream"].shape, G)
    nc = bacc.Bacc("TRN2", target_bir_lowering=False, num_devices=1)
    args = [nc.dram_tensor(f"in_{k}", v.shape, F32, kind="ExternalInput").ap() for k, v in arrays.items()]
    out = nc.dram_tensor("out_0", (S, D), F32, kind="ExternalOutput").ap()
    two_blocks(nc, *args, out)
    r = run_bass_kernel_spmd(nc, [{f"in_{k}": v for k, v in arrays.items()}], core_ids=[0])
    return r.results[0]["out_0"].reshape(1, S, D)
```
